# Optimizing a Trainium2 kernel written in Bass

```python
import math
import jax
import jax.numpy as jnp
from jax import lax
import numpy as np

D_MODEL = 1024
BATCH = 1
SEQ = 512
DEPTH = 2

GRID_W = 64
CTX_LEN = 256
N_MOD = 9
FFN_DIM = 256 * ((8 * D_MODEL // 3 + 255) // 256)
SSD_P = 64
SSD_HEADS = D_MODEL // SSD_P
SSD_DI = SSD_HEADS * SSD_P
SSD_G = 2
SSD_N = 128
D_CONV = 5
CONV_CH = SSD_DI + 2 * SSD_G * SSD_N
CHUNK = 128
MLA_DN = 128
MLA_DR = 64
MLA_DV = 128
MLA_HEADS = D_MODEL // MLA_DV
MLA_Q_RANK = 3 * D_MODEL // 8
MLA_KV_RANK = D_MODEL // 4
GQA_HD = 64
GQA_HQ = D_MODEL // GQA_HD
GQA_HKV = GQA_HQ // 4
GQA_REP = GQA_HQ // GQA_HKV
WINDOW = 128
QBLK = 128
ROPE_BASE = 10000.0
EPS = 1e-6
N_EVEN = (DEPTH + 1) // 2
N_ODD = DEPTH // 2
_E0 = SSD_DI
_E1 = _E0 + CONV_CH
_E2 = _E1 + 2 * SSD_HEADS
_E3 = _E2 + MLA_Q_RANK
_E4 = _E3 + MLA_KV_RANK
E_SPLITS = [_E0, _E1, _E2, _E3, _E4]
E_IN = _E4 + MLA_DR
MIX_E = SSD_DI + MLA_HEADS * MLA_DV
O_SPLITS = [GQA_HQ * GQA_HD, GQA_HQ * GQA_HD + GQA_HKV * GQA_HD]
O_IN = GQA_HQ * GQA_HD + 2 * GQA_HKV * GQA_HD
F32 = jnp.float32

kernel_name = "hybrid_ssd_mla_swa_prefix_dit"

def rms_norm(t, gain=None):
    tf = t.astype(F32)
    y = (tf * lax.rsqrt(jnp.mean(tf * tf, axis=-1, keepdims=True) + EPS)).astype(t.dtype)
    return y if gain is None else y * gain

def modulate(t, shift, scale):
    return rms_norm(t) * (1 + scale) + shift

def swiglu(t, w_in, w_out):
    gate, up = jnp.split(t @ w_in, 2, axis=-1)
    return (jax.nn.silu(gate) * up) @ w_out

def axial_rope_tables(rows, dim):
    quarter = dim // 4
    freqs = ROPE_BASE ** (-jnp.arange(quarter, dtype=F32) / quarter)
    t = jnp.arange(rows * GRID_W)
    row = (t // GRID_W).astype(F32)
    col = (t % GRID_W).astype(F32)
    ang_r = row[:, None] * freqs
    ang_c = col[:, None] * freqs
    return (jnp.cos(ang_r), jnp.sin(ang_r), jnp.cos(ang_c), jnp.sin(ang_c))

def rope2d(t, tables):
    cos_r, sin_r, cos_c, sin_c = tables
    shp = (t.shape[1],) + (1,) * (t.ndim - 3) + (cos_r.shape[-1],)

    def rot(u, cos, sin):
        cos = cos.reshape(shp).astype(u.dtype)
        sin = sin.reshape(shp).astype(u.dtype)
        a, b = jnp.split(u, 2, axis=-1)
        return jnp.concatenate([a * cos - b * sin, b * cos + a * sin], axis=-1)

    t_r, t_c = jnp.split(t, 2, axis=-1)
    return jnp.concatenate([rot(t_r, cos_r, sin_r), rot(t_c, cos_c, sin_c)], axis=-1)

def dwconv_centered(t, w, b):
    ch = t.shape[-1]
    y = lax.conv_general_dilated(t, w[:, None, :], window_strides=(1,),
                                 padding=[(D_CONV // 2, D_CONV // 2)],
                                 dimension_numbers=("NWC", "WIO", "NWC"),
                                 feature_group_count=ch)
    return y + b

def ssd_scan(x, dt, a, bm, cm, h0, with_y):
    dtype = x.dtype
    bsz, l, h, p = x.shape
    g, n = bm.shape[2], bm.shape[3]
    r = h // g
    nc = l // CHUNK
    x = x.astype(F32).reshape(bsz, nc, CHUNK, g, r, p)
    dt = dt.astype(F32).reshape(bsz, nc, CHUNK, g, r)
    bm = bm.astype(F32).reshape(bsz, nc, CHUNK, g, n)
    cm = cm.astype(F32).reshape(bsz, nc, CHUNK, g, n)
    xdt = x * dt[..., None]
    acs = jnp.cumsum(dt * a.astype(F32).reshape(g, r), axis=2)
    states = jnp.einsum("bcsgn,bcsgr,bcsgrp->cbgrpn", bm, jnp.exp(acs[:, :, -1:] - acs), xdt)
    chunk_decay = jnp.swapaxes(jnp.exp(acs[:, :, -1]), 0, 1)

    def step(s, inp):
        st, dc = inp
        return dc[..., None, None] * s + st, s

    final, s_in = lax.scan(step, h0.astype(F32).reshape(bsz, g, r, p, n), (states, chunk_decay))
    final = final.reshape(bsz, h, p, n).astype(dtype)
    if not with_y:
        return None, final
    seg = acs[:, :, :, None] - acs[:, :, None, :]
    lower = jnp.tril(jnp.ones((CHUNK, CHUNK), bool))[:, :, None, None]
    lmat = jnp.exp(jnp.where(lower, seg, -jnp.inf))
    y = (jnp.einsum("bclgn,bcsgn,bclsgr,bcsgrp->bclgrp", cm, bm, lmat, xdt)
         + jnp.einsum("bclgn,cbgrpn,bclgr->bclgrp", cm, s_in, jnp.exp(acs)))
    return y.reshape(bsz, l, h, p).astype(dtype), final

def mla_attend(qn, qr, kn, kr, v, scale):
    bsz, m, h, _ = qn.shape
    nb = m // QBLK

    def blocks(t):
        return jnp.moveaxis(t.reshape((bsz, nb, QBLK) + t.shape[2:]), 1, 0)

    def one(qs):
        qnb, qrb = qs
        s = (jnp.einsum("bqhd,bkhd->bhqk", qnb, kn)
             + jnp.einsum("bqhd,bkd->bhqk", qrb, kr)).astype(F32) * scale
        prob = jax.nn.softmax(s, axis=-1).astype(v.dtype)
        return jnp.einsum("bhqk,bkhd->bqhd", prob, v)

    o = lax.map(one, (blocks(qn), blocks(qr)))
    return jnp.moveaxis(o, 0, 1).reshape(bsz, m, h, v.shape[-1])

def window_attend(q, k, v, kc, vc, sink, scale):
    bsz, n, hk, r, d = q.shape
    lc = kc.shape[1]
    nb = n // QBLK
    span = QBLK + 2 * WINDOW
    pad = ((0, 0), (WINDOW, WINDOW), (0, 0), (0, 0))
    kp = jnp.pad(k, pad)
    vp = jnp.pad(v, pad)
    qi = jnp.arange(QBLK)
    kj = jnp.arange(span)
    band = jnp.abs(qi[:, None] + WINDOW - kj[None, :]) <= WINDOW
    sink_l = jnp.broadcast_to(sink.astype(F32)[None, :, :, None, None], (bsz, hk, r, QBLK, 1))

    def block(i):
        start = i * QBLK
        qb = lax.dynamic_slice_in_dim(q, start, QBLK, axis=1)
        kb = lax.dynamic_slice_in_dim(kp, start, span, axis=1)
        vb = lax.dynamic_slice_in_dim(vp, start, span, axis=1)
        kpos = start - WINDOW + kj
        valid = band & ((kpos >= 0) & (kpos < n))[None, :]
        s_loc = jnp.einsum("bqhrd,bkhd->bhrqk", qb, kb).astype(F32) * scale
        s_loc = jnp.where(valid, s_loc, -jnp.inf)
        s_ctx = jnp.einsum("bqhrd,bkhd->bhrqk", qb, kc).astype(F32) * scale
        prob = jax.nn.softmax(jnp.concatenate([s_loc, s_ctx, sink_l], axis=-1), axis=-1).astype(v.dtype)
        return (jnp.einsum("bhrqk,bkhd->bqhrd", prob[..., :span], vb)
                + jnp.einsum("bhrqk,bkhd->bqhrd", prob[..., span:span + lc], vc))

    o = lax.map(block, jnp.arange(nb))
    return jnp.moveaxis(o, 0, 1).reshape(bsz, n, hk, r, d)

def sink_attend(q, k, v, sink, scale):
    bsz, m, hk, r, _ = q.shape
    s = jnp.einsum("bqhrd,bkhd->bhrqk", q, k).astype(F32) * scale
    sink_l = jnp.broadcast_to(sink.astype(F32)[None, :, :, None, None], (bsz, hk, r, m, 1))
    prob = jax.nn.softmax(jnp.concatenate([s, sink_l], axis=-1), axis=-1)[..., :-1].astype(v.dtype)
    return jnp.einsum("bhrqk,bkhd->bqhrd", prob, v)

def even_mixer(u, uc, w_in, conv_w, conv_b, dt_bias, a_log, d_skip, ssd_norm, qa_norm, w_qb,
               kv_norm, w_kvb, qn_g, qr_g, kn_g, kr_g, w_out, rope, need_ctx):
    bsz = u.shape[0]
    a_fwd = -jnp.exp(a_log[0].astype(F32))
    a_bwd = -jnp.exp(a_log[1].astype(F32))

    def project(t):
        m = t.shape[1]
        z, xbc, dtr, qa, ckv, kr = jnp.split(t @ w_in, E_SPLITS, axis=-1)
        xbc = jax.nn.silu(dwconv_centered(xbc, conv_w, conv_b))
        xs, bm, cm = jnp.split(xbc, [SSD_DI, SSD_DI + SSD_G * SSD_N], axis=-1)
        xs = xs.reshape(bsz, m, SSD_HEADS, SSD_P)
        bm = bm.reshape(bsz, m, SSD_G, SSD_N)
        cm = cm.reshape(bsz, m, SSD_G, SSD_N)
        dt_f = jax.nn.softplus(dtr[..., :SSD_HEADS] + dt_bias[0])
        dt_b = jax.nn.softplus(dtr[..., SSD_HEADS:] + dt_bias[1])
        kv = (rms_norm(ckv, kv_norm) @ w_kvb).reshape(bsz, m, MLA_HEADS, MLA_DN + MLA_DV)
        kn, v = jnp.split(kv, [MLA_DN], axis=-1)
        return z, xs, bm, cm, dt_f, dt_b, qa, rms_norm(kn, kn_g), rms_norm(kr, kr_g), v

    def queries(qa):
        q = (rms_norm(qa, qa_norm) @ w_qb).reshape(bsz, qa.shape[1], MLA_HEADS, MLA_DN + MLA_DR)
        qn, qr = jnp.split(q, [MLA_DN], axis=-1)
        return rms_norm(qn, qn_g), rms_norm(qr, qr_g)

    def ssd_merge(y_f, y_b_rev, xs, z):
        m = xs.shape[1]
        y = (y_f + jnp.flip(y_b_rev, 1) + d_skip[:, None] * xs).reshape(bsz, m, SSD_DI)
        y = rms_norm((y * jax.nn.silu(z)).reshape(bsz, m, SSD_G, SSD_DI // SSD_G))
        return y.reshape(bsz, m, SSD_DI) * ssd_norm

    def flip(t):
        return jnp.flip(t, 1)

    zc, xc, bc, cc, dfc, dbc, qac, knc, krc, vc = project(uc)
    z, xs, bm, cm, df, db, qa, kn, kr, v = project(u)
    h0 = jnp.zeros((bsz, SSD_HEADS, SSD_P, SSD_N), u.dtype)
    yfc, s_fc = ssd_scan(xc, dfc, a_fwd, bc, cc, h0, need_ctx)
    ybc, s_bc = ssd_scan(flip(xc), flip(dbc), a_bwd, flip(bc), flip(cc), h0, need_ctx)
    yf, _ = ssd_scan(xs, df, a_fwd, bm, cm, s_fc, True)
    yb, _ = ssd_scan(flip(xs), flip(db), a_bwd, flip(bm), flip(cm), s_bc, True)
    scale = (MLA_DN + MLA_DR) ** -0.5
    qn, qr = queries(qa)
    o = mla_attend(qn, rope2d(qr, rope),
                   jnp.concatenate([kn, knc], axis=1),
                   jnp.concatenate([rope2d(kr, rope), krc], axis=1),
                   jnp.concatenate([v, vc], axis=1), scale)
    y = jnp.concatenate([ssd_merge(yf, yb, xs, z),
                         o.reshape(bsz, -1, MLA_HEADS * MLA_DV)], axis=-1) @ w_out
    yc = None
    if need_ctx:
        qnc, qrc = queries(qac)
        oc = mla_attend(qnc, qrc, knc, krc, vc, scale)
        yc = jnp.concatenate([ssd_merge(yfc, ybc, xc, zc),
                              oc.reshape(bsz, -1, MLA_HEADS * MLA_DV)], axis=-1) @ w_out
    return y, yc

def odd_mixer(u, uc, w_in, q_g, k_g, sink, w_out, rope, need_ctx):
    bsz = u.shape[0]
    sink_hr = sink.reshape(GQA_HKV, GQA_REP)
    scale = GQA_HD ** -0.5

    def project(t):
        m = t.shape[1]
        q, k, v = jnp.split(t @ w_in, O_SPLITS, axis=-1)
        q = q.reshape(bsz, m, GQA_HKV, GQA_REP, GQA_HD)
        k = rms_norm(k.reshape(bsz, m, GQA_HKV, GQA_HD), k_g)
        return q, k, v.reshape(bsz, m, GQA_HKV, GQA_HD)

    qc, kc, vc = project(uc)
    q, k, v = project(u)
    q = rope2d(rms_norm(q, q_g), rope)
    k = rope2d(k, rope)
    y = window_attend(q, k, v, kc, vc, sink_hr, scale).reshape(bsz, -1, GQA_HQ * GQA_HD) @ w_out
    yc = None
    if need_ctx:
        oc = sink_attend(rms_norm(qc, q_g), kc, vc, sink_hr, scale)
        yc = oc.reshape(bsz, -1, GQA_HQ * GQA_HD) @ w_out
    return y, yc

def setup_inputs(seed: int = 0) -> dict:
    key = jax.random.key(seed)
    keys = list(jax.random.split(key, 40))
    D = D_MODEL

    def normal(shape):
        return jax.random.normal(keys.pop(), shape, F32)

    def w(shape, fan_in, s=1.0):
        return (s * fan_in ** -0.5) * normal(shape)

    def gain(shape):
        return 1.0 + 0.02 * normal(shape)

    x = normal((BATCH, SEQ, D))
    c = normal((BATCH, D))
    ctx = normal((BATCH, CTX_LEN, D))
    c_ctx = normal((D,))
    w_mod = w((DEPTH, D, N_MOD * D), D, 0.5)
    b_mod = 0.02 * normal((DEPTH, N_MOD * D))
    w_ff1_in = w((DEPTH, D, 2 * FFN_DIM), D)
    w_ff1_out = w((DEPTH, FFN_DIM, D), FFN_DIM)
    w_ff2_in = w((DEPTH, D, 2 * FFN_DIM), D)
    w_ff2_out = w((DEPTH, FFN_DIM, D), FFN_DIM)
    w_in_e = w((N_EVEN, D, E_IN), D)
    conv_w = w((N_EVEN, D_CONV, CONV_CH), D_CONV)
    conv_b = 0.02 * normal((N_EVEN, CONV_CH))
    u_dt = jax.random.uniform(keys.pop(), (N_EVEN, 2, SSD_HEADS), F32)
    dt0 = jnp.exp(u_dt * (math.log(0.1) - math.log(0.001)) + math.log(0.001))
    dt_bias = dt0 + jnp.log(-jnp.expm1(-dt0))
    a_log = jnp.log(jax.random.uniform(keys.pop(), (N_EVEN, 2, SSD_HEADS), F32, 1.0, 16.0))
    d_skip = gain((N_EVEN, SSD_HEADS))
    ssd_norm = gain((N_EVEN, SSD_DI))
    mla_qa_norm = gain((N_EVEN, MLA_Q_RANK))
    w_qb = w((N_EVEN, MLA_Q_RANK, MLA_HEADS * (MLA_DN + MLA_DR)), MLA_Q_RANK)
    mla_kv_norm = gain((N_EVEN, MLA_KV_RANK))
    w_kvb = w((N_EVEN, MLA_KV_RANK, MLA_HEADS * (MLA_DN + MLA_DV)), MLA_KV_RANK)
    mla_qn_norm = gain((N_EVEN, MLA_DN))
    mla_qr_norm = gain((N_EVEN, MLA_DR))
    mla_kn_norm = gain((N_EVEN, MLA_DN))
    mla_kr_norm = gain((N_EVEN, MLA_DR))
    w_out_e = w((N_EVEN, MIX_E, D), MIX_E)
    w_in_o = w((N_ODD, D, O_IN), D)
    gqa_q_norm = gain((N_ODD, GQA_HD))
    gqa_k_norm = gain((N_ODD, GQA_HD))
    sink = 0.5 * normal((N_ODD, GQA_HQ))
    w_out_o = w((N_ODD, GQA_HQ * GQA_HD, D), GQA_HQ * GQA_HD)
    return {"x": x, "c": c, "ctx": ctx, "c_ctx": c_ctx, "w_mod": w_mod, "b_mod": b_mod,
            "w_ff1_in": w_ff1_in, "w_ff1_out": w_ff1_out, "w_ff2_in": w_ff2_in, "w_ff2_out": w_ff2_out,
            "w_in_e": w_in_e, "conv_w": conv_w, "conv_b": conv_b, "dt_bias": dt_bias, "a_log": a_log,
            "d_skip": d_skip, "ssd_norm": ssd_norm, "mla_qa_norm": mla_qa_norm, "w_qb": w_qb,
            "mla_kv_norm": mla_kv_norm, "w_kvb": w_kvb, "mla_qn_norm": mla_qn_norm,
            "mla_qr_norm": mla_qr_norm, "mla_kn_norm": mla_kn_norm, "mla_kr_norm": mla_kr_norm,
            "w_out_e": w_out_e, "w_in_o": w_in_o, "gqa_q_norm": gqa_q_norm, "gqa_k_norm": gqa_k_norm,
            "sink": sink, "w_out_o": w_out_o}

def reference(x, c, ctx, c_ctx, w_mod, b_mod, w_ff1_in, w_ff1_out, w_ff2_in, w_ff2_out,
              w_in_e, conv_w, conv_b, dt_bias, a_log, d_skip, ssd_norm, mla_qa_norm, w_qb,
              mla_kv_norm, w_kvb, mla_qn_norm, mla_qr_norm, mla_kn_norm, mla_kr_norm, w_out_e,
              w_in_o, gqa_q_norm, gqa_k_norm, sink, w_out_o):
    bsz, n, _ = x.shape
    rows = n // GRID_W
    rope_mla = axial_rope_tables(rows, MLA_DR)
    rope_gqa = axial_rope_tables(rows, GQA_HD)
    sc = jax.nn.silu(c)
    scc = jax.nn.silu(c_ctx)
    h, hc = x, ctx
    for l in range(DEPTH):
        need_ctx = l < DEPTH - 1
        m = (sc @ w_mod[l] + b_mod[l]).reshape(bsz, N_MOD, 1, D_MODEL)
        mc = (scc @ w_mod[l] + b_mod[l]).reshape(N_MOD, D_MODEL)
        h = h + 0.5 * m[:, 2] * swiglu(modulate(h, m[:, 0], m[:, 1]), w_ff1_in[l], w_ff1_out[l])
        hc = hc + 0.5 * mc[2] * swiglu(modulate(hc, mc[0], mc[1]), w_ff1_in[l], w_ff1_out[l])
        u = modulate(h, m[:, 3], m[:, 4])
        uc = modulate(hc, mc[3], mc[4])
        if l % 2 == 0:
            e = l // 2
            y, yc = even_mixer(u, uc, w_in_e[e], conv_w[e], conv_b[e], dt_bias[e], a_log[e],
                               d_skip[e], ssd_norm[e], mla_qa_norm[e], w_qb[e], mla_kv_norm[e],
                               w_kvb[e], mla_qn_norm[e], mla_qr_norm[e], mla_kn_norm[e],
                               mla_kr_norm[e], w_out_e[e], rope_mla, need_ctx)
        else:
            o = l // 2
            y, yc = odd_mixer(u, uc, w_in_o[o], gqa_q_norm[o], gqa_k_norm[o], sink[o],
                              w_out_o[o], rope_gqa, need_ctx)
        h = h + m[:, 5] * y
        h = h + 0.5 * m[:, 8] * swiglu(modulate(h, m[:, 6], m[:, 7]), w_ff2_in[l], w_ff2_out[l])
        if need_ctx:
            hc = hc + mc[5] * yc
            hc = hc + 0.5 * mc[8] * swiglu(modulate(hc, mc[6], mc[7]), w_ff2_in[l], w_ff2_out[l])
    return h


_drawn_inputs = setup_inputs


def setup_inputs(seed=0):
    import zlib

    import numpy as np

    out = dict(_drawn_inputs(seed))
    spreads = {}
    factors = {'ctx': 2.951,
     'conv_b': 8.0,
     'd_skip': 23.464,
     'ssd_norm': 23.077,
     'mla_qa_norm': 8.0,
     'w_qb': 3.542,
     'mla_kv_norm': 8.0,
     'mla_qn_norm': 8.0,
     'mla_qr_norm': 8.0,
     'mla_kn_norm': 8.0,
     'mla_kr_norm': 8.0,
     'gqa_q_norm': 29.921,
     'gqa_k_norm': 27.805,
     'sink': 8.0}
    for name, (base, spread) in spreads.items():
        noise = np.random.default_rng([zlib.crc32(name.encode()), seed]).standard_normal(out[name].shape)
        drawn = base * np.exp(spread * noise) if base else spread * noise
        out[name] = jnp.asarray(drawn.astype(out[name].dtype))
    for name, factor in factors.items():
        out[name] = (out[name] * factor).astype(out[name].dtype)
    return out
```

```python
from contextlib import ExitStack

import numpy as np

import concourse.bass as bass
from concourse import mybir

F32 = mybir.dt.float32
ACT = mybir.ActivationFunctionType
ALU = mybir.AluOpType
AX = mybir.AxisListType.X

P = 128
D = 1024
DB = D // P
SEQ, CTX = 512, 256
T = SEQ + CTX
GRID_W = 64
FFN = 2816
FB = FFN // P
EPS = 1e-6
NT = T // P
SEGS = ((0, SEQ, 0), (SEQ, T, 1))

Z0, XBC0, DT0, QA0, CKV0, KR0 = 0, 1024, 2560, 2592, 2976, 3232
HEADS, SP = 16, 64
MH, DN, DR, DV = 8, 128, 64, 128
QH, KVH, HD = 16, 4, 64

RING = 4
SLOT = 8 * P

C_ID, C_ONE, C_BLK, C_UF, C_UB, C_TF, C_TB, C_MP, C_MN, C_SW, C_COS, C_SIN = (
    0, 128, 256, 384, 512, 640, 768, 896, 1024, 1152, 1280, 1792)
C_ALL = 2304
NEG = -1.0e30

VA_MOD, VA_C, VA_CC, VA_N = 0, 72, 80, 88
VB_MOD, VB_SSD, VB_QA, VB_KV, VB_QN, VB_KN, VB_QR, VB_KR, VB_GQ, VB_GK, VB_CB, VB_N = (
    0, 72, 80, 83, 85, 86, 87, 88, 89, 90, 91, 103)
VC_N = 60


def shape_constants():
    c = np.zeros((P, C_ALL), np.float32)
    i = np.arange(P)
    c[:, C_ID:C_ID + P] = np.eye(P)
    c[:, C_ONE:C_ONE + P] = 1.0
    c[:, C_BLK:C_BLK + P] = (i[:, None] // 64) == (i[None, :] // 64)
    c[:, C_UF:C_UF + P] = i[:, None] > i[None, :]
    c[:, C_UB:C_UB + P] = i[:, None] < i[None, :]
    c[:, C_TF:C_TF + P] = i[:, None] <= i[None, :]
    c[:, C_TB:C_TB + P] = i[:, None] >= i[None, :]
    c[:, C_MP:C_MP + P] = np.where(i[None, :] >= i[:, None], 0.0, NEG)
    c[:, C_MN:C_MN + P] = np.where(i[None, :] <= i[:, None], 0.0, NEG)
    swap = np.zeros((P, P), np.float32)
    for o in range(P):
        j = o % 32
        if j < 16:
            swap[o + 16, o] = -1.0
        else:
            swap[o - 16, o] = 1.0
    c[:, C_SW:C_SW + P] = swap
    quarter = 16
    freqs = (np.float32(10000.0) ** (-np.arange(quarter, dtype=np.float32) / np.float32(quarter))).astype(np.float32)
    t = np.arange(SEQ)
    pos = np.stack([(t // GRID_W), (t % GRID_W)]).astype(np.float32)
    for p in range(P):
        ang = pos[(p % 64) // 32] * freqs[p % 16]
        c[p, C_COS:C_COS + SEQ] = np.cos(ang)
        c[p, C_SIN:C_SIN + SEQ] = np.sin(ang)
    return c


def head_norm_items():
    items = []
    for i in range(3):
        items.append(dict(kind="qa", i=i, start=i == 0, stop=i == 2, rope=False, t=T))
    for i in range(2):
        items.append(dict(kind="ckv", i=i, start=i == 0, stop=i == 1, rope=False, t=T))
    items.append(dict(kind="kr", i=0, start=True, stop=True, rope=True, t=T))
    for kind, n, rope in (("qn", MH, False), ("kn", MH, False), ("qr", MH // 2, True)):
        for i in range(n):
            items.append(dict(kind=kind, i=i, start=True, stop=True, rope=rope, t=T))
    n_even = len(items)
    for i in range(2):
        items.append(dict(kind="gk", i=i, start=True, stop=True, rope=True, t=T))
    for i in range(8):
        items.append(dict(kind="gq", i=i, start=True, stop=True, rope=True, t=SEQ))
    norms = ropes = 0
    for it in items:
        it["norm"] = norms
        it["nrope"] = ropes
        norms += it["stop"]
        ropes += it["rope"]
    return items, n_even


def build(nc, a, out):
    items, n_even = head_norm_items()
    norms_to = lambda m: sum(x["stop"] for x in items[:m])
    ropes_to = lambda m: sum(x["rope"] for x in items[:m])

    with ExitStack() as ctx:
        def sb(name, cols):
            return ctx.enter_context(nc.sbuf_tensor(name, [P, cols], F32))

        def sem(name):
            return ctx.enter_context(nc.semaphore(name))

        ps = ctx.enter_context(nc.psum_tensor("ps", [P, 4096], F32))

        def pair(p, n=T):
            return ps[:, 1024 * p:1024 * p + n]

        def bank(b, c0=0, c1=512):
            return ps[:, 512 * b + c0:512 * b + c1]

        h_sb = sb("h_sb", DB * T)
        u_sb = sb("u_sb", DB * T)
        big = sb("big", FB * T)
        mix = sb("mix", 16128)
        ring = sb("ring", RING * SLOT)
        cst = sb("cst", C_ALL)
        va, vb, vc = sb("va", VA_N), sb("vb", VB_N), sb("vc", VC_N)
        mod = sb("mod", 6 * 48)
        sc = sb("sc", 16)
        small = sb("small", 64)
        dskip = sb("dskip", 8)
        sink = sb("sink", QH)
        stat = sb("stat", 32)

        h = h_sb[:, :].rearrange("p (b t) -> p b t", t=T)
        u = u_sb[:, :].rearrange("p (b t) -> p b t", t=T)
        hid = big[:, :].rearrange("p (b t) -> p b t", t=T)

        def c_(at, n=P):
            return cst[:, at:at + n]

        ident, ones, blk64 = c_(C_ID), c_(C_ONE), c_(C_BLK)
        eps = small[:, 0:1]
        dtb, alog, aexp = small[0:32, 1:2], small[0:32, 2:3], small[0:32, 3:4]

        sqn = mix[:, 0:2 * T].rearrange("p (b t) -> p b t", t=T)
        rsn = mix[:, 2 * T:3 * T]
        xin = u_sb[:, :].rearrange("p (n d) -> p n d", d=D)
        rows = mix[:, 4096:4096 + 3 * P].rearrange("p (n d) -> p n d", d=P)
        kn = big[:, 0:8 * T].rearrange("p (b t) -> p b t", t=T)
        vt = big[:, 8 * T:8 * T + NT * D].rearrange("p (n d) -> p n d", d=D)
        ckv = big[:, 16 * T:18 * T].rearrange("p (b t) -> p b t", t=T)
        qa = big[:, 18 * T:21 * T].rearrange("p (b t) -> p b t", t=T)
        qn = mix[:, 0:8 * T].rearrange("p (b t) -> p b t", t=T)
        qr = mix[:, 8 * T:12 * T].rearrange("p (b t) -> p b t", t=T)
        kr = mix[:, 12 * T:13 * T]
        sqh = mix[:, 13 * T:15 * T].rearrange("p (b t) -> p b t", t=T)
        rsh = mix[:, 15 * T:17 * T].rearrange("p (b t) -> p b t", t=T)
        prob = mix[:, 17 * T:20 * T].rearrange("p (b t) -> p b t", t=T)
        probT = mix[:, 13 * T:15 * T].rearrange("p (b t) -> p b t", t=T)
        gq = big[:, 0:8 * T].rearrange("p (b t) -> p b t", t=T)
        gk = big[:, 8 * T:10 * T].rearrange("p (b t) -> p b t", t=T)
        gv = big[:, 10 * T:10 * T + NT * 256].rearrange("p (n d) -> p n d", d=256)
        go = big[:, 12 * T:20 * T].rearrange("p (b t) -> p b t", t=T)
        xs = big[:, 0:8 * T].rearrange("p (b t) -> p b t", t=T)
        bc = big[:, 8 * T:12 * T].rearrange("p (b t) -> p b t", t=T)
        z = big[:, 12 * T:20 * T].rearrange("p (b t) -> p b t", t=T)
        btok = big[:, 20 * T:20 * T + NT * 256].rearrange("p (n d) -> p n d", d=256)
        xtok = u_sb[:, :].rearrange("p (n d) -> p n d", d=D)
        PADC = T + 6
        pad = mix[:, 0:2 * PADC].rearrange("p (b t) -> p b t", t=PADC)
        cv = mix[:, 2 * PADC:4 * PADC].rearrange("p (b t) -> p b t", t=PADC)
        dtw = mix[0:32, 4 * PADC:4 * PADC + 5 * T].rearrange("p (b t) -> p b t", t=T)
        o_ = 4 * PADC + 5 * T
        st = mix[:, 0:5120].rearrange("p (d k n) -> p d k n", d=2, k=5)
        xdt = mix[:, 5120:7168].rearrange("p (b d n) -> p b d n", b=2, d=2)
        xw = xdt[:, 0, :, :]
        rr = mix[:, 7168:9216].rearrange("p (b d n) -> p b d n", b=2, d=2)
        ee = mix[:, 9216:12288].rearrange("p (b n) -> p b n", b=2)
        mf = mix[:, 12288:13312].rearrange("p (b n) -> p b n", b=2)
        gg = mix[:, 13312:14848].rearrange("p (c d n) -> p c d n", c=NT, d=2)
        dtk = mix[:, 14848:15232].rearrange("p (k c h) -> p k c h", k=2, c=NT)
        dec = mix[:, 15232:15616]
        wdt = mix[:, 15616:15808].rearrange("p (d c h) -> p d c h", d=2, c=NT)
        dcb = dec[:, 192:384].rearrange("p (c h) -> p c h", c=NT)
        assert 15808 <= 16128 and o_ <= 14848

        const_in, x_in, rows_in = sem("const_in"), sem("x_in"), sem("rows_in")
        w_full = [sem(f"w_full{i}") for i in range(RING)]
        w_used = sem("w_used")
        eps_set = sem("eps_set")
        vec_t, vec_done, sc_done = sem("vec_t"), sem("vec_done"), sem("sc_done")
        xt_done, h_loaded = sem("xt_done"), sem("h_loaded")
        mod_raw, mod_done = sem("mod_raw"), sem("mod_done")
        n_sq, n_ss, n_ln, n_rs, n_t, n_u = (sem("n_" + s) for s in ("sq", "ss", "ln", "rs", "t", "u"))
        f_silu, f_hid = sem("f_silu"), sem("f_hid")
        o_res = sem("o_res")
        hn_sq, hn_raw, hn_ss, hn_ln, hn_rs, hn_n, hn_rp, hn_sin, hn_cos, hn_fin = (
            sem("hn_" + s) for s in ("sq", "raw", "ss", "ln", "rs", "n", "rp", "sin", "cos", "fin"))
        v_mm, v_done = sem("v_mm"), sem("v_done")
        at_sc, at_mk, at_m0, at_m1, at_nm, at_ex, at_sk, at_l, at_ri, at_pn, at_tr, at_pt, at_pv, at_o = (
            sem("at_" + s) for s in ("sc", "mk", "m0", "m1", "nm", "ex", "sk", "l", "ri", "pn", "tr", "pt", "pv", "o"))
        pj_ev = sem("pj_ev")
        cv_pad, cv_tap, cv_out, pad_zero = sem("cv_pad"), sem("cv_tap"), sem("cv_out"), sem("pad_zero")
        dt_abs, dt_exp, dt_ln, dt_dt, dt_da = (sem("dt_" + s) for s in ("abs", "exp", "ln", "dt", "da"))
        a_exp = sem("a_exp")
        tk_dt, tk_dtc, tk_x, tk_xc, tk_b, tk_bc = (sem("tk_" + s) for s in ("dt", "dtc", "x", "xc", "b", "bc"))
        dc_mm, dc_exp, dc_w = sem("dc_mm"), sem("dc_exp"), sem("dc_w")
        s_xw, s_mm, s_dec, s_st = sem("s_xw"), sem("s_mm"), sem("s_dec"), sem("s_st")
        g_mm, g_done = sem("g_mm"), sem("g_done")
        y_xdt, y_r, y_seg, y_exp, y_m, y_mm, y_out = (sem("y_" + s) for s in ("xdt", "r", "seg", "exp", "m", "mm", "out"))
        m_z, m_sq, m_ss, m_ln, m_rs, m_y = (sem("m_" + s) for s in ("z", "sq", "ss", "ln", "rs", "y"))
        out_t, out_c, out_st = sem("out_t"), sem("out_c"), sem("out_st")

        rk = lambda w: w.rearrange("(k p) n -> p k n", p=P)
        w_mod = [rk(a["w_mod"][l]) for l in range(2)]
        w_ffi = [rk(a[n][l]) for l in range(2) for n in ("w_ff1_in", "w_ff2_in")]
        w_ffo = [rk(a[n][l]) for l in range(2) for n in ("w_ff1_out", "w_ff2_out")]
        w_ine, w_oute = rk(a["w_in_e"][0]), rk(a["w_out_e"][0])
        w_qb, w_kvb = rk(a["w_qb"][0]), rk(a["w_kvb"][0])
        w_ino, w_outo = rk(a["w_in_o"][0]), rk(a["w_out_o"][0])

        def slot(s, k, m=P):
            return ring[:, s * SLOT:s * SLOT + k * m].rearrange("p (k m) -> p k m", m=m)

        class Filler:

            def __init__(self, sp):
                self.sp, self.n = sp, 0

            def put(self, parts, i=None, per=0, c=0):
                s = (self.n + c) % RING
                if i is None:
                    if self.n >= RING:
                        self.sp.wait_ge(w_used, self.n - RING + 1)
                else:
                    self.sp.wait_ge(w_used, i * per + (self.n + c - RING + 1))
                for dst, src in parts(s):
                    self.sp.dma_start(dst, src).then_inc(w_full[s], 16)
                if i is None:
                    self.n += 1

        class Drainer:

            def __init__(self, pe):
                self.pe, self.n, self.landed = pe, 0, [0] * RING

            def get(self, i=None, per=0, c=0, parts=1):
                s = (self.n + c) % RING
                if i is None:
                    self.landed[s] += parts
                    self.n += 1
                    self.pe.wait_ge(w_full[s], 16 * self.landed[s])
                else:
                    self.pe.wait_ge(w_full[s], i * (16 * per // RING) + 16 * (self.landed[s] + c // RING + 1))
                return s

            def passed(self, count):
                self.n += count
                self.landed = [x + count // RING for x in self.landed]

        def block(w, k0, k, c0, m=P):
            return lambda s: [(slot(s, k, m), w[:, k0:k0 + k, bass.ds(c0, m)])]

        OUT = [
            (w_ffo[0], 0, FB, T, 0, 1, hid),
            (w_oute, 8, 8, T, 1, None, qn),
            (w_oute, 0, 8, T, 1, 2, xs),
            (w_ffo[1], 0, FB, T, 2, 3, hid),
            (w_ffo[2], 0, FB, T, 3, 4, hid),
            (w_outo, 0, 8, SEQ, 4, 5, go),
            (w_ffo[3], 0, FB, SEQ, 5, None, hid),
        ]

        def out_plan(r):
            w, k0, nk, t, g, gn, act = OUT[r]
            chunks = [("w", k, min(8, nk - k)) for k in range(0, nk, 8)]
            if gn is not None:
                first, chunks = chunks[:-1], chunks[-1:]
                mods = [("m", q, 8) for q in range(3)]
                while mods:
                    chunks.insert(-1, mods.pop(0))
                    if first:
                        chunks.insert(-1, first.pop(0))
            per_d = len(chunks)
            dpb = 2 if gn is not None else 4
            assert per_d * dpb % RING == 0 and chunks[-1][0] == "w"
            return chunks, per_d, dpb

        def sync_out(f, r):
            w, k0, nk, t, g, gn, act = OUT[r]
            chunks, per_d, dpb = out_plan(r)
            per = per_d * dpb
            with f.sp.Fori(1, DB // dpb + 1) as i:
                for dd in range(-dpb, 0):
                    for c, (what, k, n) in enumerate(chunks):
                        if what == "w":
                            f.put(block(w, k0 + k, n, i * (dpb * P) + dd * P), i, per, dd * per_d + c)
                        else:
                            col = (gn % 3 * 3 + k) * D + dd * P
                            f.put(block(w_mod[gn // 3], 0, 8, i * (dpb * P) + col), i, per, dd * per_d + c)
            f.n += per * (DB // dpb)


        BASE = {}
        n_ = 0
        for name, count in [("mod", 24), ("ffi0", 2 * FB), ("out0", 0), ("even", n_even), ("v_e", 2),
                            ("out1", 0), ("proj", 21), ("out2", 0), ("ffi1", 2 * FB), ("out3", 0),
                            ("ffi2", 2 * FB), ("out4", 0), ("odd", len(items) - n_even), ("v_o", 2),
                            ("out5", 0), ("ffi3", 2 * FB), ("out6", 0)]:
            BASE[name] = n_
            if name.startswith("out"):
                chunks, per_d, dpb = out_plan(int(name[3:]))
                count = per_d * DB
            n_ += count
        for f_ in range(4):
            assert (2 * FB) % RING == 0

        def mod_group(g):
            return mod[:, 48 * g:48 * g + 48].rearrange("p (q d s) -> p q d s", q=3, d=8)

        def bmod(g):
            v = va if g < 3 else vb
            return v[:, g % 3 * 24:g % 3 * 24 + 24].rearrange("p (q d) -> p q d", q=3)

        NORM_T = [T, T, T, T, T, SEQ]
        NORM_AFTER = [None, 0, 2, 3, 4, 5]

        def h_ready(eng, n, d):
            if n == 0:
                eng.wait_ge(h_loaded, d + 1)
            else:
                eng.wait_ge(o_res, 8 * NORM_AFTER[n] + d + 1)

        def act_norm(act, n):
            t = NORM_T[n]
            for d in range(DB):
                h_ready(act, n, d)
                if n or d >= 2:
                    if 8 * n + d - 1 > 0:
                        act.wait_ge(n_ss, 8 * n + d - 1)
                act.activation(sqn[:, d % 2, :t], h[:, d, :t], ACT.Square).then_inc(n_sq, 1)
            act.wait_ge(n_ss, 8 * n + 8)
            if n == 0:
                act.wait_ge(eps_set, 1)
            act.activation(rsn[:, :t], pair(3, t), ACT.Ln, bias=eps, scale=1.0 / D).then_inc(n_ln, 1)
            act.wait_ge(n_ln, n + 1)
            act.activation(rsn[:, :t], rsn[:, :t], ACT.Exp, scale=-0.5).then_inc(n_rs, 1)
            for d in range(DB):
                act.wait_ge(n_t, 8 * n + d + 1)
                for t0, t1, s in SEGS:
                    if t0 < t:
                        x = act.activation(u[:, d, t0:t1], u[:, d, t0:t1], ACT.Identity,
                                           bias=mod_group(n)[:, 0, d, s:s + 1])
                x.then_inc(n_u, 1)

        def pe_norm(pe, n):
            t = NORM_T[n]
            if n == 0:
                pe.wait_ge(const_in, 16)
            for d in range(DB):
                pe.wait_ge(n_sq, 8 * n + d + 1)
                for c0 in range(0, t, 512):
                    c1 = min(t, c0 + 512)
                    mm = pe.matmul(pair(3)[:, c0:c1], ones, sqn[:, d % 2, c0:c1], start=d == 0, stop=d == DB - 1)
                mm.then_inc(n_ss, 1)

        def dve_norm(dve, n):
            t = NORM_T[n]
            dve.wait_ge(n_rs, n + 1)
            dve.wait_ge(mod_done, n + 1)
            for d in range(DB):
                h_ready(dve, n, d)
                for t0, t1, s in SEGS:
                    if t0 < t:
                        x = dve.scalar_tensor_tensor(out=u[:, d, t0:t1], in0=h[:, d, t0:t1],
                                                     scalar=mod_group(n)[:, 1, d, s:s + 1],
                                                     in1=rsn[:, t0:t1], op0=ALU.mult, op1=ALU.mult)
                x.then_inc(n_t, 1)

        def pe_mod_block(pe, s, col):
            at = ps[:, 2048 + col:2050 + col] if isinstance(col, int) else ps[:, bass.ds(col + 2048, 2)]
            for k in range(8):
                mm = pe.matmul(at, slot(s, 8)[:, k, :], sc[:, 2 * k:2 * k + 2], start=k == 0, stop=k == 7)
            mm.then_inc(w_used, 1)

        def dve_mod(dve, g, end):
            dve.wait_ge(w_used, end)
            raw = bank(4, 0, 48).rearrange("p (q d s) -> p q d s", q=3, d=8)
            m = mod_group(g)
            for q in range(3):
                for s in range(2):
                    x = dve.scalar_tensor_tensor(out=m[:, q, :, s], in0=raw[:, q, :, s],
                                                 scalar=1.0 if q == 1 else 0.0, in1=bmod(g)[:, q, :],
                                                 op0=ALU.add, op1=ALU.add)
            x.then_inc(mod_raw, 1)
            dve.wait_ge(mod_raw, g + 1)
            dve.tensor_scalar(m[:, 2, :, :], m[:, 2, :, :], 1.0 if g % 3 == 1 else 0.5, None,
                              ALU.mult).then_inc(mod_done, 1)

        FF_NORM = [0, 2, 3, 5]
        FF_T = [T, T, T, SEQ]

        def sync_ffi(f, i_f):
            with f.sp.Fori(0, FB // 2) as i:
                for jj in range(2):
                    for half in range(2):
                        col = half * FFN + jj * P
                        f.put(block(w_ffi[i_f], 0, 8, i * (2 * P) + col), i, 4, 2 * jj + half)
            f.n += 2 * FB

        def pe_ffi(pe, dr, i_f):
            n, t = FF_NORM[i_f], FF_T[i_f]

            def body(i):
                for jj in range(2):
                    for half, sem_ in ((0, f_silu), (1, f_hid)):
                        v = FB * i_f + jj - 1
                        if not isinstance(i, int):
                            pe.wait_ge(sem_, i * 2 + v)
                        elif 2 * i + v > 0:
                            pe.wait_ge(sem_, 2 * i + v)
                        s = dr.get(i, 4, 2 * jj + half)
                        for k in range(DB):
                            if isinstance(i, int) and i == 0 and jj == 0 and half == 0:
                                pe.wait_ge(n_u, 8 * n + k + 1)
                            for c0 in range(0, t, 512):
                                c1 = min(t, c0 + 512)
                                mm = pe.matmul(pair(2 * half + jj)[:, c0:c1], slot(s, 8)[:, k, :],
                                               u[:, k, c0:c1], start=k == 0, stop=k == DB - 1)
                        mm.then_inc(w_used, 1)

            body(0)
            with pe.Fori(1, FB // 2) as i:
                body(i)
            dr.passed(2 * FB)

        def act_ffi(act, i_f):
            t, b = FF_T[i_f], BASE[f"ffi{i_f}"]
            with act.Fori(0, FB // 2) as i:
                for jj in range(2):
                    act.wait_ge(w_used, i * 4 + (b + 2 * jj + 1))
                    act.activation(hid[:, bass.ds(i * 2 + jj, 1), :t],
                                   pair(jj, t).rearrange("p (o t) -> p o t", o=1), ACT.Silu).then_inc(f_silu, 1)

        def dve_ffi(dve, i_f):
            t, b = FF_T[i_f], BASE[f"ffi{i_f}"]
            with dve.Fori(0, FB // 2) as i:
                for jj in range(2):
                    dve.wait_ge(w_used, i * 4 + (b + 2 * jj + 2))
                    dve.wait_ge(f_silu, i * 2 + (FB * i_f + jj + 1))
                    dve.tensor_tensor(hid[:, bass.ds(i * 2 + jj, 1), :t], hid[:, bass.ds(i * 2 + jj, 1), :t],
                                      pair(2 + jj, t).rearrange("p (o t) -> p o t", o=1),
                                      ALU.mult).then_inc(f_hid, 1)

        def pe_out(pe, dr, r):
            w, k0, nk, t, g, gn, src = OUT[r]
            chunks, per_d, dpb = out_plan(r)
            per = per_d * dpb

            def body(i):
                for dd in range(dpb):
                    v = 8 * r + dd - 1
                    if not isinstance(i, int):
                        pe.wait_ge(o_res, i * dpb + v)
                    elif v + i * dpb > 0:
                        pe.wait_ge(o_res, v + i * dpb)
                    for c, (what, k, n) in enumerate(chunks):
                        s = dr.get(i, per, dd * per_d + c)
                        if what == "m":
                            pe_mod_block(pe, s, i * (2 * dpb) + (16 * k + 2 * dd))
                            continue
                        for kk in range(n):
                            for c0 in range(0, t, 512):
                                c1 = min(t, c0 + 512)
                                mm = pe.matmul(pair(dd % 2)[:, c0:c1], slot(s, n)[:, kk, :],
                                               src[:, k + kk, c0:c1],
                                               start=k + kk == 0, stop=k + kk == nk - 1)
                        mm.then_inc(w_used, 1)

            body(0)
            with pe.Fori(1, DB // dpb) as i:
                body(i)
            dr.passed(per_d * DB)

        def dve_out(dve, r):
            w, k0, nk, t, g, gn, src = OUT[r]
            chunks, per_d, dpb = out_plan(r)
            b = BASE[f"out{r}"]
            for d in range(DB):
                dve.wait_ge(w_used, b + (d + 1) * per_d)
                for t0, t1, s in SEGS:
                    if t0 < t:
                        x = dve.scalar_tensor_tensor(out=h[:, d, t0:t1], in0=pair(d % 2)[:, t0:t1],
                                                     scalar=mod_group(g)[:, 2, d, s:s + 1],
                                                     in1=h[:, d, t0:t1], op0=ALU.mult, op1=ALU.add)
                x.then_inc(o_res, 1)
            if gn is not None:
                dve_mod(dve, gn, b + DB * per_d)

        GAIN = {"qn": VB_QN, "kn": VB_KN, "qr": VB_QR, "kr": VB_KR, "gq": VB_GQ, "gk": VB_GK}
        WIDTH = {"qa": 384, "ckv": 256, "kr": 64, "qn": 128, "kn": 128, "qr": 64, "gk": 64, "gq": 64}
        DST = {"qa": qa, "ckv": ckv, "qn": qn, "kn": kn, "qr": qr, "gk": gk, "gq": gq}

        def dst_of(it):
            return kr if it["kind"] == "kr" else DST[it["kind"]][:, it["i"], :]

        def gain_of(it):
            k = {"qa": VB_QA + it["i"], "ckv": VB_KV + it["i"]}.get(it["kind"], GAIN.get(it["kind"]))
            return vb[:, k:k + 1]

        def item_chunk(it):
            kind, i = it["kind"], it["i"]
            if kind == "qa":
                return block(w_ine, 0, 8, QA0 + P * i)
            if kind == "ckv":
                return block(w_ine, 0, 8, CKV0 + P * i)
            if kind == "kr":
                return None
            if kind == "qn":
                return block(w_qb, 0, 3, i * (DN + DR))
            if kind == "kn":
                return block(w_kvb, 0, 2, i * (DN + DV))
            if kind == "gk":
                return block(w_ino, 0, 8, QH * HD + P * i)
            if kind == "qr":
                c0 = 2 * i * (DN + DR) + DN
                return lambda s: [(slot(s, 3)[:, :, 64 * e:64 * e + 64],
                                   w_qb[:, :, c0 + e * (DN + DR):c0 + e * (DN + DR) + 64]) for e in range(2)]
            c0 = HD * (8 * (i // 4) + i % 4)
            return lambda s: [(slot(s, 8)[:, :, 64 * e:64 * e + 64],
                               w_ino[:, :, c0 + 4 * HD * e:c0 + 4 * HD * e + 64]) for e in range(2)]

        def item_in(it):
            return {"qn": (3, qa), "qr": (3, qa), "kn": (2, ckv)}.get(it["kind"], (8, u))

        def sync_items(f, m0, m1):
            for m in range(m0, m1):
                it = items[m]
                if it["kind"] == "kr":
                    src = w_ine[:, :, KR0:KR0 + DR]
                    s = f.n % RING
                    f.sp.wait_ge(w_used, f.n - RING + 1)
                    f.sp.dma_start(slot(s, 8)[:, :, 0:64], src).then_inc(w_full[s], 16)
                    f.n += 1
                else:
                    f.put(item_chunk(it))

        def pe_items(pe, dr, m0, m1, norm_n):
            for q in range(m0, m1 + 2):
                if q < m1:
                    it = items[q]
                    nk, src = item_in(it)
                    if q - m0 >= 2:
                        pe.wait_ge(hn_raw, q - 1)
                    if q == m0:
                        pe.wait_ge(n_u, 8 * norm_n + 8)
                    if it["kind"] in ("qn", "qr", "kn"):
                        pe.wait_ge(hn_n, 2 if it["kind"] == "kn" else 1)
                    s = dr.get(parts=2 if it["kind"] in ("qr", "gq") else 1)
                    for k in range(nk):
                        for c0 in range(0, it["t"], 512):
                            c1 = min(it["t"], c0 + 512)
                            if it["kind"] == "kr":
                                for e in range(2):
                                    mm = pe.matmul(pair(q % 2)[64 * e:64 * e + 64, c0:c1], slot(s, 8)[:, k, 0:64],
                                                   src[:, k, c0:c1], start=k == 0, stop=k == nk - 1)
                            else:
                                mm = pe.matmul(pair(q % 2)[:, c0:c1], slot(s, nk)[:, k, :], src[:, k, c0:c1],
                                               start=k == 0, stop=k == nk - 1)
                    mm.then_inc(w_used, 1)
                m = q - 1
                if m0 <= m < m1:
                    it = items[m]
                    pe.wait_ge(hn_sq, m + 1)
                    if it["start"] and it["norm"] > 0:
                        pe.wait_ge(hn_ln, it["norm"])
                    w = blk64 if WIDTH[it["kind"]] == 64 else ones
                    for c0 in range(0, it["t"], 512):
                        c1 = min(it["t"], c0 + 512)
                        mm = pe.matmul(pair(2)[:, c0:c1], w, sqh[:, m % 2, c0:c1], start=it["start"], stop=it["stop"])
                    mm.then_inc(hn_ss, 1)
                m = q - 2
                if m0 <= m < m1 and items[m]["rope"]:
                    it = items[m]
                    pe.wait_ge(hn_n, it["norm"] + 1)
                    if it["nrope"] > 0:
                        pe.wait_ge(hn_sin, it["nrope"])
                    pe.matmul(bank(6), c_(C_SW), dst_of(it)[:, 0:SEQ], start=True, stop=True).then_inc(hn_rp, 1)

        def act_items(act, m0, m1, base):
            for q in range(m0, m1 + 1):
                if q < m1:
                    it = items[q]
                    t = it["t"]
                    act.wait_ge(w_used, base + q - m0 + 1)
                    if q >= 2:
                        act.wait_ge(hn_ss, q - 1)
                    act.activation(sqh[:, q % 2, :t], pair(q % 2, t), ACT.Square).then_inc(hn_sq, 1)
                    act.activation(dst_of(it)[:, :t], pair(q % 2, t), ACT.Identity,
                                   scale=gain_of(it)).then_inc(hn_raw, 1)
                m = q - 1
                if m0 <= m and items[m]["stop"]:
                    it = items[m]
                    t, nn = it["t"], it["norm"]
                    act.wait_ge(hn_ss, m + 1)
                    if nn >= 2:
                        act.wait_ge(hn_n, nn - 1)
                        last = [x for x in items if x["stop"]][nn - 2]
                        if last["rope"]:
                            act.wait_ge(hn_fin, last["nrope"] + 1)
                    act.activation(rsh[:, nn % 2, :t], pair(2, t), ACT.Ln, bias=eps,
                                   scale=1.0 / WIDTH[it["kind"]]).then_inc(hn_ln, 1)
                    act.wait_ge(hn_ln, nn + 1)
                    act.activation(rsh[:, nn % 2, :t], rsh[:, nn % 2, :t], ACT.Exp, scale=-0.5).then_inc(hn_rs, 1)

        def dve_items(dve, m0, m1):
            for m in range(m0, m1):
                it = items[m]
                if not it["stop"]:
                    continue
                t, nn, kind = it["t"], it["norm"], it["kind"]
                dve.wait_ge(hn_rs, nn + 1)
                dve.wait_ge(hn_raw, m + 1)
                for i in range(it["i"] + 1 if kind in ("qa", "ckv") else 1):
                    d = DST[kind][:, i, :t] if kind in ("qa", "ckv") else dst_of(it)[:, :t]
                    x = dve.tensor_tensor(d, d, rsh[:, nn % 2, :t], ALU.mult)
                x.then_inc(hn_n, 1)
                if it["rope"]:
                    d, nr = dst_of(it)[:, 0:SEQ], it["nrope"]
                    tmp = rsh[:, nn % 2, 0:SEQ]
                    dve.wait_ge(hn_rp, nr + 1)
                    dve.tensor_tensor(tmp, cst[:, C_SIN:C_SIN + SEQ], bank(6), ALU.mult).then_inc(hn_sin, 1)
                    dve.tensor_tensor(d, d, cst[:, C_COS:C_COS + SEQ], ALU.mult).then_inc(hn_cos, 1)
                    dve.wait_ge(hn_sin, nr + 1)
                    dve.wait_ge(hn_cos, nr + 1)
                    dve.tensor_tensor(d, d, tmp, ALU.add).then_inc(hn_fin, 1)

        def sync_v(f, which):
            for half in range(2):
                if which == "e":
                    src = w_kvb.rearrange("p k (h n) -> p k h n", n=DN + DV)[:, :, 4 * half:4 * half + 4, DN:DN + DV]
                    f.put(lambda s, src=src: [(slot(s, 2, 512)[:, k, :].rearrange("p (h n) -> p h n", n=DV),
                                               src[:, k]) for k in range(2)])
                else:
                    f.put(block(w_ino, 0, 8, (QH + KVH) * HD + P * half))

        def pe_v(pe, dr, which):
            nk, m, src = (2, 512, ckv) if which == "e" else (8, P, u)
            off = 0 if which == "e" else 12
            for half in range(2):
                s = dr.get(parts=2 if which == "e" else 1)
                for n in range(NT):
                    q = half * NT + n
                    if q >= 4:
                        pe.wait_ge(v_done, off + q - 3)
                    elif q == 0:
                        pe.wait_ge(hn_raw, n_even if which == "e" else len(items))
                    for k in range(nk):
                        mm = pe.matmul(bank(q % 4, 0, m), src[:, k, P * n:P * n + P], slot(s, nk, m)[:, k, :],
                                       start=k == 0, stop=k == nk - 1)
                    mm.then_inc(w_used if n == NT - 1 else v_mm, 1)

        def dve_v(dve, which):
            m, dst, base = (512, vt, BASE["v_e"]) if which == "e" else (P, gv, BASE["v_o"])
            off = 0 if which == "e" else 10
            for half in range(2):
                for n in range(NT):
                    if n < NT - 1:
                        dve.wait_ge(v_mm, off + 5 * half + n + 1)
                    else:
                        dve.wait_ge(w_used, base + half + 1)
                    dve.tensor_copy(dst[:, n, m * half:m * half + m], bank((half * NT + n) % 4, 0, m)).then_inc(v_done, 1)

        units = []
        for hh in range(MH):
            e = 64 * (hh % 2)
            for qt in range(NT):
                q0 = P * qt
                keys = [(0, SEQ), (SEQ, T)] if qt < 4 else [(SEQ, T)]
                sco = []
                at = 0
                for k0, k1 in keys:
                    sco.append((qn[:, hh, q0:q0 + P], kn[:, hh, k0:k1], at, True, False))
                    sco.append((qr[e:e + 64, hh // 2, q0:q0 + P], kr[e:e + 64, k0:k1], at, False, True))
                    at += k1 - k0
                tiles = range(NT) if qt < 4 else range(4, NT)
                units.append(dict(sc=sco, n=at, masks=[], scale=(DN + DR) ** -0.5, sink=None, m=DV, o=0,
                                  v=[vt[:, k, DV * hh:DV * hh + DV] for k in tiles], out=qn[:, hh, q0:q0 + P]))
        n_mla = len(units)
        for hh in range(QH):
            b, e8, ii = hh // 8, (hh % 8) // 4, hh % 4
            e, g = 64 * e8, hh // 4
            for qt in range(SEQ // P):
                q0 = P * qt
                q = gq[e:e + 64, 4 * b + ii, q0:q0 + P]
                sco = [(q, gk[e:e + 64, b, SEQ:T], 0, True, True)]
                tiles = [4, 5]
                masks = []
                lo, hi = max(0, qt - 1), min(3, qt + 1)
                if qt > 0:
                    masks.append((256, c_(C_MP)))
                if qt < 3:
                    masks.append((256 + P * (qt + 1 - lo), c_(C_MN)))
                sco.append((q, gk[e:e + 64, b, P * lo:P * lo + 256], 256, True, True))
                if hi - lo == 2:
                    sco.append((q, gk[e:e + 64, b, P * hi:P * hi + P], 512, True, True))
                tiles += list(range(lo, hi + 1))
                units.append(dict(sc=sco, n=P * len(tiles), masks=masks, scale=HD ** -0.5,
                                  sink=sink[:, hh:hh + 1], m=HD, o=64 * (hh % 2),
                                  v=[gv[:, k, HD * g:HD * g + HD] for k in tiles],
                                  out=go[64 * (hh % 2):64 * (hh % 2) + 64, hh // 2, q0:q0 + P]))
        n_mask = n_sink = 0
        for x in units:
            x["nmask"], x["nsink"] = n_mask, n_sink
            n_mask += len(x["masks"])
            n_sink += x["sink"] is not None

        def pe_attend(pe, u0, u1):
            for q in range(u0, u1 + 3):
                if q < u1:
                    x = units[q]
                    if q - u0 >= 2:
                        pe.wait_ge(at_ex, q - 1)
                    for lhs, rhs, c0, start, stop in x["sc"]:
                        mm = pe.matmul(pair(q % 2, 1024)[:, c0:c0 + rhs.shape[-1]], lhs, rhs, start=start, stop=stop)
                    mm.then_inc(at_sc, 1)
                i = q - 2
                if u0 <= i < u1:
                    pe.wait_ge(at_pn, i + 1)
                    if i > u0:
                        pe.wait_ge(at_pt, i)
                    nb = units[i]["n"] // P
                    for k in range(nb):
                        mm = pe.transpose(pair(2)[:, P * k:P * k + P], prob[:, i % 3, P * k:P * k + P], ident)
                    mm.then_inc(at_tr, 1)
                i = q - 3
                if u0 <= i < u1:
                    x = units[i]
                    pe.wait_ge(at_pt, i + 1)
                    if i - u0 >= 2:
                        pe.wait_ge(at_o, i - 1)
                    for k, v in enumerate(x["v"]):
                        mm = pe.matmul(bank(6 + i % 2)[x["o"]:x["o"] + x["m"], 0:P], v, probT[:, i % 2, P * k:P * k + P],
                                       start=k == 0, stop=k == len(x["v"]) - 1)
                    mm.then_inc(at_pv, 1)

        def act_attend(act, u0, u1):
            for q in range(u0, u1 + 2):
                if q < u1:
                    x = units[q]
                    act.wait_ge(at_nm, q + 1)
                    if q >= 3:
                        act.wait_ge(at_tr, q - 2)
                    act.activation(prob[:, q % 3, :x["n"]], pair(q % 2, 1024)[:, :x["n"]], ACT.Exp,
                                   bias=stat[:, 4 + q % 4:5 + q % 4], scale=x["scale"],
                                   accum_out=stat[:, 8 + q % 4:9 + q % 4]).then_inc(at_ex, 1)
                    if x["sink"] is not None:
                        act.activation(stat[:, 12 + q % 4:13 + q % 4], x["sink"], ACT.Exp,
                                       bias=stat[:, 4 + q % 4:5 + q % 4]).then_inc(at_sk, 1)
                i = q - 2
                if u0 <= i:
                    act.wait_ge(at_tr, i + 1)
                    if i >= 2:
                        act.wait_ge(at_pv, i - 1)
                    n = units[i]["n"]
                    act.copy(probT[:, i % 2, :n], pair(2, n)).then_inc(at_pt, 1)

        def dve_attend(dve, u0, u1):
            for q in range(u0, u1 + 3):
                if q < u1:
                    x = units[q]
                    dve.wait_ge(at_sc, q + 1)
                    s = pair(q % 2, 1024)
                    for c0, mk in x["masks"]:
                        dve.tensor_tensor(s[:, c0:c0 + P], mk, s[:, c0:c0 + P], ALU.add).then_inc(at_mk, 1)
                    if x["masks"]:
                        dve.wait_ge(at_mk, x["nmask"] + len(x["masks"]))
                    m = stat[:, q % 4:q % 4 + 1]
                    dve.tensor_reduce(m, s[:, :x["n"]], AX, ALU.max).then_inc(at_m0, 1)
                    dve.wait_ge(at_m0, q + 1)
                    nm = stat[:, 4 + q % 4:5 + q % 4]
                    if x["sink"] is not None:
                        dve.tensor_scalar(m, m, x["scale"], x["sink"], ALU.mult, ALU.max).then_inc(at_m1, 1)
                        dve.wait_ge(at_m1, x["nsink"] + 1)
                        dve.tensor_scalar(nm, m, -1.0, None, ALU.mult).then_inc(at_nm, 1)
                    else:
                        dve.tensor_scalar(nm, m, -x["scale"], None, ALU.mult).then_inc(at_nm, 1)
                i = q - 1
                if u0 <= i < u1:
                    x = units[i]
                    ls = stat[:, 8 + i % 4:9 + i % 4]
                    dve.wait_ge(at_ex, i + 1)
                    if x["sink"] is not None:
                        dve.wait_ge(at_sk, x["nsink"] + 1)
                        dve.tensor_tensor(ls, ls, stat[:, 12 + i % 4:13 + i % 4], ALU.add).then_inc(at_l, 1)
                        dve.wait_ge(at_l, x["nsink"] + 1)
                    ri = stat[:, 16 + i % 4:17 + i % 4]
                    dve.reciprocal(ri, ls).then_inc(at_ri, 1)
                    dve.wait_ge(at_ri, i + 1)
                    dve.tensor_scalar(prob[:, i % 3, :x["n"]], prob[:, i % 3, :x["n"]], ri, None,
                                      ALU.mult).then_inc(at_pn, 1)
                i = q - 3
                if u0 <= i < u1:
                    x = units[i]
                    dve.wait_ge(at_pv, i + 1)
                    dve.tensor_copy(x["out"], bank(6 + i % 2)[x["o"]:x["o"] + x["m"], 0:P]).then_inc(at_o, 1)

        PJ = [("dt", 0)] + [("c", i) for i in range(12)] + [("z", i) for i in range(8)]

        def sync_proj(f):
            f.put(block(w_ine, 0, 8, DT0, 32))
            with f.sp.Fori(0, 3) as i:
                for c in range(4):
                    f.put(block(w_ine, 0, 8, i * 512 + (XBC0 + P * c)), i, 4, c)
            f.n += 12
            with f.sp.Fori(0, 2) as i:
                for c in range(4):
                    f.put(block(w_ine, 0, 8, i * 512 + (Z0 + P * c)), i, 4, c)
            f.n += 8

        def pe_proj(pe, dr):
            def product(q, m, s):
                for k in range(DB):
                    for c0 in range(0, T, 512):
                        c1 = min(T, c0 + 512)
                        mm = pe.matmul(pair(q % 4)[0:m, c0:c1], slot(s, 8, m)[:, k, :], u[:, k, c0:c1],
                                       start=k == 0, stop=k == DB - 1)
                mm.then_inc(w_used, 1)

            pe.wait_ge(o_res, 8 * 1 + 8)
            product(0, 32, dr.get())
            for q in range(1, 5):
                if q == 4:
                    pe.wait_ge(pj_ev, 1)
                product(q, P, dr.get())
            with pe.Fori(1, 5) as i:
                for c in range(4):
                    pe.wait_ge(pj_ev, i * 4 + (c - 2))
                    product(1 + c, P, dr.get(i - 1, 4, c))
            dr.passed(16)

        def act_proj(act):
            b = BASE["proj"]
            for q in range(len(PJ) + 1):
                if q < len(PJ):
                    kind, i = PJ[q]
                    act.wait_ge(w_used, b + q + 1)
                    if kind == "dt":
                        act.activation(dtw[:, 0, :], pair(0)[0:32, :], ACT.Identity, bias=dtb).then_inc(pj_ev, 1)
                    elif kind == "c":
                        if i == 0:
                            act.wait_ge(pad_zero, 1)
                        if i >= 2:
                            act.wait_ge(cv_tap, 5 * (i - 1))
                        act.copy(pad[:, i % 2, 2:2 + SEQ], pair(q % 4)[:, 0:SEQ]).then_inc(cv_pad, 1)
                        act.copy(pad[:, i % 2, 4 + SEQ:4 + T], pair(q % 4)[:, SEQ:T]).then_inc(pj_ev, 1)
                    else:
                        act.activation(z[:, i, :], pair(q % 4), ACT.Silu).then_inc(pj_ev, 1)
                if q >= 2 and PJ[q - 1][0] == "c":
                    i = PJ[q - 1][1]
                    act.wait_ge(cv_tap, 5 * (i + 1))
                    dst = xs[:, i, :] if i < 8 else bc[:, i - 8, :]
                    bias = vb[:, VB_CB + i:VB_CB + i + 1]
                    act.activation(dst[:, 0:SEQ], cv[:, i % 2, 0:SEQ], ACT.Silu, bias=bias)
                    act.activation(dst[:, SEQ:T], cv[:, i % 2, 2 + SEQ:2 + T], ACT.Silu, bias=bias).then_inc(cv_out, 1)
            act.wait_ge(pj_ev, 1)
            act.activation(dtw[:, 1, :], dtw[:, 0, :], ACT.Abs).then_inc(dt_abs, 1)
            act.wait_ge(dt_abs, 1)
            act.activation(dtw[:, 1, :], dtw[:, 1, :], ACT.Exp, scale=-1.0).then_inc(dt_exp, 1)
            act.wait_ge(dt_exp, 1)
            act.activation(dtw[:, 2, :], dtw[:, 1, :], ACT.Ln, bias=1.0).then_inc(dt_ln, 1)
            act.activation(aexp, alog, ACT.Exp).then_inc(a_exp, 1)

        def dve_proj(dve):
            dve.wait_ge(at_o, n_mla)
            dve.wait_ge(o_res, 16)
            for b in range(2):
                dve.memset(pad[:, b, 0:2], 0.0)
                dve.memset(pad[:, b, 2 + SEQ:4 + SEQ], 0.0)
                x = dve.memset(pad[:, b, 4 + T:6 + T], 0.0)
            x.then_inc(pad_zero, 1)
            dve.wait_ge(pad_zero, 1)
            n = T + 2
            for i in range(12):
                dve.wait_ge(cv_pad, i + 1)
                dve.wait_ge(pj_ev, i + 2)
                if i >= 2:
                    dve.wait_ge(cv_out, i - 1)
                y = cv[:, i % 2, 0:n]
                for tap in range(5):
                    w = vc[:, 12 * tap + i:12 * tap + i + 1]
                    if tap:
                        dve.wait_ge(cv_tap, 5 * i + tap)
                        dve.scalar_tensor_tensor(out=y, in0=pad[:, i % 2, tap:tap + n], scalar=w, in1=y,
                                                 op0=ALU.mult, op1=ALU.add).then_inc(cv_tap, 1)
                    else:
                        dve.tensor_scalar(y, pad[:, i % 2, 0:n], w, None, ALU.mult).then_inc(cv_tap, 1)
            dve.wait_ge(dt_ln, 1)
            dve.scalar_tensor_tensor(out=dtw[:, 3, :], in0=dtw[:, 0, :], scalar=0.0, in1=dtw[:, 2, :],
                                     op0=ALU.max, op1=ALU.add).then_inc(dt_dt, 1)
            dve.wait_ge(dt_dt, 1)
            dve.wait_ge(a_exp, 1)
            dve.tensor_scalar(dtw[:, 4, :], dtw[:, 3, :], aexp, -1.0, ALU.mult, ALU.mult).then_inc(dt_da, 1)

        ORDER = ((4, 5, 0, 1, 2, 3), (5, 4, 3, 2, 1, 0))

        def pe_turn(pe):
            pe.wait_ge(dt_da, 1)
            pe.wait_ge(pj_ev, len(PJ))
            for kk in range(2):
                for c in range(NT):
                    mm = pe.transpose(bank(0)[:, 192 * kk + 32 * c:192 * kk + 32 * c + 32],
                                      dtw[:, 3 + kk, P * c:P * c + P], ident[0:32, 0:32])
            mm.then_inc(tk_dt, 1)
            pe.wait_ge(cv_out, 12)
            for c in range(NT):
                if c >= 2:
                    pe.wait_ge(tk_xc, c - 1)
                for b in range(8):
                    mm = pe.transpose(pair(1 + c % 2, 1024)[:, P * b:P * b + P], xs[:, b, P * c:P * c + P], ident)
                mm.then_inc(tk_x, 1)
            for c2 in range(3):
                if c2 == 2:
                    pe.wait_ge(tk_bc, 1)
                for k in range(4):
                    c, g = 2 * c2 + k // 2, k % 2
                    mm = pe.transpose(bank(6 + c2 % 2)[:, P * k:P * k + P], bc[:, g, P * c:P * c + P], ident)
                mm.then_inc(tk_b, 1)

        def dve_turn(dve):
            dve.wait_ge(tk_dt, 1)
            dve.tensor_copy(mix[:, 14848:15232], bank(0, 0, 384)).then_inc(tk_dtc, 1)
            for c in range(NT):
                dve.wait_ge(tk_x, c + 1)
                dve.tensor_copy(xtok[:, c, :], pair(1 + c % 2, 1024)).then_inc(tk_xc, 1)
            for c2 in range(3):
                dve.wait_ge(tk_b, c2 + 1)
                dve.tensor_copy(big[:, 20 * T + 512 * c2:20 * T + 512 * c2 + 512], bank(6 + c2 % 2)).then_inc(tk_bc, 1)
            dve.wait_ge(dc_exp, 1)
            dve.tensor_tensor(wdt[:, 0], dec[:, 0:96].rearrange("p (c h) -> p c h", c=NT), dtk[:, 0, :, 0:16], ALU.mult)
            dve.tensor_tensor(wdt[:, 1], dec[:, 96:192].rearrange("p (c h) -> p c h", c=NT), dtk[:, 0, :, 16:32],
                              ALU.mult).then_inc(dc_w, 1)

        def pe_decay(pe):
            pe.wait_ge(tk_dtc, 1)
            pe.matmul(bank(0, 0, 96), c_(C_UF), dtk[:, 1, :, 0:16], start=True, stop=True)
            pe.matmul(bank(0, 96, 192), c_(C_UB), dtk[:, 1, :, 16:32], start=True, stop=True)
            pe.matmul(bank(0, 192, 384), ones, dtk[:, 1, :, :], start=True, stop=True).then_inc(dc_mm, 1)

        def act_decay(act):
            act.wait_ge(dc_mm, 1)
            act.activation(dec[:, 0:384], bank(0, 0, 384), ACT.Exp).then_inc(dc_exp, 1)

        STEPS = [(g, dr_, k) for g in range(2) for k in range(5) for dr_ in range(2)]

        def head_bc(v, n):
            return v.rearrange("p (h o) -> p h o", o=1).broadcast_to([P, v.shape[-1], n])

        def pool_states(pool, g):
            for q in range(10 * g, 10 * g + 10):
                _, dr_, k = STEPS[q]
                c = ORDER[dr_][k]
                if q == 0:
                    pool.wait_ge(dc_w, 1)
                    pool.wait_ge(tk_xc, NT)
                if q % 10 == 0 and g == 1:
                    pool.wait_ge(y_mm, 12)
                if q >= 2:
                    pool.wait_ge(s_mm, q - 1)
                pool.tensor_tensor(xw[:, q % 2, :].rearrange("p (h n) -> p h n", n=SP),
                                   xtok[:, c, 512 * g:512 * g + 512].rearrange("p (h n) -> p h n", n=SP),
                                   head_bc(wdt[:, dr_, c, 8 * g:8 * g + 8], SP), ALU.mult).then_inc(s_xw, 1)

        def pe_states(pe, g):
            for q in range(10 * g, 10 * g + 10):
                _, dr_, k = STEPS[q]
                c = ORDER[dr_][k]
                pe.wait_ge(s_xw, q + 1)
                if q == 0:
                    pe.wait_ge(tk_bc, 3)
                if q == 10:
                    pe.wait_ge(y_out, 12)
                if q >= 2:
                    pe.wait_ge(s_st, q - 1)
                pe.matmul(bank(6 + q % 2), btok[:, c, P * g:P * g + P], xw[:, q % 2, :],
                          start=True, stop=True).then_inc(s_mm, 1)

        def dve_states(dve, g):
            ndec = 8 * g
            for q in range(10 * g, 10 * g + 10):
                _, dr_, k = STEPS[q]
                c = ORDER[dr_][k]
                s = st[:, dr_, k, :]
                if k == 0:
                    dve.wait_ge(s_mm, q + 1)
                    dve.tensor_copy(s, bank(6 + q % 2)).then_inc(s_st, 1)
                    continue
                dve.wait_ge(s_st, q - 1)
                h0 = 16 * dr_ + 8 * g
                dve.tensor_tensor(s.rearrange("p (h n) -> p h n", n=SP),
                                  st[:, dr_, k - 1, :].rearrange("p (h n) -> p h n", n=SP),
                                  head_bc(dcb[:, c, h0:h0 + 8], SP), ALU.mult).then_inc(s_dec, 1)
                ndec += 1
                dve.wait_ge(s_dec, ndec)
                dve.wait_ge(s_mm, q + 1)
                dve.tensor_tensor(s, s, bank(6 + q % 2), ALU.add).then_inc(s_st, 1)

        def pe_gram(pe, g):
            for c in range(NT):
                q = NT * g + c
                if q % NT >= 2:
                    pe.wait_ge(g_done, 2 * (q - 1))
                elif g == 1:
                    pe.wait_ge(s_st, 20)
                else:
                    pe.wait_ge(s_st, 10)
                t0 = P * c
                pe.matmul(bank(6 + c % 2, 0, P), bc[:, g, t0:t0 + P], bc[:, 2 + g, t0:t0 + P],
                          start=True, stop=True).then_inc(g_mm, 1)

        def dve_gram(dve, g):
            for c in range(NT):
                dve.wait_ge(g_mm, NT * g + c + 1)
                for dr_, tri in ((0, C_TF), (1, C_TB)):
                    dve.tensor_tensor(gg[:, c, dr_, :], c_(tri), bank(6 + c % 2, 0, P), ALU.mult).then_inc(g_done, 1)

        YU = [(g, c, hf) for g in range(2) for c in range(NT) for hf in range(2)]

        def pool_y(pool, g):
            for v in range(12 * g, 12 * g + 12):
                _, c, hf = YU[v]
                q = v // 2
                if hf == 0:
                    if v % 12 == 0:
                        pool.wait_ge(s_mm, 10 * g + 10)
                    if q % NT >= 2:
                        pool.wait_ge(y_mm, 2 * (q - 1))
                    for dr_ in range(2):
                        pool.tensor_tensor(xdt[:, q % 2, dr_, :].rearrange("p (h n) -> p h n", n=SP),
                                           xtok[:, c, 512 * g:512 * g + 512].rearrange("p (h n) -> p h n", n=SP),
                                           head_bc(dtk[:, 0, c, 16 * dr_ + 8 * g:16 * dr_ + 8 * g + 8], SP),
                                           ALU.mult).then_inc(y_xdt, 1)
                if v >= 2:
                    pool.wait_ge(y_seg, v - 1)
                for dr_, tri in ((0, C_TF), (1, C_TB)):
                    h0 = 16 * dr_ + 8 * g + 4 * hf
                    pool.tensor_tensor(rr[:, v % 2, dr_, :].rearrange("p (h n) -> p h n", n=P),
                                       c_(tri).rearrange("p (o n) -> p o n", o=1).broadcast_to([P, 4, P]),
                                       head_bc(dtk[:, 1, c, h0:h0 + 4], P), ALU.mult).then_inc(y_r, 1)

        def pe_y(pe, g):
            for v in range(12 * g, 12 * g + 13):
                if v < 12 * g + 12:
                    pe.wait_ge(y_r, 2 * v + 2)
                    if v % 12 < 2:
                        pe.wait_ge(s_st, 10 * g + 10)
                        pe.wait_ge(g_done, 12 * g + 12)
                    if v >= 2:
                        pe.wait_ge(y_exp, v - 1)
                    b = 3 * (v % 2)
                    pe.matmul(bank(b), c_(C_UF), rr[:, v % 2, 0, :], start=True, stop=False)
                    pe.matmul(bank(b), c_(C_UB), rr[:, v % 2, 1, :], start=False, stop=True)
                    pe.matmul(bank(b + 1), ones, rr[:, v % 2, 0, :], start=True, stop=True)
                    pe.matmul(bank(b + 2), ones, rr[:, v % 2, 1, :], start=True, stop=True).then_inc(y_seg, 1)
                w = v - 1
                if w >= 12 * g:
                    _, c, hf = YU[w]
                    q = w // 2
                    pe.wait_ge(y_m, 4 * w + 4)
                    pe.wait_ge(y_xdt, 2 * q + 2)
                    if w % 12 >= 2:
                        pe.wait_ge(y_out, w - 1)
                    e = ee[:, w % 2, :]
                    for pp in range(2):
                        for eo in range(2):
                            i = 2 * pp + eo
                            at = bank(6 + w % 2)[64 * eo:64 * eo + 64, P * pp:P * pp + P]
                            x0 = SP * (4 * hf + i)
                            terms = [(xdt[:, q % 2, 0, x0:x0 + SP], mf[:, w % 2, P * i:P * i + P]),
                                     (xdt[:, q % 2, 1, x0:x0 + SP], e[:, P * i:P * i + P])]
                            for dr_ in range(2):
                                k = ORDER[dr_].index(c)
                                if k:
                                    terms.append((st[:, dr_, k - 1, x0:x0 + SP],
                                                  e[:, 512 * (1 + dr_) + P * i:512 * (1 + dr_) + P * i + P]))
                            for n, (lhs, rhs) in enumerate(terms):
                                mm = pe.matmul(at, lhs, rhs, start=n == 0, stop=n == len(terms) - 1)
                    mm.then_inc(y_mm, 1)

        def act_y(act, g):
            for v in range(12 * g, 12 * g + 12):
                act.wait_ge(y_seg, v + 1)
                if v >= 2:
                    act.wait_ge(y_mm, v - 1)
                act.activation(ee[:, v % 2, :], ps[:, 1536 * (v % 2):1536 * (v % 2) + 1536], ACT.Exp).then_inc(y_exp, 1)

        def dve_y(dve, g):
            for v in range(12 * g, 12 * g + 13):
                if v < 12 * g + 12:
                    _, c, hf = YU[v]
                    dve.wait_ge(y_exp, v + 1)
                    if v % 12 == 0:
                        dve.wait_ge(g_done, 12 * g + 12)
                    if v >= 2:
                        dve.wait_ge(y_mm, v - 1)
                    e = ee[:, v % 2, :].rearrange("p (k h n) -> p k h n", k=3, h=4)
                    over = lambda x: x.rearrange("p (o n) -> p o n", o=1).broadcast_to([P, 4, P])
                    dve.tensor_tensor(mf[:, v % 2, :].rearrange("p (h n) -> p h n", h=4), e[:, 0],
                                      over(gg[:, c, 0, :]), ALU.mult).then_inc(y_m, 1)
                    dve.tensor_tensor(e[:, 0], e[:, 0], over(gg[:, c, 1, :]), ALU.mult).then_inc(y_m, 1)
                    cc = over(bc[:, 2 + g, P * c:P * c + P])
                    dve.tensor_tensor(e[:, 1], e[:, 1], cc, ALU.mult).then_inc(y_m, 1)
                    dve.tensor_tensor(e[:, 2], e[:, 2], cc, ALU.mult).then_inc(y_m, 1)
                w = v - 1
                if w >= 12 * g:
                    _, c, hf = YU[w]
                    dve.wait_ge(y_mm, w + 1)
                    for pp in range(2):
                        b = 4 * g + 2 * hf + pp
                        y = xs[:, b, P * c:P * c + P]
                        x = dve.scalar_tensor_tensor(out=y, in0=y, scalar=dskip[:, b:b + 1],
                                                     in1=bank(6 + w % 2, P * pp, P * pp + P),
                                                     op0=ALU.mult, op1=ALU.add)
                    x.then_inc(y_out, 1)

        def pool_merge(pool):
            pool.wait_ge(y_out, 24)
            for b in range(8):
                pool.tensor_tensor(xs[:, b, :], xs[:, b, :], z[:, b, :], ALU.mult).then_inc(m_z, 1)

        def act_merge(act):
            act.wait_ge(y_mm, 24)
            for b in range(8):
                act.wait_ge(m_z, b + 1)
                if b >= 2:
                    act.wait_ge(m_ss, b - 1)
                act.activation(sqn[:, b % 2, :], xs[:, b, :], ACT.Square).then_inc(m_sq, 1)
            for g in range(2):
                act.wait_ge(m_ss, 4 * g + 4)
                if g == 1:
                    act.wait_ge(m_y, 4)
                act.activation(rsn, pair(2 + g), ACT.Ln, bias=eps, scale=1.0 / 512).then_inc(m_ln, 1)
                act.wait_ge(m_ln, g + 1)
                act.activation(rsn, rsn, ACT.Exp, scale=-0.5).then_inc(m_rs, 1)

        def pe_merge(pe):
            pe.wait_ge(y_out, 24)
            for b in range(8):
                pe.wait_ge(m_sq, b + 1)
                for c0, c1 in ((0, 512), (512, T)):
                    mm = pe.matmul(pair(2 + b // 4)[:, c0:c1], ones, sqn[:, b % 2, c0:c1], start=b % 4 == 0, stop=b % 4 == 3)
                mm.then_inc(m_ss, 1)
            pe.wait_ge(m_y, 8)

        def dve_merge(dve):
            for b in range(8):
                dve.wait_ge(m_rs, b // 4 + 1)
                dve.wait_ge(m_sq, b + 1)
                dve.scalar_tensor_tensor(out=xs[:, b, :], in0=xs[:, b, :], scalar=vb[:, VB_SSD + b:VB_SSD + b + 1],
                                         in1=rsn, op0=ALU.mult, op1=ALU.mult).then_inc(m_y, 1)

        block_ = ctx.enter_context(nc.Block())

        @block_.sync
        def _(sp):
            f = Filler(sp)
            sp.dma_start(cst[:, :], a["shape_constants"]).then_inc(const_in, 16)
            flat = lambda x: x.rearrange("l (n p) -> l n p", p=P)
            for dst, src in [
                (rows[VA_MOD:VA_MOD + 72, 0, :], flat(a["b_mod"])[0]),
                (rows[VA_C:VA_C + 8, 0, :], flat(a["c"])[0]),
                (rows[VA_CC:VA_CC + 8, 0, :], a["c_ctx"].rearrange("(n p) -> n p", p=P)),
                (rows[VB_MOD:VB_MOD + 72, 1, :], flat(a["b_mod"])[1]),
                (rows[VB_SSD:VB_SSD + 8, 1, :], flat(a["ssd_norm"])[0]),
                (rows[VB_QA:VB_QA + 3, 1, :], flat(a["mla_qa_norm"])[0]),
                (rows[VB_KV:VB_KV + 2, 1, :], flat(a["mla_kv_norm"])[0]),
                (rows[VB_QN:VB_QN + 1, 1, :], a["mla_qn_norm"]),
                (rows[VB_KN:VB_KN + 1, 1, :], a["mla_kn_norm"]),
                (rows[VB_QR:VB_QR + 1, 1, 0:64], a["mla_qr_norm"]),
                (rows[VB_QR:VB_QR + 1, 1, 64:128], a["mla_qr_norm"]),
                (rows[VB_KR:VB_KR + 1, 1, 0:64], a["mla_kr_norm"]),
                (rows[VB_KR:VB_KR + 1, 1, 64:128], a["mla_kr_norm"]),
                (rows[VB_GQ:VB_GQ + 1, 1, 0:64], a["gqa_q_norm"]),
                (rows[VB_GQ:VB_GQ + 1, 1, 64:128], a["gqa_q_norm"]),
                (rows[VB_GK:VB_GK + 1, 1, 0:64], a["gqa_k_norm"]),
                (rows[VB_GK:VB_GK + 1, 1, 64:128], a["gqa_k_norm"]),
                (rows[VB_CB:VB_CB + 12, 1, :], flat(a["conv_b"])[0]),
                (rows[0:60, 2, :], a["conv_w"][0].rearrange("t (n p) -> (t n) p", p=P)),
                (dtb, a["dt_bias"][0].rearrange("a (h o) -> (a h) o", o=1)),
                (alog, a["a_log"][0].rearrange("a (h o) -> (a h) o", o=1)),
                (dskip[0:64, :], a["d_skip"].rearrange("l (b e) -> l b e", e=2)[:, :, 0].broadcast_to([64, 8])),
                (dskip[64:128, :], a["d_skip"].rearrange("l (b e) -> l b e", e=2)[:, :, 1].broadcast_to([64, 8])),
                (sink[:, :], a["sink"].broadcast_to([P, QH])),
            ]:
                sp.dma_start(dst, src, allow_slow_non_contiguous=True).then_inc(rows_in, 16)
            for n in range(NT):
                src = a["x"][0, P * n:P * n + P, :] if n < 4 else a["ctx"][0, P * (n - 4):P * (n - 3), :]
                sp.dma_start(xin[:, n, :], src).then_inc(x_in, 16)
            for d in range(DB):
                for q in range(3):
                    f.put(block(w_mod[0], 0, 8, q * D + P * d))
            sync_ffi(f, 0)
            sync_out(f, 0)
            assert f.n == BASE["even"]
            sync_items(f, 0, n_even)
            sync_v(f, "e")
            sync_out(f, 1)
            sync_proj(f)
            sync_out(f, 2)
            sync_ffi(f, 1)
            sync_out(f, 3)
            sync_ffi(f, 2)
            sync_out(f, 4)
            sync_items(f, n_even, len(items))
            sync_v(f, "o")
            sync_out(f, 5)
            sync_ffi(f, 3)
            sync_out(f, 6)
            assert f.n == n_
            for n in range(SEQ // P):
                sp.wait_ge(out_c, 2 * n + 2)
                sp.dma_start(out[P * n:P * n + P, :], xin[:, n, :]).then_inc(out_st, 16)
            sp.wait_ge(out_st, 16 * (SEQ // P))

        @block_.tensor
        def _(pe):
            dr = Drainer(pe)
            pe.wait_ge(const_in, 16)
            pe.wait_ge(rows_in, 16 * 24)
            for n, rn in ((0, VA_N), (1, VB_N), (2, VC_N)):
                mm = pe.transpose(bank(7)[:, P * n:P * n + rn], rows[0:rn, n, :], ident[0:rn, 0:rn])
            mm.then_inc(vec_t, 1)
            pe.wait_ge(x_in, 16 * NT)
            for d in range(DB):
                if d >= 2:
                    pe.wait_ge(h_loaded, d - 1)
                for n in range(NT):
                    mm = pe.transpose(pair(d % 2)[:, P * n:P * n + P], xin[:, n, P * d:P * d + P], ident)
                mm.then_inc(xt_done, 1)
            pe.wait_ge(sc_done, 1)
            for d in range(DB):
                for q in range(3):
                    pe_mod_block(pe, dr.get(), 16 * q + 2 * d)
            pe.wait_ge(vec_done, 3)
            pe_norm(pe, 0)
            pe_ffi(pe, dr, 0)
            pe.wait_ge(f_hid, FB)
            pe_out(pe, dr, 0)
            pe_norm(pe, 1)
            pe_items(pe, dr, 0, n_even, 1)
            pe_v(pe, dr, "e")
            pe.wait_ge(v_done, 12)
            pe.wait_ge(hn_fin, ropes_to(n_even))
            pe.wait_ge(hn_n, norms_to(n_even))
            pe_attend(pe, 0, n_mla)
            pe.wait_ge(at_o, n_mla)
            pe_out(pe, dr, 1)
            pe_proj(pe, dr)
            pe_turn(pe)
            pe_decay(pe)
            for g in range(2):
                pe_states(pe, g)
                pe_gram(pe, g)
                pe_y(pe, g)
            pe_merge(pe)
            pe_out(pe, dr, 2)
            for i_f, r in ((1, 3), (2, 4)):
                pe_norm(pe, FF_NORM[i_f])
                pe_ffi(pe, dr, i_f)
                pe.wait_ge(f_hid, FB * (i_f + 1))
                pe_out(pe, dr, r)
            pe_norm(pe, 4)
            pe_items(pe, dr, n_even, len(items), 4)
            pe_v(pe, dr, "o")
            pe.wait_ge(v_done, 24)
            pe.wait_ge(hn_fin, ropes_to(len(items)))
            pe_attend(pe, n_mla, len(units))
            pe.wait_ge(at_o, len(units))
            pe_out(pe, dr, 5)
            pe_norm(pe, 5)
            pe_ffi(pe, dr, 3)
            pe.wait_ge(f_hid, 4 * FB)
            pe_out(pe, dr, 6)
            for n in range(SEQ // P):
                if n >= 2:
                    pe.wait_ge(out_c, 2 * (n - 1))
                for d in range(DB):
                    if n == 0:
                        pe.wait_ge(o_res, 8 * 6 + d + 1)
                    mm = pe.transpose(pair(2 + n % 2, 1024)[:, P * d:P * d + P], h[:, d, P * n:P * n + P], ident)
                mm.then_inc(out_t, 1)

        @block_.scalar
        def _(act):
            act.wait_ge(vec_done, 1)
            act.activation(sc[:, :].rearrange("p (k s) -> p s k", s=2),
                           va[:, VA_C:VA_C + 16].rearrange("p (s k) -> p s k", s=2), ACT.Silu).then_inc(sc_done, 1)
            act_norm(act, 0)
            act_ffi(act, 0)
            act_norm(act, 1)
            act_items(act, 0, n_even, BASE["even"])
            act_attend(act, 0, n_mla)
            act_proj(act)
            act_decay(act)
            act_y(act, 0)
            act_y(act, 1)
            act_merge(act)
            for i_f in (1, 2):
                act_norm(act, FF_NORM[i_f])
                act_ffi(act, i_f)
            act_norm(act, 4)
            act_items(act, n_even, len(items), BASE["odd"])
            act_attend(act, n_mla, len(units))
            act_norm(act, 5)
            act_ffi(act, 3)
            for n in range(SEQ // P):
                act.wait_ge(out_t, n + 1)
                act.wait_ge(w_used, n_)
                act.copy(xin[:, n, 0:512], pair(2 + n % 2, 1024)[:, 0:512]).then_inc(out_c, 1)
                act.copy(xin[:, n, 512:1024], pair(2 + n % 2, 1024)[:, 512:1024]).then_inc(out_c, 1)

        @block_.vector
        def _(dve):
            dve.memset(eps, EPS).then_inc(eps_set, 1)
            dve.wait_ge(vec_t, 1)
            for n, (v, rn) in enumerate(((va, VA_N), (vb, VB_N), (vc, VC_N))):
                dve.tensor_copy(v[:, :], bank(7)[:, P * n:P * n + rn]).then_inc(vec_done, 1)
            for d in range(DB):
                dve.wait_ge(xt_done, d + 1)
                dve.tensor_copy(h[:, d, :], pair(d % 2)).then_inc(h_loaded, 1)
            dve.wait_ge(vec_done, 3)
            dve_mod(dve, 0, 24)
            dve_norm(dve, 0)
            dve_ffi(dve, 0)
            dve_out(dve, 0)
            dve_norm(dve, 1)
            dve_items(dve, 0, n_even)
            dve_v(dve, "e")
            dve_attend(dve, 0, n_mla)
            dve_out(dve, 1)
            dve_proj(dve)
            dve_turn(dve)
            for g in range(2):
                dve_states(dve, g)
                dve_gram(dve, g)
                dve_y(dve, g)
            dve_merge(dve)
            dve_out(dve, 2)
            for i_f, r in ((1, 3), (2, 4)):
                dve_norm(dve, FF_NORM[i_f])
                dve_ffi(dve, i_f)
                dve_out(dve, r)
            dve_norm(dve, 4)
            dve_items(dve, n_even, len(items))
            dve_v(dve, "o")
            dve_attend(dve, n_mla, len(units))
            dve_out(dve, 5)
            dve_norm(dve, 5)
            dve_ffi(dve, 3)
            dve_out(dve, 6)

        @block_.gpsimd
        def _(pool):
            for g in range(2):
                pool_states(pool, g)
                pool_y(pool, g)
            pool_merge(pool)


INPUTS = ["x", "c", "ctx", "c_ctx", "w_mod", "b_mod", "w_ff1_in", "w_ff1_out", "w_ff2_in", "w_ff2_out",
          "w_in_e", "conv_w", "conv_b", "dt_bias", "a_log", "d_skip", "ssd_norm", "mla_qa_norm", "w_qb",
          "mla_kv_norm", "w_kvb", "mla_qn_norm", "mla_qr_norm", "mla_kn_norm", "mla_kr_norm", "w_out_e",
          "w_in_o", "gqa_q_norm", "gqa_k_norm", "sink", "w_out_o"]


def kernel(**inputs):
    import concourse.bacc as bacc
    from concourse.bass_utils import run_bass_kernel_spmd

    nc = bacc.Bacc("TRN2", target_bir_lowering=False, num_devices=1)
    arrays = {"shape_constants": shape_constants()}
    for name in INPUTS:
        arrays[name] = np.ascontiguousarray(inputs[name])
    sent, aps = {}, {}
    for name, v in arrays.items():
        sent[f"in_{name}"] = v
        aps[name] = nc.dram_tensor(f"in_{name}", v.shape, mybir.dt.from_np(v.dtype), kind="ExternalInput").ap()
    out = nc.dram_tensor("out_h", (SEQ, D), F32, kind="ExternalOutput").ap()
    build(nc, aps, out)
    r = run_bass_kernel_spmd(nc, [sent], core_ids=[0])
    return r.results[0]["out_h"].reshape(1, SEQ, D)
```

```python
from contextlib import ExitStack

import numpy as np

import concourse.bass as bass
from concourse import mybir

F32 = mybir.dt.float32
F32R = mybir.dt.float32r
ACT = mybir.ActivationFunctionType
ALU = mybir.AluOpType
AX = mybir.AxisListType.X

P = 128
D = 1024
DB = D // P
SEQ, CTX = 512, 256
T = SEQ + CTX
GRID_W = 64
FFN = 2816
FB = FFN // P
EPS = 1e-6
NT = T // P
SEGS = ((0, SEQ, 0), (SEQ, T, 1))

Z0, XBC0, DT0, QA0, CKV0, KR0 = 0, 1024, 2560, 2592, 2976, 3232
HEADS, SP = 16, 64
MH, DN, DR, DV = 8, 128, 64, 128
QH, KVH, HD = 16, 4, 64

HALF = (12, 10)
RING = 4
SLOT = 8 * P

C_ID, C_ONE, C_BLK, C_UF, C_UB, C_TF, C_TB, C_MP, C_MN, C_SW, C_COS, C_SIN = (
    0, 128, 256, 384, 512, 640, 768, 896, 1024, 1152, 1280, 1792)
C_ALL = 2304
NEG = -1.0e30

VA_MOD, VA_C, VA_CC, VA_N = 0, 72, 80, 88
VB_MOD, VB_SSD, VB_QA, VB_KV, VB_QN, VB_KN, VB_QR, VB_KR, VB_GQ, VB_GK, VB_CB, VB_N = (
    0, 72, 80, 83, 85, 86, 87, 88, 89, 90, 91, 103)
VC_N = 60


def shape_constants():
    c = np.zeros((P, C_ALL), np.float32)
    i = np.arange(P)
    c[:, C_ID:C_ID + P] = np.eye(P)
    c[:, C_ONE:C_ONE + P] = 1.0
    c[:, C_BLK:C_BLK + P] = (i[:, None] // 64) == (i[None, :] // 64)
    c[:, C_UF:C_UF + P] = i[:, None] > i[None, :]
    c[:, C_UB:C_UB + P] = i[:, None] < i[None, :]
    c[:, C_TF:C_TF + P] = i[:, None] <= i[None, :]
    c[:, C_TB:C_TB + P] = i[:, None] >= i[None, :]
    c[:, C_MP:C_MP + P] = np.where(i[None, :] >= i[:, None], 0.0, NEG)
    c[:, C_MN:C_MN + P] = np.where(i[None, :] <= i[:, None], 0.0, NEG)
    swap = np.zeros((P, P), np.float32)
    for o in range(P):
        j = o % 32
        if j < 16:
            swap[o + 16, o] = -1.0
        else:
            swap[o - 16, o] = 1.0
    c[:, C_SW:C_SW + P] = swap
    quarter = 16
    freqs = (np.float32(10000.0) ** (-np.arange(quarter, dtype=np.float32) / np.float32(quarter))).astype(np.float32)
    t = np.arange(SEQ)
    pos = np.stack([(t // GRID_W), (t % GRID_W)]).astype(np.float32)
    for p in range(P):
        ang = pos[(p % 64) // 32] * freqs[p % 16]
        c[p, C_COS:C_COS + SEQ] = np.cos(ang)
        c[p, C_SIN:C_SIN + SEQ] = np.sin(ang)
    return c


def head_norm_items():
    items = []
    for i in range(3):
        items.append(dict(kind="qa", i=i, start=i == 0, stop=i == 2, rope=False, t=T))
    for i in range(2):
        items.append(dict(kind="ckv", i=i, start=i == 0, stop=i == 1, rope=False, t=T))
    items.append(dict(kind="kr", i=0, start=True, stop=True, rope=True, t=T))
    for kind, n, rope in (("qn", MH, False), ("kn", MH, False), ("qr", MH // 2, True)):
        for i in range(n):
            items.append(dict(kind=kind, i=i, start=True, stop=True, rope=rope, t=T))
    n_even = len(items)
    for i in range(2):
        items.append(dict(kind="gk", i=i, start=True, stop=True, rope=True, t=T))
    for i in range(8):
        items.append(dict(kind="gq", i=i, start=True, stop=True, rope=True, t=SEQ))
    norms = ropes = 0
    for it in items:
        it["norm"] = norms
        it["nrope"] = ropes
        norms += it["stop"]
        ropes += it["rope"]
    return items, n_even


def build(nc, a, out):
    items, n_even = head_norm_items()
    norms_to = lambda m: sum(x["stop"] for x in items[:m])
    ropes_to = lambda m: sum(x["rope"] for x in items[:m])

    with ExitStack() as ctx:
        def sb(name, cols):
            return ctx.enter_context(nc.sbuf_tensor(name, [P, cols], F32))

        def sem(name):
            return ctx.enter_context(nc.semaphore(name))

        ps = ctx.enter_context(nc.psum_tensor("ps", [P, 4096], F32))

        def pair(p, n=T):
            return ps[:, 1024 * p:1024 * p + n]

        def bank(b, c0=0, c1=512):
            return ps[:, 512 * b + c0:512 * b + c1]

        h_sb = sb("h_sb", DB * T)
        arena = -(-nc.sbuf_base // 32) * 32

        def at(name, first, cols, dt=F32):
            return nc.alloc_sbuf_tensor_at(name, [P, cols], dt, offset=arena + 4 * first)

        u_sb = at("u_sb", 0, 8 * T)
        big = at("big", 8 * T, 22 * T)
        mix = at("mix", 30 * T, 21 * T)
        u_hi, u_lo = at("u_hi", 0, 8 * T, F32R), at("u_lo", 8 * T, 8 * T, F32R)
        hid_hi, hid_lo = at("hid_hi", 16 * T, HALF[0] * T, F32R), at("hid_lo", 28 * T, HALF[0] * T, F32R)
        hid_f = at("hid_f", 40 * T, 2 * T)
        w_hi, w_lo = (at(n, 51 * T - 4 * SLOT + 2 * SLOT * i, 2 * SLOT, F32R) for i, n in enumerate(("w_hi", "w_lo")))
        sb("stretch", (arena - nc.sbuf_base) // 4 + 51 * T)
        ring = sb("ring", RING * SLOT)
        cst = sb("cst", C_ALL)
        va, vb, vc = sb("va", VA_N), sb("vb", VB_N), sb("vc", VC_N)
        mod = sb("mod", 6 * 48)
        sc = sb("sc", 16)
        small = sb("small", 64)
        dskip = sb("dskip", 8)
        sink = sb("sink", QH)
        stat = sb("stat", 32)

        h = h_sb[:, :].rearrange("p (b t) -> p b t", t=T)
        u = u_sb[:, :].rearrange("p (b t) -> p b t", t=T)
        u_hi, u_lo, hid_hi, hid_lo, hid_f = (
            x[:, :].rearrange("p (b t) -> p b t", t=T) for x in (u_hi, u_lo, hid_hi, hid_lo, hid_f))

        def c_(at, n=P):
            return cst[:, at:at + n]

        ident, ones, blk64 = c_(C_ID), c_(C_ONE), c_(C_BLK)
        eps = small[:, 0:1]
        dtb, alog, aexp = small[0:32, 1:2], small[0:32, 2:3], small[0:32, 3:4]

        sqn = mix[:, 12 * T:14 * T].rearrange("p (b t) -> p b t", t=T)
        rsn = mix[:, 14 * T:15 * T]
        xin = u_sb[:, :].rearrange("p (n d) -> p n d", d=D)
        rows = mix[:, 4096:4096 + 3 * P].rearrange("p (n d) -> p n d", d=P)
        kn = big[:, 0:8 * T].rearrange("p (b t) -> p b t", t=T)
        vt = big[:, 8 * T:8 * T + NT * D].rearrange("p (n d) -> p n d", d=D)
        ckv = big[:, 16 * T:18 * T].rearrange("p (b t) -> p b t", t=T)
        qa = big[:, 18 * T:21 * T].rearrange("p (b t) -> p b t", t=T)
        qn = mix[:, 0:8 * T].rearrange("p (b t) -> p b t", t=T)
        qr = mix[:, 8 * T:12 * T].rearrange("p (b t) -> p b t", t=T)
        kr = mix[:, 12 * T:13 * T]
        sqh = mix[:, 13 * T:15 * T].rearrange("p (b t) -> p b t", t=T)
        rsh = mix[:, 15 * T:17 * T].rearrange("p (b t) -> p b t", t=T)
        prob = mix[:, 17 * T:20 * T].rearrange("p (b t) -> p b t", t=T)
        probT = mix[:, 13 * T:15 * T].rearrange("p (b t) -> p b t", t=T)
        gq = big[:, 0:8 * T].rearrange("p (b t) -> p b t", t=T)
        gk = big[:, 8 * T:10 * T].rearrange("p (b t) -> p b t", t=T)
        gv = big[:, 10 * T:10 * T + NT * 256].rearrange("p (n d) -> p n d", d=256)
        go = big[:, 12 * T:20 * T].rearrange("p (b t) -> p b t", t=T)
        xs = big[:, 0:8 * T].rearrange("p (b t) -> p b t", t=T)
        bc = big[:, 8 * T:12 * T].rearrange("p (b t) -> p b t", t=T)
        z = big[:, 12 * T:20 * T].rearrange("p (b t) -> p b t", t=T)
        btok = big[:, 20 * T:20 * T + NT * 256].rearrange("p (n d) -> p n d", d=256)
        xtok = u_sb[:, :].rearrange("p (n d) -> p n d", d=D)
        PADC = T + 6
        pad = mix[:, 0:2 * PADC].rearrange("p (b t) -> p b t", t=PADC)
        cv = mix[:, 2 * PADC:4 * PADC].rearrange("p (b t) -> p b t", t=PADC)
        dtw = mix[0:32, 4 * PADC:4 * PADC + 5 * T].rearrange("p (b t) -> p b t", t=T)
        o_ = 4 * PADC + 5 * T
        st = mix[:, 0:5120].rearrange("p (d k n) -> p d k n", d=2, k=5)
        xdt = mix[:, 5120:7168].rearrange("p (b d n) -> p b d n", b=2, d=2)
        xw = xdt[:, 0, :, :]
        rr = mix[:, 7168:9216].rearrange("p (b d n) -> p b d n", b=2, d=2)
        ee = mix[:, 9216:12288].rearrange("p (b n) -> p b n", b=2)
        mf = mix[:, 12288:13312].rearrange("p (b n) -> p b n", b=2)
        gg = mix[:, 13312:14848].rearrange("p (c d n) -> p c d n", c=NT, d=2)
        dtk = mix[:, 14848:15232].rearrange("p (k c h) -> p k c h", k=2, c=NT)
        dec = mix[:, 15232:15616]
        wdt = mix[:, 15616:15808].rearrange("p (d c h) -> p d c h", d=2, c=NT)
        dcb = dec[:, 192:384].rearrange("p (c h) -> p c h", c=NT)
        assert 15808 <= 16128 and o_ <= 14848

        const_in, x_in, rows_in = sem("const_in"), sem("x_in"), sem("rows_in")
        w_full = [sem(f"w_full{i}") for i in range(RING)]
        w_used = sem("w_used")
        eps_set = sem("eps_set")
        vec_t, vec_done, sc_done = sem("vec_t"), sem("vec_done"), sem("sc_done")
        xt_done, h_loaded = sem("xt_done"), sem("h_loaded")
        mod_raw, mod_done = sem("mod_raw"), sem("mod_done")
        n_sq, n_ss, n_ln, n_rs, n_t, n_u = (sem("n_" + s) for s in ("sq", "ss", "ln", "rs", "t", "u"))
        n_lo = sem("n_lo")
        w_split_hi, w_split_lo = sem("w_split_hi"), sem("w_split_lo")
        f_silu, f_prod, f_hi, f_lo = sem("f_silu"), sem("f_prod"), sem("f_hi"), sem("f_lo")
        o_res = sem("o_res")
        hn_sq, hn_raw, hn_ss, hn_ln, hn_rs, hn_n, hn_rp, hn_sin, hn_cos, hn_fin = (
            sem("hn_" + s) for s in ("sq", "raw", "ss", "ln", "rs", "n", "rp", "sin", "cos", "fin"))
        v_mm, v_done = sem("v_mm"), sem("v_done")
        at_sc, at_mk, at_m0, at_m1, at_nm, at_ex, at_sk, at_l, at_ri, at_pn, at_tr, at_pt, at_pv, at_o = (
            sem("at_" + s) for s in ("sc", "mk", "m0", "m1", "nm", "ex", "sk", "l", "ri", "pn", "tr", "pt", "pv", "o"))
        pj_ev = sem("pj_ev")
        cv_pad, cv_tap, cv_out, pad_zero = sem("cv_pad"), sem("cv_tap"), sem("cv_out"), sem("pad_zero")
        dt_abs, dt_exp, dt_ln, dt_dt, dt_da = (sem("dt_" + s) for s in ("abs", "exp", "ln", "dt", "da"))
        a_exp = sem("a_exp")
        tk_dt, tk_dtc, tk_x, tk_xc, tk_b, tk_bc = (sem("tk_" + s) for s in ("dt", "dtc", "x", "xc", "b", "bc"))
        dc_mm, dc_exp, dc_w = sem("dc_mm"), sem("dc_exp"), sem("dc_w")
        s_xw, s_mm, s_dec, s_st = sem("s_xw"), sem("s_mm"), sem("s_dec"), sem("s_st")
        g_mm, g_done = sem("g_mm"), sem("g_done")
        y_xdt, y_r, y_seg, y_exp, y_m, y_mm, y_out = (sem("y_" + s) for s in ("xdt", "r", "seg", "exp", "m", "mm", "out"))
        m_z, m_sq, m_ss, m_ln, m_rs, m_y = (sem("m_" + s) for s in ("z", "sq", "ss", "ln", "rs", "y"))
        out_t, out_c, out_st = sem("out_t"), sem("out_c"), sem("out_st")

        rk = lambda w: w.rearrange("(k p) n -> p k n", p=P)
        w_mod = [rk(a["w_mod"][l]) for l in range(2)]
        w_ffi = [rk(a[n][l]) for l in range(2) for n in ("w_ff1_in", "w_ff2_in")]
        w_ffo = [rk(a[n][l]) for l in range(2) for n in ("w_ff1_out", "w_ff2_out")]
        w_ine, w_oute = rk(a["w_in_e"][0]), rk(a["w_out_e"][0])
        w_qb, w_kvb = rk(a["w_qb"][0]), rk(a["w_kvb"][0])
        w_ino, w_outo = rk(a["w_in_o"][0]), rk(a["w_out_o"][0])

        def slot(s, k, m=P):
            return ring[:, s * SLOT:s * SLOT + k * m].rearrange("p (k m) -> p k m", m=m)

        class Filler:

            def __init__(self, sp):
                self.sp, self.n = sp, 0

            def put(self, parts, i=None, per=0, c=0):
                s = (self.n + c) % RING
                if i is None:
                    if self.n >= RING:
                        self.sp.wait_ge(w_used, self.n - RING + 1)
                else:
                    self.sp.wait_ge(w_used, i * per + (self.n + c - RING + 1))
                for dst, src in parts(s):
                    self.sp.dma_start(dst, src).then_inc(w_full[s], 16)
                if i is None:
                    self.n += 1

        class Drainer:

            def __init__(self, eng):
                self.eng, self.n, self.landed = eng, 0, [0] * RING

            def get(self, i=None, per=0, c=0, parts=1):
                s = (self.n + c) % RING
                if i is None:
                    self.landed[s] += parts
                    self.n += 1
                    self.eng.wait_ge(w_full[s], 16 * self.landed[s])
                else:
                    self.eng.wait_ge(w_full[s], i * (16 * per // RING) + 16 * (self.landed[s] + c // RING + 1))
                return s

            def passed(self, count):
                for _ in range(count):
                    self.landed[self.n % RING] += 1
                    self.n += 1

            def passed_items(self, m0, m1):
                for it in items[m0:m1]:
                    self.landed[self.n % RING] += 2 if it["kind"] in ("qr", "gq") else 1
                    self.n += 1

            def passed_v(self, parts):
                for _ in range(2):
                    self.landed[self.n % RING] += parts
                    self.n += 1

        def block(w, k0, k, c0, m=P):
            return lambda s: [(slot(s, k, m), w[:, k0:k0 + k, bass.ds(c0, m)])]

        OUT = [(w_oute, 8, 8, T, 1, None, qn), (w_oute, 0, 8, T, 1, 2, xs), (w_outo, 0, 8, SEQ, 4, 5, go)]
        FF_NORM = [0, 2, 3, 5]
        FF_T = [T, T, T, SEQ]
        FF_NEXT = [1, 3, 4, None]
        for i_f in range(4):
            for half in range(2):
                OUT.append((w_ffo[i_f], HALF[0] * half, HALF[half], FF_T[i_f], FF_NORM[i_f],
                            FF_NEXT[i_f] if half else None, (i_f, half)))
        R_MLA, R_SSD, R_GQA = 0, 1, 2
        R_FF = lambda i_f, half: 3 + 2 * i_f + half
        RUN = [R_FF(0, 0), R_FF(0, 1), R_MLA, R_SSD, R_FF(1, 0), R_FF(1, 1), R_FF(2, 0), R_FF(2, 1), R_GQA,
               R_FF(3, 0), R_FF(3, 1)]
        RES = {r: 8 * i for i, r in enumerate(RUN)}

        def out_plan(r):
            w, k0, nk, t, g, gn, act = OUT[r]
            most = 8 if nk == 8 else nk // 2
            chunks = [("w", k, most) for k in range(0, nk, most)]
            if gn is not None:
                first, chunks = chunks[:-1], chunks[-1:]
                mods = [("m", q, 8) for q in range(3)]
                while mods:
                    chunks.insert(-1, mods.pop(0))
                    if first:
                        chunks.insert(-1, first.pop(0))
            per_d = len(chunks)
            dpb = 2 if per_d % 2 == 0 else 4
            assert per_d * dpb % RING == 0 and chunks[-1][0] == "w"
            return chunks, per_d, dpb

        def sync_out(f, r):
            w, k0, nk, t, g, gn, act = OUT[r]
            chunks, per_d, dpb = out_plan(r)
            per = per_d * dpb
            with f.sp.Fori(1, DB // dpb + 1) as i:
                for dd in range(-dpb, 0):
                    for c, (what, k, n) in enumerate(chunks):
                        if what == "w":
                            f.put(block(w, k0 + k, n, i * (dpb * P) + dd * P), i, per, dd * per_d + c)
                        else:
                            col = (gn % 3 * 3 + k) * D + dd * P
                            f.put(block(w_mod[gn // 3], 0, 8, i * (dpb * P) + col), i, per, dd * per_d + c)
            f.n += per * (DB // dpb)


        BASE, SPLIT = {}, {}
        n_ = m_ = 0

        def ff_names(i_f):
            return [("ffi", i_f, 0), ("out", R_FF(i_f, 0)), ("ffi", i_f, 1), ("out", R_FF(i_f, 1))]

        for name, count in [("mod", 24)] + [(x, 0) for x in ff_names(0)] + [
                ("even", n_even), ("v_e", 2), (("out", R_MLA), 0), ("proj", 21), (("out", R_SSD), 0)] + [
                (x, 0) for x in ff_names(1) + ff_names(2)] + [
                ("odd", len(items) - n_even), ("v_o", 2), (("out", R_GQA), 0)] + [(x, 0) for x in ff_names(3)]:
            BASE[name], SPLIT[name] = n_, m_
            if name[0] == "ffi":
                count = 2 * HALF[name[2]]
                m_ += count
            if name[0] == "out":
                chunks, per_d, dpb = out_plan(name[1])
                count = per_d * DB
                m_ += 0 if name[1] < 3 else 2 * DB
            n_ += count
        FH = {(i_f, half): FB * i_f + HALF[0] * half for i_f in range(4) for half in range(2)}

        def act_split(act, s, m, cols, i=None, per=0):
            act.copy(w_hi[:, (m % 2) * SLOT:(m % 2) * SLOT + cols], ring[:, s * SLOT:s * SLOT + cols]).then_inc(w_split_hi, 1)

        def dve_split(dve, s, m, cols, i=None, per=0):
            if i is None:
                dve.wait_ge(w_split_hi, m + 1)
            else:
                dve.wait_ge(w_split_hi, i * per + (m + 1))
            b = (m % 2) * SLOT
            dve.tensor_tensor(w_lo[:, b:b + cols], ring[:, s * SLOT:s * SLOT + cols], w_hi[:, b:b + cols],
                              ALU.subtract).then_inc(w_split_lo, 1)

        def three_products(pe, p, m, k, hi, lo, t, start, stop):
            wh, wl = (w[:, (m % 2) * SLOT + P * k:(m % 2) * SLOT + P * k + P] for w in (w_hi, w_lo))
            cs = [(c0, min(t, c0 + 512)) for c0 in range(0, t, 512)]
            for n, (w, x) in enumerate(((wh, hi), (wh, lo), (wl, hi))):
                for c0, c1 in cs:
                    mm = pe.matmul(pair(p)[:, c0:c1], w, x[:, c0:c1], start=start and n == 0, stop=stop and n == 2)
            return mm

        def mod_group(g):
            return mod[:, 48 * g:48 * g + 48].rearrange("p (q d s) -> p q d s", q=3, d=8)

        def bmod(g):
            v = va if g < 3 else vb
            return v[:, g % 3 * 24:g % 3 * 24 + 24].rearrange("p (q d) -> p q d", q=3)

        NORM_T = [T, T, T, T, T, SEQ]
        NORM_AFTER = [None, R_FF(0, 1), R_SSD, R_FF(1, 1), R_FF(2, 1), R_GQA]

        def h_ready(eng, n, d):
            if n == 0:
                eng.wait_ge(h_loaded, d + 1)
            else:
                eng.wait_ge(o_res, RES[NORM_AFTER[n]] + d + 1)

        def act_norm(act, n):
            t = NORM_T[n]
            for d in range(DB):
                h_ready(act, n, d)
                if n or d >= 2:
                    if 8 * n + d - 1 > 0:
                        act.wait_ge(n_ss, 8 * n + d - 1)
                act.activation(sqn[:, d % 2, :t], h[:, d, :t], ACT.Square).then_inc(n_sq, 1)
            act.wait_ge(n_ss, 8 * n + 8)
            if n == 0:
                act.wait_ge(eps_set, 1)
            act.activation(rsn[:, :t], pair(3, t), ACT.Ln, bias=eps, scale=1.0 / D).then_inc(n_ln, 1)
            act.wait_ge(n_ln, n + 1)
            act.activation(rsn[:, :t], rsn[:, :t], ACT.Exp, scale=-0.5).then_inc(n_rs, 1)
            for d in range(DB):
                act.wait_ge(n_t, 8 * n + d + 1)
                src, dst = (hid_f[:, d % 2], u_hi[:, d]) if n in FF_NORM else (u[:, d], u[:, d])
                for t0, t1, s in SEGS:
                    if t0 < t:
                        x = act.activation(dst[:, t0:t1], src[:, t0:t1], ACT.Identity,
                                           bias=mod_group(n)[:, 0, d, s:s + 1])
                x.then_inc(n_u, 1)

        def pe_norm(pe, n):
            t = NORM_T[n]
            if n == 0:
                pe.wait_ge(const_in, 16)
            for d in range(DB):
                pe.wait_ge(n_sq, 8 * n + d + 1)
                for c0 in range(0, t, 512):
                    c1 = min(t, c0 + 512)
                    mm = pe.matmul(pair(3)[:, c0:c1], ones, sqn[:, d % 2, c0:c1], start=d == 0, stop=d == DB - 1)
                mm.then_inc(n_ss, 1)

        def dve_norm(dve, n):
            t = NORM_T[n]
            dve.wait_ge(n_rs, n + 1)
            dve.wait_ge(mod_done, n + 1)
            for q in range(DB + 1):
                if q < DB:
                    h_ready(dve, n, q)
                    dst = hid_f[:, q % 2] if n in FF_NORM else u[:, q]
                    if n in FF_NORM and q >= 2:
                        dve.wait_ge(n_lo, 8 * FF_NORM.index(n) + q - 1)
                    for t0, t1, s in SEGS:
                        if t0 < t:
                            x = dve.scalar_tensor_tensor(out=dst[:, t0:t1], in0=h[:, q, t0:t1],
                                                         scalar=mod_group(n)[:, 1, q, s:s + 1],
                                                         in1=rsn[:, t0:t1], op0=ALU.mult, op1=ALU.mult)
                    x.then_inc(n_t, 1)
                d = q - 1
                if d >= 0 and n in FF_NORM:
                    dve.wait_ge(n_u, 8 * n + d + 1)
                    for t0, t1, s in SEGS:
                        if t0 < t:
                            x = dve.scalar_tensor_tensor(out=u_lo[:, d, t0:t1], in0=hid_f[:, d % 2, t0:t1],
                                                         scalar=mod_group(n)[:, 0, d, s:s + 1],
                                                         in1=u_hi[:, d, t0:t1], op0=ALU.add, op1=ALU.subtract)
                    x.then_inc(n_lo, 1)

        def pe_mod_block(pe, s, col):
            at = ps[:, 2048 + col:2050 + col] if isinstance(col, int) else ps[:, bass.ds(col + 2048, 2)]
            for k in range(8):
                mm = pe.matmul(at, slot(s, 8)[:, k, :], sc[:, 2 * k:2 * k + 2], start=k == 0, stop=k == 7)
            mm.then_inc(w_used, 1)

        def dve_mod(dve, g, end):
            dve.wait_ge(w_used, end)
            raw = bank(4, 0, 48).rearrange("p (q d s) -> p q d s", q=3, d=8)
            m = mod_group(g)
            for q in range(3):
                for s in range(2):
                    x = dve.scalar_tensor_tensor(out=m[:, q, :, s], in0=raw[:, q, :, s],
                                                 scalar=1.0 if q == 1 else 0.0, in1=bmod(g)[:, q, :],
                                                 op0=ALU.add, op1=ALU.add)
            x.then_inc(mod_raw, 1)
            dve.wait_ge(mod_raw, g + 1)
            dve.tensor_scalar(m[:, 2, :, :], m[:, 2, :, :], 1.0 if g % 3 == 1 else 0.5, None,
                              ALU.mult).then_inc(mod_done, 1)

        def sync_ffi(f, i_f, half):
            with f.sp.Fori(0, HALF[half] // 2) as i:
                for jj in range(2):
                    for up in range(2):
                        col = up * FFN + (HALF[0] * half + jj) * P
                        f.put(block(w_ffi[i_f], 0, 8, i * (2 * P) + col), i, 4, 2 * jj + up)
            f.n += 2 * HALF[half]

        def pe_ffi(pe, dr, i_f, half):
            t, b, m = FF_T[i_f], FH[i_f, half], SPLIT["ffi", i_f, half]
            if half:
                pe.wait_ge(o_res, RES[R_FF(i_f, 0)] + DB)

            def body(i):
                for jj in range(2):
                    for up, sem_ in ((0, f_silu), (1, f_prod)):
                        v = b + jj - 1
                        if not isinstance(i, int):
                            pe.wait_ge(sem_, i * 2 + v)
                        elif v > 0:
                            pe.wait_ge(sem_, v)
                        mm_ = m + 2 * jj + up
                        pe.wait_ge(w_split_lo, i * 4 + (mm_ + 1))
                        for k in range(DB):
                            if isinstance(i, int) and jj == 0 and up == 0 and half == 0:
                                pe.wait_ge(n_lo, 8 * i_f + k + 1)
                            mm = three_products(pe, 2 * up + jj, mm_, k, u_hi[:, k], u_lo[:, k], t, k == 0, k == DB - 1)
                        mm.then_inc(w_used, 1)

            body(0)
            with pe.Fori(1, HALF[half] // 2) as i:
                body(i)
            dr.passed(2 * HALF[half])

        def act_ffi(act, ar, i_f, half):
            t, n, m, b = FF_T[i_f], BASE["ffi", i_f, half], SPLIT["ffi", i_f, half], FH[i_f, half]

            def body(i):
                for jj in range(2):
                    for up in range(2):
                        c = 2 * jj + up
                        s = ar.get(i, 4, c)
                        act.wait_ge(w_used, i * 4 + (n + c - 1))
                        act_split(act, s, m + c, SLOT)
                    if not isinstance(i, int) or jj:
                        round_hidden(act, i * 2 + (jj - 1), 1 - jj, i * 2 + (b + jj), t)
                    act.wait_ge(w_used, i * 4 + (n + 2 * jj + 1))
                    v = b + jj - 1
                    if not isinstance(i, int):
                        act.wait_ge(f_lo, i * 2 + v)
                    elif v > 0:
                        act.wait_ge(f_lo, v)
                    act.activation(hid_f[:, jj, :t], pair(jj, t), ACT.Silu).then_inc(f_silu, 1)

            body(0)
            with act.Fori(1, HALF[half] // 2) as i:
                body(i)
            ar.passed(2 * HALF[half])

        def round_hidden(act, j, q, done, t):
            act.wait_ge(f_prod, done)
            dst = hid_hi[:, j:j + 1, :t] if isinstance(j, int) else hid_hi[:, bass.ds(j, 1), :t]
            act.copy(dst, hid_f[:, q:q + 1, :t]).then_inc(f_hi, 1)

        def dve_ffi(dve, dv, i_f, half):
            t, n, m, b = FF_T[i_f], BASE["ffi", i_f, half], SPLIT["ffi", i_f, half], FH[i_f, half]

            def body(i):
                for jj in range(2):
                    s = (dv.n + 2 * jj) % RING
                    dve_split(dve, s, m + 2 * jj, SLOT, i, 4)
                    if not isinstance(i, int) or jj:
                        dve.wait_ge(w_used, i * 4 + (n + 2 * jj))
                        dve.wait_ge(f_silu, i * 2 + (b + jj))
                        q = 1 - jj
                        dve.tensor_tensor(hid_f[:, q, :t], hid_f[:, q, :t], pair(2 + q, t), ALU.mult).then_inc(f_prod, 1)
                    s = (dv.n + 2 * jj + 1) % RING
                    dve_split(dve, s, m + 2 * jj + 1, SLOT, i, 4)
                    if not isinstance(i, int) or jj:
                        dve.wait_ge(f_hi, i * 2 + (b + jj))
                        j = i * 2 + (jj - 1)
                        d = (lambda x: x[:, j:j + 1, :t] if isinstance(j, int) else x[:, bass.ds(j, 1), :t])
                        dve.tensor_tensor(d(hid_lo), hid_f[:, q:q + 1, :t], d(hid_hi), ALU.subtract).then_inc(f_lo, 1)

            body(0)
            with dve.Fori(1, HALF[half] // 2) as i:
                body(i)
            dv.n += 2 * HALF[half]

        def split_places(r):
            w, k0, nk, t, g, gn, src = OUT[r]
            chunks, per_d, dpb = out_plan(r)
            n, m = BASE["out", r], SPLIT["out", r]
            at_ = [n + d * per_d + c for d in range(DB) for c, x in enumerate(chunks) if x[0] == "w"]
            before = [n - 2, n - 1] + at_
            return [(a_, m + q, before[q]) for q, a_ in enumerate(at_)]

        def act_out_ff(act, ar, r):
            w, k0, nk, t, g, gn, (i_f, half) = OUT[r]
            n0 = ar.n
            for q, (n, m, old) in enumerate(split_places(r)):
                ar.passed(n - ar.n)
                s = ar.get()
                act.wait_ge(w_used, old + 1)
                act_split(act, s, m, P * nk // 2)
                if q == 1:
                    round_hidden(act, nk - 1, (nk - 1) % 2, FH[i_f, half] + nk, t)
            assert ar.n - n0 == out_plan(r)[1] * DB

        def dve_out_ff(dve, dv, r):
            w, k0, nk, t, g, gn, (i_f, half) = OUT[r]
            chunks, per_d, dpb = out_plan(r)
            places, b, q = split_places(r), BASE["out", r], (nk - 1) % 2
            for x in range(2 * DB + 2):
                if x < 2 * DB:
                    n, m, old = places[x]
                    dve_split(dve, n % RING, m, P * nk // 2)
                if x == 0:
                    dve.wait_ge(w_used, b)
                    dve.wait_ge(f_silu, FH[i_f, half] + nk)
                    dve.tensor_tensor(hid_f[:, q, :t], hid_f[:, q, :t], pair(2 + q, t), ALU.mult).then_inc(f_prod, 1)
                if x == 1:
                    dve.wait_ge(f_hi, FH[i_f, half] + nk)
                    dve.tensor_tensor(hid_lo[:, nk - 1, :t], hid_f[:, q, :t], hid_hi[:, nk - 1, :t],
                                      ALU.subtract).then_inc(f_lo, 1)
                if x >= 3 and x % 2 == 1:
                    dve_residual(dve, r, (x - 3) // 2)
            dv.n += per_d * DB
            if gn is not None:
                dve_mod(dve, gn, b + DB * per_d)

        def pe_out(pe, dr, r):
            w, k0, nk, t, g, gn, src = OUT[r]
            chunks, per_d, dpb = out_plan(r)
            per = per_d * dpb
            ff = r >= 3
            if ff:
                pe.wait_ge(f_lo, FH[src] + nk - 1)

            def body(i):
                for dd in range(dpb):
                    v = i * dpb + (RES[r] + dd - 1)
                    if not isinstance(v, int) or v > 0:
                        pe.wait_ge(o_res, v)
                    part = 0
                    for c, (what, k, n) in enumerate(chunks):
                        if what == "m":
                            s = dr.get(i, per, dd * per_d + c)
                            pe_mod_block(pe, s, i * (2 * dpb) + (16 * k + 2 * dd))
                            continue
                        if ff:
                            m = SPLIT["out", r] + 2 * dd + part
                            part += 1
                            pe.wait_ge(w_split_lo, i * (2 * dpb) + (m + 1))
                        else:
                            s = dr.get(i, per, dd * per_d + c)
                        for kk in range(n):
                            first, last = k + kk == 0, k + kk == nk - 1
                            if ff:
                                if isinstance(i, int) and dd == 0 and (first or last):
                                    pe.wait_ge(f_lo, FH[src] + nk - first)
                                mm = three_products(pe, dd % 2, m, kk, hid_hi[:, k + kk], hid_lo[:, k + kk], t, first, last)
                                continue
                            for c0 in range(0, t, 512):
                                c1 = min(t, c0 + 512)
                                mm = pe.matmul(pair(dd % 2)[:, c0:c1], slot(s, n)[:, kk, :],
                                               src[:, k + kk, c0:c1], start=first, stop=last)
                        mm.then_inc(w_used, 1)

            body(0)
            with pe.Fori(1, DB // dpb) as i:
                body(i)
            dr.passed(per_d * DB)

        def dve_residual(dve, r, d):
            w, k0, nk, t, g, gn, src = OUT[r]
            dve.wait_ge(w_used, BASE["out", r] + (d + 1) * out_plan(r)[1])
            for t0, t1, s in SEGS:
                if t0 < t:
                    x = dve.scalar_tensor_tensor(out=h[:, d, t0:t1], in0=pair(d % 2)[:, t0:t1],
                                                 scalar=mod_group(g)[:, 2, d, s:s + 1],
                                                 in1=h[:, d, t0:t1], op0=ALU.mult, op1=ALU.add)
            x.then_inc(o_res, 1)

        def dve_out(dve, dv, r):
            gn, per_d = OUT[r][5], out_plan(r)[1]
            for d in range(DB):
                dve_residual(dve, r, d)
            if gn is not None:
                dve_mod(dve, gn, BASE["out", r] + DB * per_d)
            dv.n += per_d * DB

        GAIN = {"qn": VB_QN, "kn": VB_KN, "qr": VB_QR, "kr": VB_KR, "gq": VB_GQ, "gk": VB_GK}
        WIDTH = {"qa": 384, "ckv": 256, "kr": 64, "qn": 128, "kn": 128, "qr": 64, "gk": 64, "gq": 64}
        DST = {"qa": qa, "ckv": ckv, "qn": qn, "kn": kn, "qr": qr, "gk": gk, "gq": gq}

        def dst_of(it):
            return kr if it["kind"] == "kr" else DST[it["kind"]][:, it["i"], :]

        def gain_of(it):
            k = {"qa": VB_QA + it["i"], "ckv": VB_KV + it["i"]}.get(it["kind"], GAIN.get(it["kind"]))
            return vb[:, k:k + 1]

        def item_chunk(it):
            kind, i = it["kind"], it["i"]
            if kind == "qa":
                return block(w_ine, 0, 8, QA0 + P * i)
            if kind == "ckv":
                return block(w_ine, 0, 8, CKV0 + P * i)
            if kind == "kr":
                return None
            if kind == "qn":
                return block(w_qb, 0, 3, i * (DN + DR))
            if kind == "kn":
                return block(w_kvb, 0, 2, i * (DN + DV))
            if kind == "gk":
                return block(w_ino, 0, 8, QH * HD + P * i)
            if kind == "qr":
                c0 = 2 * i * (DN + DR) + DN
                return lambda s: [(slot(s, 3)[:, :, 64 * e:64 * e + 64],
                                   w_qb[:, :, c0 + e * (DN + DR):c0 + e * (DN + DR) + 64]) for e in range(2)]
            c0 = HD * (8 * (i // 4) + i % 4)
            return lambda s: [(slot(s, 8)[:, :, 64 * e:64 * e + 64],
                               w_ino[:, :, c0 + 4 * HD * e:c0 + 4 * HD * e + 64]) for e in range(2)]

        def item_in(it):
            return {"qn": (3, qa), "qr": (3, qa), "kn": (2, ckv)}.get(it["kind"], (8, u))

        def sync_items(f, m0, m1):
            for m in range(m0, m1):
                it = items[m]
                if it["kind"] == "kr":
                    src = w_ine[:, :, KR0:KR0 + DR]
                    s = f.n % RING
                    f.sp.wait_ge(w_used, f.n - RING + 1)
                    f.sp.dma_start(slot(s, 8)[:, :, 0:64], src).then_inc(w_full[s], 16)
                    f.n += 1
                else:
                    f.put(item_chunk(it))

        def pe_items(pe, dr, m0, m1, norm_n):
            for q in range(m0, m1 + 2):
                if q < m1:
                    it = items[q]
                    nk, src = item_in(it)
                    if q - m0 >= 2:
                        pe.wait_ge(hn_raw, q - 1)
                    if q == m0:
                        pe.wait_ge(n_u, 8 * norm_n + 8)
                    if it["kind"] in ("qn", "qr", "kn"):
                        pe.wait_ge(hn_n, 2 if it["kind"] == "kn" else 1)
                    s = dr.get(parts=2 if it["kind"] in ("qr", "gq") else 1)
                    for k in range(nk):
                        for c0 in range(0, it["t"], 512):
                            c1 = min(it["t"], c0 + 512)
                            if it["kind"] == "kr":
                                for e in range(2):
                                    mm = pe.matmul(pair(q % 2)[64 * e:64 * e + 64, c0:c1], slot(s, 8)[:, k, 0:64],
                                                   src[:, k, c0:c1], start=k == 0, stop=k == nk - 1)
                            else:
                                mm = pe.matmul(pair(q % 2)[:, c0:c1], slot(s, nk)[:, k, :], src[:, k, c0:c1],
                                               start=k == 0, stop=k == nk - 1)
                    mm.then_inc(w_used, 1)
                m = q - 1
                if m0 <= m < m1:
                    it = items[m]
                    pe.wait_ge(hn_sq, m + 1)
                    if it["start"] and it["norm"] > 0:
                        pe.wait_ge(hn_ln, it["norm"])
                    w = blk64 if WIDTH[it["kind"]] == 64 else ones
                    for c0 in range(0, it["t"], 512):
                        c1 = min(it["t"], c0 + 512)
                        mm = pe.matmul(pair(2)[:, c0:c1], w, sqh[:, m % 2, c0:c1], start=it["start"], stop=it["stop"])
                    mm.then_inc(hn_ss, 1)
                m = q - 2
                if m0 <= m < m1 and items[m]["rope"]:
                    it = items[m]
                    pe.wait_ge(hn_n, it["norm"] + 1)
                    if it["nrope"] > 0:
                        pe.wait_ge(hn_sin, it["nrope"])
                    pe.matmul(bank(6), c_(C_SW), dst_of(it)[:, 0:SEQ], start=True, stop=True).then_inc(hn_rp, 1)

        def act_items(act, m0, m1, base):
            for q in range(m0, m1 + 1):
                if q < m1:
                    it = items[q]
                    t = it["t"]
                    act.wait_ge(w_used, base + q - m0 + 1)
                    if q >= 2:
                        act.wait_ge(hn_ss, q - 1)
                    act.activation(sqh[:, q % 2, :t], pair(q % 2, t), ACT.Square).then_inc(hn_sq, 1)
                    act.activation(dst_of(it)[:, :t], pair(q % 2, t), ACT.Identity,
                                   scale=gain_of(it)).then_inc(hn_raw, 1)
                m = q - 1
                if m0 <= m and items[m]["stop"]:
                    it = items[m]
                    t, nn = it["t"], it["norm"]
                    act.wait_ge(hn_ss, m + 1)
                    if nn >= 2:
                        act.wait_ge(hn_n, nn - 1)
                        last = [x for x in items if x["stop"]][nn - 2]
                        if last["rope"]:
                            act.wait_ge(hn_fin, last["nrope"] + 1)
                    act.activation(rsh[:, nn % 2, :t], pair(2, t), ACT.Ln, bias=eps,
                                   scale=1.0 / WIDTH[it["kind"]]).then_inc(hn_ln, 1)
                    act.wait_ge(hn_ln, nn + 1)
                    act.activation(rsh[:, nn % 2, :t], rsh[:, nn % 2, :t], ACT.Exp, scale=-0.5).then_inc(hn_rs, 1)

        def dve_items(dve, m0, m1):
            for m in range(m0, m1):
                it = items[m]
                if not it["stop"]:
                    continue
                t, nn, kind = it["t"], it["norm"], it["kind"]
                dve.wait_ge(hn_rs, nn + 1)
                dve.wait_ge(hn_raw, m + 1)
                for i in range(it["i"] + 1 if kind in ("qa", "ckv") else 1):
                    d = DST[kind][:, i, :t] if kind in ("qa", "ckv") else dst_of(it)[:, :t]
                    x = dve.tensor_tensor(d, d, rsh[:, nn % 2, :t], ALU.mult)
                x.then_inc(hn_n, 1)
                if it["rope"]:
                    d, nr = dst_of(it)[:, 0:SEQ], it["nrope"]
                    tmp = rsh[:, nn % 2, 0:SEQ]
                    dve.wait_ge(hn_rp, nr + 1)
                    dve.tensor_tensor(tmp, cst[:, C_SIN:C_SIN + SEQ], bank(6), ALU.mult).then_inc(hn_sin, 1)
                    dve.tensor_tensor(d, d, cst[:, C_COS:C_COS + SEQ], ALU.mult).then_inc(hn_cos, 1)
                    dve.wait_ge(hn_sin, nr + 1)
                    dve.wait_ge(hn_cos, nr + 1)
                    dve.tensor_tensor(d, d, tmp, ALU.add).then_inc(hn_fin, 1)

        def sync_v(f, which):
            for half in range(2):
                if which == "e":
                    src = w_kvb.rearrange("p k (h n) -> p k h n", n=DN + DV)[:, :, 4 * half:4 * half + 4, DN:DN + DV]
                    f.put(lambda s, src=src: [(slot(s, 2, 512)[:, k, :].rearrange("p (h n) -> p h n", n=DV),
                                               src[:, k]) for k in range(2)])
                else:
                    f.put(block(w_ino, 0, 8, (QH + KVH) * HD + P * half))

        def pe_v(pe, dr, which):
            nk, m, src = (2, 512, ckv) if which == "e" else (8, P, u)
            off = 0 if which == "e" else 12
            for half in range(2):
                s = dr.get(parts=2 if which == "e" else 1)
                for n in range(NT):
                    q = half * NT + n
                    if q >= 4:
                        pe.wait_ge(v_done, off + q - 3)
                    elif q == 0:
                        pe.wait_ge(hn_raw, n_even if which == "e" else len(items))
                    for k in range(nk):
                        mm = pe.matmul(bank(q % 4, 0, m), src[:, k, P * n:P * n + P], slot(s, nk, m)[:, k, :],
                                       start=k == 0, stop=k == nk - 1)
                    mm.then_inc(w_used if n == NT - 1 else v_mm, 1)

        def dve_v(dve, which):
            m, dst, base = (512, vt, BASE["v_e"]) if which == "e" else (P, gv, BASE["v_o"])
            off = 0 if which == "e" else 10
            for half in range(2):
                for n in range(NT):
                    if n < NT - 1:
                        dve.wait_ge(v_mm, off + 5 * half + n + 1)
                    else:
                        dve.wait_ge(w_used, base + half + 1)
                    dve.tensor_copy(dst[:, n, m * half:m * half + m], bank((half * NT + n) % 4, 0, m)).then_inc(v_done, 1)

        units = []
        for hh in range(MH):
            e = 64 * (hh % 2)
            for qt in range(NT):
                q0 = P * qt
                keys = [(0, SEQ), (SEQ, T)] if qt < 4 else [(SEQ, T)]
                sco = []
                at = 0
                for k0, k1 in keys:
                    sco.append((qn[:, hh, q0:q0 + P], kn[:, hh, k0:k1], at, True, False))
                    sco.append((qr[e:e + 64, hh // 2, q0:q0 + P], kr[e:e + 64, k0:k1], at, False, True))
                    at += k1 - k0
                tiles = range(NT) if qt < 4 else range(4, NT)
                units.append(dict(sc=sco, n=at, masks=[], scale=(DN + DR) ** -0.5, sink=None, m=DV, o=0,
                                  v=[vt[:, k, DV * hh:DV * hh + DV] for k in tiles], out=qn[:, hh, q0:q0 + P]))
        n_mla = len(units)
        for hh in range(QH):
            b, e8, ii = hh // 8, (hh % 8) // 4, hh % 4
            e, g = 64 * e8, hh // 4
            for qt in range(SEQ // P):
                q0 = P * qt
                q = gq[e:e + 64, 4 * b + ii, q0:q0 + P]
                sco = [(q, gk[e:e + 64, b, SEQ:T], 0, True, True)]
                tiles = [4, 5]
                masks = []
                lo, hi = max(0, qt - 1), min(3, qt + 1)
                if qt > 0:
                    masks.append((256, c_(C_MP)))
                if qt < 3:
                    masks.append((256 + P * (qt + 1 - lo), c_(C_MN)))
                sco.append((q, gk[e:e + 64, b, P * lo:P * lo + 256], 256, True, True))
                if hi - lo == 2:
                    sco.append((q, gk[e:e + 64, b, P * hi:P * hi + P], 512, True, True))
                tiles += list(range(lo, hi + 1))
                units.append(dict(sc=sco, n=P * len(tiles), masks=masks, scale=HD ** -0.5,
                                  sink=sink[:, hh:hh + 1], m=HD, o=64 * (hh % 2),
                                  v=[gv[:, k, HD * g:HD * g + HD] for k in tiles],
                                  out=go[64 * (hh % 2):64 * (hh % 2) + 64, hh // 2, q0:q0 + P]))
        n_mask = n_sink = 0
        for x in units:
            x["nmask"], x["nsink"] = n_mask, n_sink
            n_mask += len(x["masks"])
            n_sink += x["sink"] is not None

        def pe_attend(pe, u0, u1):
            for q in range(u0, u1 + 3):
                if q < u1:
                    x = units[q]
                    if q - u0 >= 2:
                        pe.wait_ge(at_ex, q - 1)
                    for lhs, rhs, c0, start, stop in x["sc"]:
                        mm = pe.matmul(pair(q % 2, 1024)[:, c0:c0 + rhs.shape[-1]], lhs, rhs, start=start, stop=stop)
                    mm.then_inc(at_sc, 1)
                i = q - 2
                if u0 <= i < u1:
                    pe.wait_ge(at_pn, i + 1)
                    if i > u0:
                        pe.wait_ge(at_pt, i)
                    nb = units[i]["n"] // P
                    for k in range(nb):
                        mm = pe.transpose(pair(2)[:, P * k:P * k + P], prob[:, i % 3, P * k:P * k + P], ident)
                    mm.then_inc(at_tr, 1)
                i = q - 3
                if u0 <= i < u1:
                    x = units[i]
                    pe.wait_ge(at_pt, i + 1)
                    if i - u0 >= 2:
                        pe.wait_ge(at_o, i - 1)
                    for k, v in enumerate(x["v"]):
                        mm = pe.matmul(bank(6 + i % 2)[x["o"]:x["o"] + x["m"], 0:P], v, probT[:, i % 2, P * k:P * k + P],
                                       start=k == 0, stop=k == len(x["v"]) - 1)
                    mm.then_inc(at_pv, 1)

        def act_attend(act, u0, u1):
            for q in range(u0, u1 + 2):
                if q < u1:
                    x = units[q]
                    act.wait_ge(at_nm, q + 1)
                    if q >= 3:
                        act.wait_ge(at_tr, q - 2)
                    act.activation(prob[:, q % 3, :x["n"]], pair(q % 2, 1024)[:, :x["n"]], ACT.Exp,
                                   bias=stat[:, 4 + q % 4:5 + q % 4], scale=x["scale"],
                                   accum_out=stat[:, 8 + q % 4:9 + q % 4]).then_inc(at_ex, 1)
                    if x["sink"] is not None:
                        act.activation(stat[:, 12 + q % 4:13 + q % 4], x["sink"], ACT.Exp,
                                       bias=stat[:, 4 + q % 4:5 + q % 4]).then_inc(at_sk, 1)
                i = q - 2
                if u0 <= i:
                    act.wait_ge(at_tr, i + 1)
                    if i >= 2:
                        act.wait_ge(at_pv, i - 1)
                    n = units[i]["n"]
                    act.copy(probT[:, i % 2, :n], pair(2, n)).then_inc(at_pt, 1)

        def dve_attend(dve, u0, u1):
            for q in range(u0, u1 + 3):
                if q < u1:
                    x = units[q]
                    dve.wait_ge(at_sc, q + 1)
                    s = pair(q % 2, 1024)
                    for c0, mk in x["masks"]:
                        dve.tensor_tensor(s[:, c0:c0 + P], mk, s[:, c0:c0 + P], ALU.add).then_inc(at_mk, 1)
                    if x["masks"]:
                        dve.wait_ge(at_mk, x["nmask"] + len(x["masks"]))
                    m = stat[:, q % 4:q % 4 + 1]
                    dve.tensor_reduce(m, s[:, :x["n"]], AX, ALU.max).then_inc(at_m0, 1)
                    dve.wait_ge(at_m0, q + 1)
                    nm = stat[:, 4 + q % 4:5 + q % 4]
                    if x["sink"] is not None:
                        dve.tensor_scalar(m, m, x["scale"], x["sink"], ALU.mult, ALU.max).then_inc(at_m1, 1)
                        dve.wait_ge(at_m1, x["nsink"] + 1)
                        dve.tensor_scalar(nm, m, -1.0, None, ALU.mult).then_inc(at_nm, 1)
                    else:
                        dve.tensor_scalar(nm, m, -x["scale"], None, ALU.mult).then_inc(at_nm, 1)
                i = q - 1
                if u0 <= i < u1:
                    x = units[i]
                    ls = stat[:, 8 + i % 4:9 + i % 4]
                    dve.wait_ge(at_ex, i + 1)
                    if x["sink"] is not None:
                        dve.wait_ge(at_sk, x["nsink"] + 1)
                        dve.tensor_tensor(ls, ls, stat[:, 12 + i % 4:13 + i % 4], ALU.add).then_inc(at_l, 1)
                        dve.wait_ge(at_l, x["nsink"] + 1)
                    ri = stat[:, 16 + i % 4:17 + i % 4]
                    dve.reciprocal(ri, ls).then_inc(at_ri, 1)
                    dve.wait_ge(at_ri, i + 1)
                    dve.tensor_scalar(prob[:, i % 3, :x["n"]], prob[:, i % 3, :x["n"]], ri, None,
                                      ALU.mult).then_inc(at_pn, 1)
                i = q - 3
                if u0 <= i < u1:
                    x = units[i]
                    dve.wait_ge(at_pv, i + 1)
                    dve.tensor_copy(x["out"], bank(6 + i % 2)[x["o"]:x["o"] + x["m"], 0:P]).then_inc(at_o, 1)

        PJ = [("dt", 0)] + [("c", i) for i in range(12)] + [("z", i) for i in range(8)]

        def sync_proj(f):
            f.put(block(w_ine, 0, 8, DT0, 32))
            with f.sp.Fori(0, 3) as i:
                for c in range(4):
                    f.put(block(w_ine, 0, 8, i * 512 + (XBC0 + P * c)), i, 4, c)
            f.n += 12
            with f.sp.Fori(0, 2) as i:
                for c in range(4):
                    f.put(block(w_ine, 0, 8, i * 512 + (Z0 + P * c)), i, 4, c)
            f.n += 8

        def pe_proj(pe, dr):
            def product(q, m, s):
                for k in range(DB):
                    for c0 in range(0, T, 512):
                        c1 = min(T, c0 + 512)
                        mm = pe.matmul(pair(q % 4)[0:m, c0:c1], slot(s, 8, m)[:, k, :], u[:, k, c0:c1],
                                       start=k == 0, stop=k == DB - 1)
                mm.then_inc(w_used, 1)

            pe.wait_ge(o_res, RES[R_MLA] + 8)
            product(0, 32, dr.get())
            for q in range(1, 5):
                if q == 4:
                    pe.wait_ge(pj_ev, 1)
                product(q, P, dr.get())
            with pe.Fori(1, 5) as i:
                for c in range(4):
                    pe.wait_ge(pj_ev, i * 4 + (c - 2))
                    product(1 + c, P, dr.get(i - 1, 4, c))
            dr.passed(16)

        def act_proj(act):
            b = BASE["proj"]
            for q in range(len(PJ) + 1):
                if q < len(PJ):
                    kind, i = PJ[q]
                    act.wait_ge(w_used, b + q + 1)
                    if kind == "dt":
                        act.activation(dtw[:, 0, :], pair(0)[0:32, :], ACT.Identity, bias=dtb).then_inc(pj_ev, 1)
                    elif kind == "c":
                        if i == 0:
                            act.wait_ge(pad_zero, 1)
                        if i >= 2:
                            act.wait_ge(cv_tap, 5 * (i - 1))
                        act.copy(pad[:, i % 2, 2:2 + SEQ], pair(q % 4)[:, 0:SEQ]).then_inc(cv_pad, 1)
                        act.copy(pad[:, i % 2, 4 + SEQ:4 + T], pair(q % 4)[:, SEQ:T]).then_inc(pj_ev, 1)
                    else:
                        act.activation(z[:, i, :], pair(q % 4), ACT.Silu).then_inc(pj_ev, 1)
                if q >= 2 and PJ[q - 1][0] == "c":
                    i = PJ[q - 1][1]
                    act.wait_ge(cv_tap, 5 * (i + 1))
                    dst = xs[:, i, :] if i < 8 else bc[:, i - 8, :]
                    bias = vb[:, VB_CB + i:VB_CB + i + 1]
                    act.activation(dst[:, 0:SEQ], cv[:, i % 2, 0:SEQ], ACT.Silu, bias=bias)
                    act.activation(dst[:, SEQ:T], cv[:, i % 2, 2 + SEQ:2 + T], ACT.Silu, bias=bias).then_inc(cv_out, 1)
            act.wait_ge(pj_ev, 1)
            act.activation(dtw[:, 1, :], dtw[:, 0, :], ACT.Abs).then_inc(dt_abs, 1)
            act.wait_ge(dt_abs, 1)
            act.activation(dtw[:, 1, :], dtw[:, 1, :], ACT.Exp, scale=-1.0).then_inc(dt_exp, 1)
            act.wait_ge(dt_exp, 1)
            act.activation(dtw[:, 2, :], dtw[:, 1, :], ACT.Ln, bias=1.0).then_inc(dt_ln, 1)
            act.activation(aexp, alog, ACT.Exp).then_inc(a_exp, 1)

        def dve_proj(dve):
            dve.wait_ge(at_o, n_mla)
            dve.wait_ge(o_res, RES[R_MLA] + 8)
            for b in range(2):
                dve.memset(pad[:, b, 0:2], 0.0)
                dve.memset(pad[:, b, 2 + SEQ:4 + SEQ], 0.0)
                x = dve.memset(pad[:, b, 4 + T:6 + T], 0.0)
            x.then_inc(pad_zero, 1)
            dve.wait_ge(pad_zero, 1)
            n = T + 2
            for i in range(12):
                dve.wait_ge(cv_pad, i + 1)
                dve.wait_ge(pj_ev, i + 2)
                if i >= 2:
                    dve.wait_ge(cv_out, i - 1)
                y = cv[:, i % 2, 0:n]
                for tap in range(5):
                    w = vc[:, 12 * tap + i:12 * tap + i + 1]
                    if tap:
                        dve.wait_ge(cv_tap, 5 * i + tap)
                        dve.scalar_tensor_tensor(out=y, in0=pad[:, i % 2, tap:tap + n], scalar=w, in1=y,
                                                 op0=ALU.mult, op1=ALU.add).then_inc(cv_tap, 1)
                    else:
                        dve.tensor_scalar(y, pad[:, i % 2, 0:n], w, None, ALU.mult).then_inc(cv_tap, 1)
            dve.wait_ge(dt_ln, 1)
            dve.scalar_tensor_tensor(out=dtw[:, 3, :], in0=dtw[:, 0, :], scalar=0.0, in1=dtw[:, 2, :],
                                     op0=ALU.max, op1=ALU.add).then_inc(dt_dt, 1)
            dve.wait_ge(dt_dt, 1)
            dve.wait_ge(a_exp, 1)
            dve.tensor_scalar(dtw[:, 4, :], dtw[:, 3, :], aexp, -1.0, ALU.mult, ALU.mult).then_inc(dt_da, 1)

        ORDER = ((4, 5, 0, 1, 2, 3), (5, 4, 3, 2, 1, 0))

        def pe_turn(pe):
            pe.wait_ge(dt_da, 1)
            pe.wait_ge(pj_ev, len(PJ))
            for kk in range(2):
                for c in range(NT):
                    mm = pe.transpose(bank(0)[:, 192 * kk + 32 * c:192 * kk + 32 * c + 32],
                                      dtw[:, 3 + kk, P * c:P * c + P], ident[0:32, 0:32])
            mm.then_inc(tk_dt, 1)
            pe.wait_ge(cv_out, 12)
            for c in range(NT):
                if c >= 2:
                    pe.wait_ge(tk_xc, c - 1)
                for b in range(8):
                    mm = pe.transpose(pair(1 + c % 2, 1024)[:, P * b:P * b + P], xs[:, b, P * c:P * c + P], ident)
                mm.then_inc(tk_x, 1)
            for c2 in range(3):
                if c2 == 2:
                    pe.wait_ge(tk_bc, 1)
                for k in range(4):
                    c, g = 2 * c2 + k // 2, k % 2
                    mm = pe.transpose(bank(6 + c2 % 2)[:, P * k:P * k + P], bc[:, g, P * c:P * c + P], ident)
                mm.then_inc(tk_b, 1)

        def dve_turn(dve):
            dve.wait_ge(tk_dt, 1)
            dve.tensor_copy(mix[:, 14848:15232], bank(0, 0, 384)).then_inc(tk_dtc, 1)
            for c in range(NT):
                dve.wait_ge(tk_x, c + 1)
                dve.tensor_copy(xtok[:, c, :], pair(1 + c % 2, 1024)).then_inc(tk_xc, 1)
            for c2 in range(3):
                dve.wait_ge(tk_b, c2 + 1)
                dve.tensor_copy(big[:, 20 * T + 512 * c2:20 * T + 512 * c2 + 512], bank(6 + c2 % 2)).then_inc(tk_bc, 1)
            dve.wait_ge(dc_exp, 1)
            dve.tensor_tensor(wdt[:, 0], dec[:, 0:96].rearrange("p (c h) -> p c h", c=NT), dtk[:, 0, :, 0:16], ALU.mult)
            dve.tensor_tensor(wdt[:, 1], dec[:, 96:192].rearrange("p (c h) -> p c h", c=NT), dtk[:, 0, :, 16:32],
                              ALU.mult).then_inc(dc_w, 1)

        def pe_decay(pe):
            pe.wait_ge(tk_dtc, 1)
            pe.matmul(bank(0, 0, 96), c_(C_UF), dtk[:, 1, :, 0:16], start=True, stop=True)
            pe.matmul(bank(0, 96, 192), c_(C_UB), dtk[:, 1, :, 16:32], start=True, stop=True)
            pe.matmul(bank(0, 192, 384), ones, dtk[:, 1, :, :], start=True, stop=True).then_inc(dc_mm, 1)

        def act_decay(act):
            act.wait_ge(dc_mm, 1)
            act.activation(dec[:, 0:384], bank(0, 0, 384), ACT.Exp).then_inc(dc_exp, 1)

        STEPS = [(g, dr_, k) for g in range(2) for k in range(5) for dr_ in range(2)]

        def head_bc(v, n):
            return v.rearrange("p (h o) -> p h o", o=1).broadcast_to([P, v.shape[-1], n])

        def pool_states(pool, g):
            for q in range(10 * g, 10 * g + 10):
                _, dr_, k = STEPS[q]
                c = ORDER[dr_][k]
                if q == 0:
                    pool.wait_ge(dc_w, 1)
                    pool.wait_ge(tk_xc, NT)
                if q % 10 == 0 and g == 1:
                    pool.wait_ge(y_mm, 12)
                if q >= 2:
                    pool.wait_ge(s_mm, q - 1)
                pool.tensor_tensor(xw[:, q % 2, :].rearrange("p (h n) -> p h n", n=SP),
                                   xtok[:, c, 512 * g:512 * g + 512].rearrange("p (h n) -> p h n", n=SP),
                                   head_bc(wdt[:, dr_, c, 8 * g:8 * g + 8], SP), ALU.mult).then_inc(s_xw, 1)

        def pe_states(pe, g):
            for q in range(10 * g, 10 * g + 10):
                _, dr_, k = STEPS[q]
                c = ORDER[dr_][k]
                pe.wait_ge(s_xw, q + 1)
                if q == 0:
                    pe.wait_ge(tk_bc, 3)
                if q == 10:
                    pe.wait_ge(y_out, 12)
                if q >= 2:
                    pe.wait_ge(s_st, q - 1)
                pe.matmul(bank(6 + q % 2), btok[:, c, P * g:P * g + P], xw[:, q % 2, :],
                          start=True, stop=True).then_inc(s_mm, 1)

        def dve_states(dve, g):
            ndec = 8 * g
            for q in range(10 * g, 10 * g + 10):
                _, dr_, k = STEPS[q]
                c = ORDER[dr_][k]
                s = st[:, dr_, k, :]
                if k == 0:
                    dve.wait_ge(s_mm, q + 1)
                    dve.tensor_copy(s, bank(6 + q % 2)).then_inc(s_st, 1)
                    continue
                dve.wait_ge(s_st, q - 1)
                h0 = 16 * dr_ + 8 * g
                dve.tensor_tensor(s.rearrange("p (h n) -> p h n", n=SP),
                                  st[:, dr_, k - 1, :].rearrange("p (h n) -> p h n", n=SP),
                                  head_bc(dcb[:, c, h0:h0 + 8], SP), ALU.mult).then_inc(s_dec, 1)
                ndec += 1
                dve.wait_ge(s_dec, ndec)
                dve.wait_ge(s_mm, q + 1)
                dve.tensor_tensor(s, s, bank(6 + q % 2), ALU.add).then_inc(s_st, 1)

        def pe_gram(pe, g):
            for c in range(NT):
                q = NT * g + c
                if q % NT >= 2:
                    pe.wait_ge(g_done, 2 * (q - 1))
                elif g == 1:
                    pe.wait_ge(s_st, 20)
                else:
                    pe.wait_ge(s_st, 10)
                t0 = P * c
                pe.matmul(bank(6 + c % 2, 0, P), bc[:, g, t0:t0 + P], bc[:, 2 + g, t0:t0 + P],
                          start=True, stop=True).then_inc(g_mm, 1)

        def dve_gram(dve, g):
            for c in range(NT):
                dve.wait_ge(g_mm, NT * g + c + 1)
                for dr_, tri in ((0, C_TF), (1, C_TB)):
                    dve.tensor_tensor(gg[:, c, dr_, :], c_(tri), bank(6 + c % 2, 0, P), ALU.mult).then_inc(g_done, 1)

        YU = [(g, c, hf) for g in range(2) for c in range(NT) for hf in range(2)]

        def pool_y(pool, g):
            for v in range(12 * g, 12 * g + 12):
                _, c, hf = YU[v]
                q = v // 2
                if hf == 0:
                    if v % 12 == 0:
                        pool.wait_ge(s_mm, 10 * g + 10)
                    if q % NT >= 2:
                        pool.wait_ge(y_mm, 2 * (q - 1))
                    for dr_ in range(2):
                        pool.tensor_tensor(xdt[:, q % 2, dr_, :].rearrange("p (h n) -> p h n", n=SP),
                                           xtok[:, c, 512 * g:512 * g + 512].rearrange("p (h n) -> p h n", n=SP),
                                           head_bc(dtk[:, 0, c, 16 * dr_ + 8 * g:16 * dr_ + 8 * g + 8], SP),
                                           ALU.mult).then_inc(y_xdt, 1)
                if v >= 2:
                    pool.wait_ge(y_seg, v - 1)
                for dr_, tri in ((0, C_TF), (1, C_TB)):
                    h0 = 16 * dr_ + 8 * g + 4 * hf
                    pool.tensor_tensor(rr[:, v % 2, dr_, :].rearrange("p (h n) -> p h n", n=P),
                                       c_(tri).rearrange("p (o n) -> p o n", o=1).broadcast_to([P, 4, P]),
                                       head_bc(dtk[:, 1, c, h0:h0 + 4], P), ALU.mult).then_inc(y_r, 1)

        def pe_y(pe, g):
            for v in range(12 * g, 12 * g + 13):
                if v < 12 * g + 12:
                    pe.wait_ge(y_r, 2 * v + 2)
                    if v % 12 < 2:
                        pe.wait_ge(s_st, 10 * g + 10)
                        pe.wait_ge(g_done, 12 * g + 12)
                    if v >= 2:
                        pe.wait_ge(y_exp, v - 1)
                    b = 3 * (v % 2)
                    pe.matmul(bank(b), c_(C_UF), rr[:, v % 2, 0, :], start=True, stop=False)
                    pe.matmul(bank(b), c_(C_UB), rr[:, v % 2, 1, :], start=False, stop=True)
                    pe.matmul(bank(b + 1), ones, rr[:, v % 2, 0, :], start=True, stop=True)
                    pe.matmul(bank(b + 2), ones, rr[:, v % 2, 1, :], start=True, stop=True).then_inc(y_seg, 1)
                w = v - 1
                if w >= 12 * g:
                    _, c, hf = YU[w]
                    q = w // 2
                    pe.wait_ge(y_m, 4 * w + 4)
                    pe.wait_ge(y_xdt, 2 * q + 2)
                    if w % 12 >= 2:
                        pe.wait_ge(y_out, w - 1)
                    e = ee[:, w % 2, :]
                    for pp in range(2):
                        for eo in range(2):
                            i = 2 * pp + eo
                            at = bank(6 + w % 2)[64 * eo:64 * eo + 64, P * pp:P * pp + P]
                            x0 = SP * (4 * hf + i)
                            terms = [(xdt[:, q % 2, 0, x0:x0 + SP], mf[:, w % 2, P * i:P * i + P]),
                                     (xdt[:, q % 2, 1, x0:x0 + SP], e[:, P * i:P * i + P])]
                            for dr_ in range(2):
                                k = ORDER[dr_].index(c)
                                if k:
                                    terms.append((st[:, dr_, k - 1, x0:x0 + SP],
                                                  e[:, 512 * (1 + dr_) + P * i:512 * (1 + dr_) + P * i + P]))
                            for n, (lhs, rhs) in enumerate(terms):
                                mm = pe.matmul(at, lhs, rhs, start=n == 0, stop=n == len(terms) - 1)
                    mm.then_inc(y_mm, 1)

        def act_y(act, g):
            for v in range(12 * g, 12 * g + 12):
                act.wait_ge(y_seg, v + 1)
                if v >= 2:
                    act.wait_ge(y_mm, v - 1)
                act.activation(ee[:, v % 2, :], ps[:, 1536 * (v % 2):1536 * (v % 2) + 1536], ACT.Exp).then_inc(y_exp, 1)

        def dve_y(dve, g):
            for v in range(12 * g, 12 * g + 13):
                if v < 12 * g + 12:
                    _, c, hf = YU[v]
                    dve.wait_ge(y_exp, v + 1)
                    if v % 12 == 0:
                        dve.wait_ge(g_done, 12 * g + 12)
                    if v >= 2:
                        dve.wait_ge(y_mm, v - 1)
                    e = ee[:, v % 2, :].rearrange("p (k h n) -> p k h n", k=3, h=4)
                    over = lambda x: x.rearrange("p (o n) -> p o n", o=1).broadcast_to([P, 4, P])
                    dve.tensor_tensor(mf[:, v % 2, :].rearrange("p (h n) -> p h n", h=4), e[:, 0],
                                      over(gg[:, c, 0, :]), ALU.mult).then_inc(y_m, 1)
                    dve.tensor_tensor(e[:, 0], e[:, 0], over(gg[:, c, 1, :]), ALU.mult).then_inc(y_m, 1)
                    cc = over(bc[:, 2 + g, P * c:P * c + P])
                    dve.tensor_tensor(e[:, 1], e[:, 1], cc, ALU.mult).then_inc(y_m, 1)
                    dve.tensor_tensor(e[:, 2], e[:, 2], cc, ALU.mult).then_inc(y_m, 1)
                w = v - 1
                if w >= 12 * g:
                    _, c, hf = YU[w]
                    dve.wait_ge(y_mm, w + 1)
                    for pp in range(2):
                        b = 4 * g + 2 * hf + pp
                        y = xs[:, b, P * c:P * c + P]
                        x = dve.scalar_tensor_tensor(out=y, in0=y, scalar=dskip[:, b:b + 1],
                                                     in1=bank(6 + w % 2, P * pp, P * pp + P),
                                                     op0=ALU.mult, op1=ALU.add)
                    x.then_inc(y_out, 1)

        def pool_merge(pool):
            pool.wait_ge(y_out, 24)
            for b in range(8):
                pool.tensor_tensor(xs[:, b, :], xs[:, b, :], z[:, b, :], ALU.mult).then_inc(m_z, 1)

        def act_merge(act):
            act.wait_ge(y_mm, 24)
            for b in range(8):
                act.wait_ge(m_z, b + 1)
                if b >= 2:
                    act.wait_ge(m_ss, b - 1)
                act.activation(sqn[:, b % 2, :], xs[:, b, :], ACT.Square).then_inc(m_sq, 1)
            for g in range(2):
                act.wait_ge(m_ss, 4 * g + 4)
                if g == 1:
                    act.wait_ge(m_y, 4)
                act.activation(rsn, pair(2 + g), ACT.Ln, bias=eps, scale=1.0 / 512).then_inc(m_ln, 1)
                act.wait_ge(m_ln, g + 1)
                act.activation(rsn, rsn, ACT.Exp, scale=-0.5).then_inc(m_rs, 1)

        def pe_merge(pe):
            pe.wait_ge(y_out, 24)
            for b in range(8):
                pe.wait_ge(m_sq, b + 1)
                for c0, c1 in ((0, 512), (512, T)):
                    mm = pe.matmul(pair(2 + b // 4)[:, c0:c1], ones, sqn[:, b % 2, c0:c1], start=b % 4 == 0, stop=b % 4 == 3)
                mm.then_inc(m_ss, 1)
            pe.wait_ge(m_y, 8)

        def dve_merge(dve):
            for b in range(8):
                dve.wait_ge(m_rs, b // 4 + 1)
                dve.wait_ge(m_sq, b + 1)
                dve.scalar_tensor_tensor(out=xs[:, b, :], in0=xs[:, b, :], scalar=vb[:, VB_SSD + b:VB_SSD + b + 1],
                                         in1=rsn, op0=ALU.mult, op1=ALU.mult).then_inc(m_y, 1)

        def sync_ff(f, i_f):
            for half in range(2):
                sync_ffi(f, i_f, half)
                sync_out(f, R_FF(i_f, half))

        def pe_ff(pe, dr, i_f):
            for half in range(2):
                pe_ffi(pe, dr, i_f, half)
                pe_out(pe, dr, R_FF(i_f, half))

        def act_ff(act, ar, i_f):
            for half in range(2):
                act_ffi(act, ar, i_f, half)
                act_out_ff(act, ar, R_FF(i_f, half))

        def dve_ff(dve, dv, i_f):
            for half in range(2):
                dve_ffi(dve, dv, i_f, half)
                dve_out_ff(dve, dv, R_FF(i_f, half))

        block_ = ctx.enter_context(nc.Block())

        @block_.sync
        def _(sp):
            f = Filler(sp)
            sp.dma_start(cst[:, :], a["shape_constants"]).then_inc(const_in, 16)
            flat = lambda x: x.rearrange("l (n p) -> l n p", p=P)
            for dst, src in [
                (rows[VA_MOD:VA_MOD + 72, 0, :], flat(a["b_mod"])[0]),
                (rows[VA_C:VA_C + 8, 0, :], flat(a["c"])[0]),
                (rows[VA_CC:VA_CC + 8, 0, :], a["c_ctx"].rearrange("(n p) -> n p", p=P)),
                (rows[VB_MOD:VB_MOD + 72, 1, :], flat(a["b_mod"])[1]),
                (rows[VB_SSD:VB_SSD + 8, 1, :], flat(a["ssd_norm"])[0]),
                (rows[VB_QA:VB_QA + 3, 1, :], flat(a["mla_qa_norm"])[0]),
                (rows[VB_KV:VB_KV + 2, 1, :], flat(a["mla_kv_norm"])[0]),
                (rows[VB_QN:VB_QN + 1, 1, :], a["mla_qn_norm"]),
                (rows[VB_KN:VB_KN + 1, 1, :], a["mla_kn_norm"]),
                (rows[VB_QR:VB_QR + 1, 1, 0:64], a["mla_qr_norm"]),
                (rows[VB_QR:VB_QR + 1, 1, 64:128], a["mla_qr_norm"]),
                (rows[VB_KR:VB_KR + 1, 1, 0:64], a["mla_kr_norm"]),
                (rows[VB_KR:VB_KR + 1, 1, 64:128], a["mla_kr_norm"]),
                (rows[VB_GQ:VB_GQ + 1, 1, 0:64], a["gqa_q_norm"]),
                (rows[VB_GQ:VB_GQ + 1, 1, 64:128], a["gqa_q_norm"]),
                (rows[VB_GK:VB_GK + 1, 1, 0:64], a["gqa_k_norm"]),
                (rows[VB_GK:VB_GK + 1, 1, 64:128], a["gqa_k_norm"]),
                (rows[VB_CB:VB_CB + 12, 1, :], flat(a["conv_b"])[0]),
                (rows[0:60, 2, :], a["conv_w"][0].rearrange("t (n p) -> (t n) p", p=P)),
                (dtb, a["dt_bias"][0].rearrange("a (h o) -> (a h) o", o=1)),
                (alog, a["a_log"][0].rearrange("a (h o) -> (a h) o", o=1)),
                (dskip[0:64, :], a["d_skip"].rearrange("l (b e) -> l b e", e=2)[:, :, 0].broadcast_to([64, 8])),
                (dskip[64:128, :], a["d_skip"].rearrange("l (b e) -> l b e", e=2)[:, :, 1].broadcast_to([64, 8])),
                (sink[:, :], a["sink"].broadcast_to([P, QH])),
            ]:
                sp.dma_start(dst, src, allow_slow_non_contiguous=True).then_inc(rows_in, 16)
            for n in range(NT):
                src = a["x"][0, P * n:P * n + P, :] if n < 4 else a["ctx"][0, P * (n - 4):P * (n - 3), :]
                sp.dma_start(xin[:, n, :], src).then_inc(x_in, 16)
            for d in range(DB):
                for q in range(3):
                    f.put(block(w_mod[0], 0, 8, q * D + P * d))
            sync_ff(f, 0)
            assert f.n == BASE["even"]
            sync_items(f, 0, n_even)
            sync_v(f, "e")
            sync_out(f, R_MLA)
            sync_proj(f)
            sync_out(f, R_SSD)
            sync_ff(f, 1)
            sync_ff(f, 2)
            sync_items(f, n_even, len(items))
            sync_v(f, "o")
            sync_out(f, R_GQA)
            sync_ff(f, 3)
            assert f.n == n_
            for n in range(SEQ // P):
                sp.wait_ge(out_c, 2 * n + 2)
                sp.dma_start(out[P * n:P * n + P, :], xin[:, n, :]).then_inc(out_st, 16)
            sp.wait_ge(out_st, 16 * (SEQ // P))

        @block_.tensor
        def _(pe):
            dr = Drainer(pe)
            pe.wait_ge(const_in, 16)
            pe.wait_ge(rows_in, 16 * 24)
            for n, rn in ((0, VA_N), (1, VB_N), (2, VC_N)):
                mm = pe.transpose(bank(7)[:, P * n:P * n + rn], rows[0:rn, n, :], ident[0:rn, 0:rn])
            mm.then_inc(vec_t, 1)
            pe.wait_ge(x_in, 16 * NT)
            for d in range(DB):
                if d >= 2:
                    pe.wait_ge(h_loaded, d - 1)
                for n in range(NT):
                    mm = pe.transpose(pair(d % 2)[:, P * n:P * n + P], xin[:, n, P * d:P * d + P], ident)
                mm.then_inc(xt_done, 1)
            pe.wait_ge(sc_done, 1)
            for d in range(DB):
                for q in range(3):
                    pe_mod_block(pe, dr.get(), 16 * q + 2 * d)
            pe.wait_ge(vec_done, 3)
            pe_norm(pe, 0)
            pe_ff(pe, dr, 0)
            pe_norm(pe, 1)
            pe_items(pe, dr, 0, n_even, 1)
            pe_v(pe, dr, "e")
            pe.wait_ge(v_done, 12)
            pe.wait_ge(hn_fin, ropes_to(n_even))
            pe.wait_ge(hn_n, norms_to(n_even))
            pe_attend(pe, 0, n_mla)
            pe.wait_ge(at_o, n_mla)
            pe_out(pe, dr, R_MLA)
            pe_proj(pe, dr)
            pe_turn(pe)
            pe_decay(pe)
            for g in range(2):
                pe_states(pe, g)
                pe_gram(pe, g)
                pe_y(pe, g)
            pe_merge(pe)
            pe_out(pe, dr, R_SSD)
            for i_f in (1, 2):
                pe_norm(pe, FF_NORM[i_f])
                pe_ff(pe, dr, i_f)
            pe_norm(pe, 4)
            pe_items(pe, dr, n_even, len(items), 4)
            pe_v(pe, dr, "o")
            pe.wait_ge(v_done, 24)
            pe.wait_ge(hn_fin, ropes_to(len(items)))
            pe_attend(pe, n_mla, len(units))
            pe.wait_ge(at_o, len(units))
            pe_out(pe, dr, R_GQA)
            pe_norm(pe, 5)
            pe_ff(pe, dr, 3)
            for n in range(SEQ // P):
                if n >= 2:
                    pe.wait_ge(out_c, 2 * (n - 1))
                for d in range(DB):
                    if n == 0:
                        pe.wait_ge(o_res, RES[R_FF(3, 1)] + d + 1)
                    mm = pe.transpose(pair(2 + n % 2, 1024)[:, P * d:P * d + P], h[:, d, P * n:P * n + P], ident)
                mm.then_inc(out_t, 1)

        @block_.scalar
        def _(act):
            act.wait_ge(vec_done, 1)
            act.activation(sc[:, :].rearrange("p (k s) -> p s k", s=2),
                           va[:, VA_C:VA_C + 16].rearrange("p (s k) -> p s k", s=2), ACT.Silu).then_inc(sc_done, 1)
            ar = Drainer(act)
            ar.passed(24)
            act_norm(act, 0)
            act_ff(act, ar, 0)
            act_norm(act, 1)
            ar.passed_items(0, n_even)
            ar.passed_v(2)
            ar.passed(out_plan(R_MLA)[1] * DB + 21 + out_plan(R_SSD)[1] * DB)
            act_items(act, 0, n_even, BASE["even"])
            act_attend(act, 0, n_mla)
            act_proj(act)
            act_decay(act)
            act_y(act, 0)
            act_y(act, 1)
            act_merge(act)
            for i_f in (1, 2):
                act_norm(act, FF_NORM[i_f])
                act_ff(act, ar, i_f)
            act_norm(act, 4)
            ar.passed_items(n_even, len(items))
            ar.passed_v(1)
            ar.passed(out_plan(R_GQA)[1] * DB)
            act_items(act, n_even, len(items), BASE["odd"])
            act_attend(act, n_mla, len(units))
            act_norm(act, 5)
            act_ff(act, ar, 3)
            for n in range(SEQ // P):
                act.wait_ge(out_t, n + 1)
                act.wait_ge(w_used, n_)
                act.copy(xin[:, n, 0:512], pair(2 + n % 2, 1024)[:, 0:512]).then_inc(out_c, 1)
                act.copy(xin[:, n, 512:1024], pair(2 + n % 2, 1024)[:, 512:1024]).then_inc(out_c, 1)

        @block_.vector
        def _(dve):
            dve.memset(eps, EPS).then_inc(eps_set, 1)
            dve.wait_ge(vec_t, 1)
            for n, (v, rn) in enumerate(((va, VA_N), (vb, VB_N), (vc, VC_N))):
                dve.tensor_copy(v[:, :], bank(7)[:, P * n:P * n + rn]).then_inc(vec_done, 1)
            for d in range(DB):
                dve.wait_ge(xt_done, d + 1)
                dve.tensor_copy(h[:, d, :], pair(d % 2)).then_inc(h_loaded, 1)
            dve.wait_ge(vec_done, 3)
            dve_mod(dve, 0, 24)
            dv = Drainer(dve)
            dv.n = BASE["ffi", 0, 0]
            dve_norm(dve, 0)
            dve_ff(dve, dv, 0)
            dve_norm(dve, 1)
            dve_items(dve, 0, n_even)
            dve_v(dve, "e")
            dve_attend(dve, 0, n_mla)
            dv.n = BASE["out", R_MLA]
            dve_out(dve, dv, R_MLA)
            dve_proj(dve)
            dve_turn(dve)
            for g in range(2):
                dve_states(dve, g)
                dve_gram(dve, g)
                dve_y(dve, g)
            dve_merge(dve)
            dv.n = BASE["out", R_SSD]
            dve_out(dve, dv, R_SSD)
            for i_f in (1, 2):
                dve_norm(dve, FF_NORM[i_f])
                dve_ff(dve, dv, i_f)
            dve_norm(dve, 4)
            dve_items(dve, n_even, len(items))
            dve_v(dve, "o")
            dve_attend(dve, n_mla, len(units))
            dv.n = BASE["out", R_GQA]
            dve_out(dve, dv, R_GQA)
            dve_norm(dve, 5)
            dve_ff(dve, dv, 3)

        @block_.gpsimd
        def _(pool):
            for g in range(2):
                pool_states(pool, g)
                pool_y(pool, g)
            pool_merge(pool)


INPUTS = ["x", "c", "ctx", "c_ctx", "w_mod", "b_mod", "w_ff1_in", "w_ff1_out", "w_ff2_in", "w_ff2_out",
          "w_in_e", "conv_w", "conv_b", "dt_bias", "a_log", "d_skip", "ssd_norm", "mla_qa_norm", "w_qb",
          "mla_kv_norm", "w_kvb", "mla_qn_norm", "mla_qr_norm", "mla_kn_norm", "mla_kr_norm", "w_out_e",
          "w_in_o", "gqa_q_norm", "gqa_k_norm", "sink", "w_out_o"]


def kernel(**inputs):
    import concourse.bacc as bacc
    from concourse.bass_utils import run_bass_kernel_spmd

    nc = bacc.Bacc("TRN2", target_bir_lowering=False, num_devices=1)
    arrays = {"shape_constants": shape_constants()}
    for name in INPUTS:
        arrays[name] = np.ascontiguousarray(inputs[name])
    sent, aps = {}, {}
    for name, v in arrays.items():
        sent[f"in_{name}"] = v
        aps[name] = nc.dram_tensor(f"in_{name}", v.shape, mybir.dt.from_np(v.dtype), kind="ExternalInput").ap()
    out = nc.dram_tensor("out_h", (SEQ, D), F32, kind="ExternalOutput").ap()
    build(nc, aps, out)
    r = run_bass_kernel_spmd(nc, [sent], core_ids=[0])
    return r.results[0]["out_h"].reshape(1, SEQ, D)
```

```python
from contextlib import ExitStack

import numpy as np

import concourse.bass as bass
from concourse import mybir

F32 = mybir.dt.float32
F32R = mybir.dt.float32r
ACT = mybir.ActivationFunctionType
ALU = mybir.AluOpType
AX = mybir.AxisListType.X

P = 128
D = 1024
DB = D // P
SEQ, CTX = 512, 256
T = SEQ + CTX
GRID_W = 64
FFN = 2816
FB = FFN // P
EPS = 1e-6
NT = T // P
SEGS = ((0, SEQ, 0), (SEQ, T, 1))

Z0, XBC0, DT0, QA0, CKV0, KR0 = 0, 1024, 2560, 2592, 2976, 3232
HEADS, SP = 16, 64
MH, DN, DR, DV = 8, 128, 64, 128
QH, KVH, HD = 16, 4, 64

PART = (8, 8, 6)
RING = 4
SLOT = 8 * P

C_ID, C_ONE, C_BLK, C_UF, C_UB, C_TF, C_TB, C_MP, C_MN, C_SW, C_COS, C_SIN = (
    0, 128, 256, 384, 512, 640, 768, 896, 1024, 1152, 1280, 1792)
C_ALL = 2304
NEG = -1.0e30

VA_MOD, VA_C, VA_CC, VA_N = 0, 72, 80, 88
VB_MOD, VB_SSD, VB_QA, VB_KV, VB_QN, VB_KN, VB_QR, VB_KR, VB_GQ, VB_GK, VB_CB, VB_N = (
    0, 72, 80, 83, 85, 86, 87, 88, 89, 90, 91, 103)
VC_N = 60


def shape_constants():
    c = np.zeros((P, C_ALL), np.float32)
    i = np.arange(P)
    c[:, C_ID:C_ID + P] = np.eye(P)
    c[:, C_ONE:C_ONE + P] = 1.0
    c[:, C_BLK:C_BLK + P] = (i[:, None] // 64) == (i[None, :] // 64)
    c[:, C_UF:C_UF + P] = i[:, None] > i[None, :]
    c[:, C_UB:C_UB + P] = i[:, None] < i[None, :]
    c[:, C_TF:C_TF + P] = i[:, None] <= i[None, :]
    c[:, C_TB:C_TB + P] = i[:, None] >= i[None, :]
    c[:, C_MP:C_MP + P] = np.where(i[None, :] >= i[:, None], 0.0, NEG)
    c[:, C_MN:C_MN + P] = np.where(i[None, :] <= i[:, None], 0.0, NEG)
    swap = np.zeros((P, P), np.float32)
    for o in range(P):
        j = o % 32
        if j < 16:
            swap[o + 16, o] = -1.0
        else:
            swap[o - 16, o] = 1.0
    c[:, C_SW:C_SW + P] = swap
    quarter = 16
    freqs = (np.float32(10000.0) ** (-np.arange(quarter, dtype=np.float32) / np.float32(quarter))).astype(np.float32)
    t = np.arange(SEQ)
    pos = np.stack([(t // GRID_W), (t % GRID_W)]).astype(np.float32)
    for p in range(P):
        ang = pos[(p % 64) // 32] * freqs[p % 16]
        c[p, C_COS:C_COS + SEQ] = np.cos(ang)
        c[p, C_SIN:C_SIN + SEQ] = np.sin(ang)
    return c


def head_norm_items():
    items = []
    for i in range(3):
        items.append(dict(kind="qa", i=i, start=i == 0, stop=i == 2, rope=False, t=T))
    for i in range(2):
        items.append(dict(kind="ckv", i=i, start=i == 0, stop=i == 1, rope=False, t=T))
    items.append(dict(kind="kr", i=0, start=True, stop=True, rope=True, t=T))
    for kind, n, rope in (("qn", MH, False), ("kn", MH, False), ("qr", MH // 2, True)):
        for i in range(n):
            items.append(dict(kind=kind, i=i, start=True, stop=True, rope=rope, t=T))
    n_even = len(items)
    for i in range(2):
        items.append(dict(kind="gk", i=i, start=True, stop=True, rope=True, t=T))
    for i in range(8):
        items.append(dict(kind="gq", i=i, start=True, stop=True, rope=True, t=SEQ))
    norms = ropes = 0
    for it in items:
        it["norm"] = norms
        it["nrope"] = ropes
        norms += it["stop"]
        ropes += it["rope"]
    return items, n_even


def build(nc, a, out):
    items, n_even = head_norm_items()
    norms_to = lambda m: sum(x["stop"] for x in items[:m])
    ropes_to = lambda m: sum(x["rope"] for x in items[:m])

    with ExitStack() as ctx:
        def sb(name, cols):
            return ctx.enter_context(nc.sbuf_tensor(name, [P, cols], F32))

        def sem(name):
            return ctx.enter_context(nc.semaphore(name))

        ps = ctx.enter_context(nc.psum_tensor("ps", [P, 4096], F32))

        def pair(p, n=T):
            return ps[:, 1024 * p:1024 * p + n]

        def bank(b, c0=0, c1=512):
            return ps[:, 512 * b + c0:512 * b + c1]

        h_sb = sb("h_sb", DB * T)
        arena = -(-nc.sbuf_base // 32) * 32

        def at(name, first, cols, dt=F32):
            return nc.alloc_sbuf_tensor_at(name, [P, cols], dt, offset=arena + 4 * first)

        u_sb = at("u_sb", 0, 8 * T)
        big = at("big", 8 * T, 22 * T)
        mix = at("mix", 30 * T, 21 * T)
        u_hi, u_lo = at("u_hi", 0, 8 * T, F32R), at("u_lo", 8 * T, 8 * T, F32R)
        hid_hi, hid_lo = at("hid_hi", 16 * T, PART[0] * T, F32R), at("hid_lo", 24 * T, PART[0] * T, F32R)
        hid_f = at("hid_f", 32 * T, 2 * T)
        m_in = [at(f"m_in{i}", x * T, 2 * D) for i, x in enumerate((20, 34))]
        m_hi = [at(f"m_hi{i}", x * T, 2 * D, F32R) for i, x in enumerate((20, 34))]
        m_sum, m_lo = at("m_sum", 37 * T, 6 * D), at("m_lo", 37 * T, 6 * D, F32R)
        w_hi, w_lo = (at(n, 51 * T - 4 * SLOT + 2 * SLOT * i, 2 * SLOT, F32R) for i, n in enumerate(("w_hi", "w_lo")))
        sb("stretch", (arena - nc.sbuf_base) // 4 + 51 * T)
        ring = sb("ring", RING * SLOT)
        ones_r = ctx.enter_context(nc.sbuf_tensor("ones_r", [P, 2], F32R))
        cst = sb("cst", C_ALL)
        va, vb, vc = sb("va", VA_N), sb("vb", VB_N), sb("vc", VC_N)
        mod = sb("mod", 6 * 48)
        sc = sb("sc", 16)
        small = sb("small", 64)
        dskip = sb("dskip", 8)
        sink = sb("sink", QH)
        stat = sb("stat", 32)

        h = h_sb[:, :].rearrange("p (b t) -> p b t", t=T)
        u = u_sb[:, :].rearrange("p (b t) -> p b t", t=T)
        u_hi, u_lo, hid_hi, hid_lo, hid_f = (
            x[:, :].rearrange("p (b t) -> p b t", t=T) for x in (u_hi, u_lo, hid_hi, hid_lo, hid_f))

        def c_(at, n=P):
            return cst[:, at:at + n]

        ident, ones, blk64 = c_(C_ID), c_(C_ONE), c_(C_BLK)
        eps = small[:, 0:1]
        dtb, alog, aexp = small[0:32, 1:2], small[0:32, 2:3], small[0:32, 3:4]

        sqn = mix[:, 4 * T:6 * T].rearrange("p (b t) -> p b t", t=T)
        rsn = mix[:, 6 * T:7 * T]
        xin = u_sb[:, :].rearrange("p (n d) -> p n d", d=D)
        rows = mix[:, 4096:4096 + 3 * P].rearrange("p (n d) -> p n d", d=P)
        kn = big[:, 0:8 * T].rearrange("p (b t) -> p b t", t=T)
        vt = big[:, 8 * T:8 * T + NT * D].rearrange("p (n d) -> p n d", d=D)
        ckv = big[:, 16 * T:18 * T].rearrange("p (b t) -> p b t", t=T)
        qa = big[:, 18 * T:21 * T].rearrange("p (b t) -> p b t", t=T)
        qn = mix[:, 0:8 * T].rearrange("p (b t) -> p b t", t=T)
        qr = mix[:, 8 * T:12 * T].rearrange("p (b t) -> p b t", t=T)
        kr = mix[:, 12 * T:13 * T]
        sqh = mix[:, 13 * T:15 * T].rearrange("p (b t) -> p b t", t=T)
        rsh = mix[:, 15 * T:17 * T].rearrange("p (b t) -> p b t", t=T)
        prob = mix[:, 17 * T:20 * T].rearrange("p (b t) -> p b t", t=T)
        probT = mix[:, 13 * T:15 * T].rearrange("p (b t) -> p b t", t=T)
        gq = big[:, 0:8 * T].rearrange("p (b t) -> p b t", t=T)
        gk = big[:, 8 * T:10 * T].rearrange("p (b t) -> p b t", t=T)
        gv = big[:, 10 * T:10 * T + NT * 256].rearrange("p (n d) -> p n d", d=256)
        go = big[:, 12 * T:20 * T].rearrange("p (b t) -> p b t", t=T)
        xs = big[:, 0:8 * T].rearrange("p (b t) -> p b t", t=T)
        bc = big[:, 8 * T:12 * T].rearrange("p (b t) -> p b t", t=T)
        z = big[:, 12 * T:20 * T].rearrange("p (b t) -> p b t", t=T)
        btok = big[:, 20 * T:20 * T + NT * 256].rearrange("p (n d) -> p n d", d=256)
        xtok = u_sb[:, :].rearrange("p (n d) -> p n d", d=D)
        PADC = T + 6
        pad = mix[:, 0:2 * PADC].rearrange("p (b t) -> p b t", t=PADC)
        cv = mix[:, 2 * PADC:4 * PADC].rearrange("p (b t) -> p b t", t=PADC)
        dtw = mix[0:32, 4 * PADC:4 * PADC + 5 * T].rearrange("p (b t) -> p b t", t=T)
        st = mix[:, 0:5120].rearrange("p (d k n) -> p d k n", d=2, k=5)
        xdt = mix[:, 5120:7168].rearrange("p (b d n) -> p b d n", b=2, d=2)
        xw = xdt[:, 0, :, :]
        rr = mix[:, 7168:9216].rearrange("p (b d n) -> p b d n", b=2, d=2)
        ee = mix[:, 9216:12288].rearrange("p (b n) -> p b n", b=2)
        mf = mix[:, 12288:13312].rearrange("p (b n) -> p b n", b=2)
        gg = mix[:, 13312:14848].rearrange("p (c d n) -> p c d n", c=NT, d=2)
        dtk = mix[:, 14848:15232].rearrange("p (k c h) -> p k c h", k=2, c=NT)
        dec = mix[:, 15232:15616]
        wdt = mix[:, 15616:15808].rearrange("p (d c h) -> p d c h", d=2, c=NT)
        dcb = dec[:, 192:384].rearrange("p (c h) -> p c h", c=NT)
        assert 4 * PADC + 5 * T <= 14848 and 15808 <= 21 * T

        const_in, x_in, rows_in = sem("const_in"), sem("x_in"), sem("rows_in")
        w_full = [sem(f"w_full{i}") for i in range(RING)]
        w_used = sem("w_used")
        eps_set = sem("eps_set")
        vec_t, vec_done, sc_done = sem("vec_t"), sem("vec_done"), sem("sc_done")
        xt_done, h_loaded = sem("xt_done"), sem("h_loaded")
        m_full = [sem("m_full0"), sem("m_full1")]
        m_used, m_split_hi, m_split_lo, m_mm = sem("m_used"), sem("m_split_hi"), sem("m_split_lo"), sem("m_mm")
        ones_set, mod_raw, mod_done = sem("ones_set"), sem("mod_raw"), sem("mod_done")
        n_sq, n_ss, n_ln, n_rs, n_t, n_u = (sem("n_" + s) for s in ("sq", "ss", "ln", "rs", "t", "u"))
        n_lo = sem("n_lo")
        w_split_hi, w_split_lo = sem("w_split_hi"), sem("w_split_lo")
        f_silu, f_prod, f_hi, f_lo = sem("f_silu"), sem("f_prod"), sem("f_hi"), sem("f_lo")
        o_res = sem("o_res")
        hn_sq, hn_raw, hn_ss, hn_ln, hn_rs, hn_n, hn_rp, hn_sin, hn_cos, hn_fin = (
            sem("hn_" + s) for s in ("sq", "raw", "ss", "ln", "rs", "n", "rp", "sin", "cos", "fin"))
        v_mm, v_done = sem("v_mm"), sem("v_done")
        at_sc, at_mk, at_m0, at_m1, at_nm, at_ex, at_sk, at_l, at_ri, at_pn, at_tr, at_pt, at_pv, at_o = (
            sem("at_" + s) for s in ("sc", "mk", "m0", "m1", "nm", "ex", "sk", "l", "ri", "pn", "tr", "pt", "pv", "o"))
        pj_ev = sem("pj_ev")
        cv_pad, cv_tap, cv_out, pad_zero = sem("cv_pad"), sem("cv_tap"), sem("cv_out"), sem("pad_zero")
        dt_abs, dt_exp, dt_ln, dt_dt, dt_da = (sem("dt_" + s) for s in ("abs", "exp", "ln", "dt", "da"))
        a_exp = sem("a_exp")
        tk_dt, tk_dtc, tk_x, tk_xc, tk_b, tk_bc = (sem("tk_" + s) for s in ("dt", "dtc", "x", "xc", "b", "bc"))
        dc_mm, dc_exp, dc_w = sem("dc_mm"), sem("dc_exp"), sem("dc_w")
        s_xw, s_mm, s_dec, s_st = sem("s_xw"), sem("s_mm"), sem("s_dec"), sem("s_st")
        g_mm, g_done = sem("g_mm"), sem("g_done")
        y_xdt, y_r, y_seg, y_exp, y_m, y_mm, y_out = (sem("y_" + s) for s in ("xdt", "r", "seg", "exp", "m", "mm", "out"))
        m_z, m_sq, m_ss, m_ln, m_rs, m_y = (sem("m_" + s) for s in ("z", "sq", "ss", "ln", "rs", "y"))
        out_t, out_c, out_st = sem("out_t"), sem("out_c"), sem("out_st")

        rk = lambda w: w.rearrange("(k p) n -> p k n", p=P)
        w_mod = [rk(a["w_mod"][l]) for l in range(2)]
        w_ffi = [rk(a[n][l]) for l in range(2) for n in ("w_ff1_in", "w_ff2_in")]
        w_ffo = [rk(a[n][l]) for l in range(2) for n in ("w_ff1_out", "w_ff2_out")]
        w_ine, w_oute = rk(a["w_in_e"][0]), rk(a["w_out_e"][0])
        w_qb, w_kvb = rk(a["w_qb"][0]), rk(a["w_kvb"][0])
        w_ino, w_outo = rk(a["w_in_o"][0]), rk(a["w_out_o"][0])

        def slot(s, k, m=P):
            return ring[:, s * SLOT:s * SLOT + k * m].rearrange("p (k m) -> p k m", m=m)

        class Filler:

            def __init__(self, sp):
                self.sp, self.n = sp, 0

            def put(self, parts, i=None, per=0, c=0):
                s = (self.n + c) % RING
                if i is None:
                    if self.n >= RING:
                        self.sp.wait_ge(w_used, self.n - RING + 1)
                else:
                    v = i * per + (self.n + c - RING + 1)
                    if not isinstance(v, int) or v > 0:
                        self.sp.wait_ge(w_used, v)
                for dst, src in parts(s):
                    self.sp.dma_start(dst, src).then_inc(w_full[s], 16)
                if i is None:
                    self.n += 1

        class Drainer:

            def __init__(self, eng):
                self.eng, self.n, self.landed = eng, 0, [0] * RING

            def get(self, i=None, per=0, c=0, parts=1):
                s = (self.n + c) % RING
                if i is None:
                    self.landed[s] += parts
                    self.n += 1
                    self.eng.wait_ge(w_full[s], 16 * self.landed[s])
                else:
                    self.eng.wait_ge(w_full[s], i * (16 * per // RING) + 16 * (self.landed[s] + c // RING + 1))
                return s

            def passed(self, count):
                for _ in range(count):
                    self.landed[self.n % RING] += 1
                    self.n += 1

            def passed_items(self, m0, m1):
                for it in items[m0:m1]:
                    self.landed[self.n % RING] += 2 if it["kind"] in ("qr", "gq") else 1
                    self.n += 1

            def passed_v(self, parts):
                for _ in range(2):
                    self.landed[self.n % RING] += parts
                    self.n += 1

        def block(w, k0, k, c0, m=P):
            return lambda s: [(slot(s, k, m), w[:, k0:k0 + k, bass.ds(c0, m)])]

        OUT = [(w_oute, 8, 8, T, 1, qn), (w_oute, 0, 8, T, 1, xs), (w_outo, 0, 8, SEQ, 4, go)]
        FF_NORM = [0, 2, 3, 5]
        FF_T = [T, T, T, SEQ]
        PARTS = range(len(PART))
        for i_f in range(4):
            for part in PARTS:
                OUT.append((w_ffo[i_f], sum(PART[:part]), PART[part], FF_T[i_f], FF_NORM[i_f], (i_f, part)))
        R_MLA, R_SSD, R_GQA = 0, 1, 2
        R_FF = lambda i_f, part: 3 + len(PART) * i_f + part
        RUN = ([R_FF(0, x) for x in PARTS] + [R_MLA, R_SSD] + [R_FF(1, x) for x in PARTS]
               + [R_FF(2, x) for x in PARTS] + [R_GQA] + [R_FF(3, x) for x in PARTS])
        RES = {r: DB * i for i, r in enumerate(RUN)}
        MODS = {(0, 0): 1, (0, 1): 2, (1, 0): 3, (2, 0): 4, (2, 1): 5}

        def sync_out(f, r):
            w, k0, nk = OUT[r][:3]
            with f.sp.Fori(1, DB // RING + 1) as i:
                for dd in range(-RING, 0):
                    f.put(block(w, k0, nk, i * (RING * P) + dd * P), i, RING, dd)
            f.n += DB

        BASE, SPLIT = {}, {}
        n_ = m_ = 0

        def ff_names(i_f):
            return [x for part in PARTS for x in (("ffi", i_f, part), ("out", R_FF(i_f, part)))]

        for name, count in [(x, 0) for x in ff_names(0)] + [
                ("even", n_even), ("v_e", 2), (("out", R_MLA), 0), ("proj", 21), (("out", R_SSD), 0)] + [
                (x, 0) for x in ff_names(1) + ff_names(2)] + [
                ("odd", len(items) - n_even), ("v_o", 2), (("out", R_GQA), 0)] + [(x, 0) for x in ff_names(3)]:
            BASE[name], SPLIT[name] = n_, m_
            if name[0] == "ffi":
                count = 2 * PART[name[2]]
                m_ += count
            if name[0] == "out":
                count = DB
                m_ += 0 if name[1] < 3 else DB
            n_ += count
        FH = {(i_f, part): FB * i_f + sum(PART[:part]) for i_f in range(4) for part in PARTS}

        def act_split(act, s, m, cols, i=None, per=0):
            act.copy(w_hi[:, (m % 2) * SLOT:(m % 2) * SLOT + cols], ring[:, s * SLOT:s * SLOT + cols]).then_inc(w_split_hi, 1)

        def dve_split(dve, s, m, cols, i=None, per=0):
            if i is None:
                dve.wait_ge(w_split_hi, m + 1)
            else:
                dve.wait_ge(w_split_hi, i * per + (m + 1))
            b = (m % 2) * SLOT
            dve.tensor_tensor(w_lo[:, b:b + cols], ring[:, s * SLOT:s * SLOT + cols], w_hi[:, b:b + cols],
                              ALU.subtract).then_inc(w_split_lo, 1)

        def three_products(pe, p, m, k, hi, lo, t, start, stop):
            wh, wl = (w[:, (m % 2) * SLOT + P * k:(m % 2) * SLOT + P * k + P] for w in (w_hi, w_lo))
            cs = [(c0, min(t, c0 + 512)) for c0 in range(0, t, 512)]
            for n, (w, x) in enumerate(((wh, hi), (wh, lo), (wl, hi))):
                for c0, c1 in cs:
                    mm = pe.matmul(pair(p)[:, c0:c1], w, x[:, c0:c1], start=start and n == 0, stop=stop and n == 2)
            return mm

        def mod_group(g):
            return mod[:, 48 * g:48 * g + 48].rearrange("p (q d s) -> p q d s", q=3, d=8)

        def bmod(g):
            v = va if g < 3 else vb
            return v[:, g % 3 * 24:g % 3 * 24 + 24].rearrange("p (q d) -> p q d", q=3)

        NORM_T = [T, T, T, T, T, SEQ]
        NORM_AFTER = [None, R_FF(0, 2), R_SSD, R_FF(1, 2), R_FF(2, 2), R_GQA]

        def h_ready(eng, n, d):
            if n == 0:
                eng.wait_ge(h_loaded, d + 1)
            else:
                eng.wait_ge(o_res, RES[NORM_AFTER[n]] + d + 1)

        def act_rstd(act, n):
            t = NORM_T[n]
            for d in range(DB):
                h_ready(act, n, d)
                if n or d >= 2:
                    if 8 * n + d - 1 > 0:
                        act.wait_ge(n_ss, 8 * n + d - 1)
                act.activation(sqn[:, d % 2, :t], h[:, d, :t], ACT.Square).then_inc(n_sq, 1)
            act.wait_ge(n_ss, 8 * n + 8)
            if n == 0:
                act.wait_ge(eps_set, 1)
            act.activation(rsn[:, :t], pair(3, t), ACT.Ln, bias=eps, scale=1.0 / D).then_inc(n_ln, 1)
            act.wait_ge(n_ln, n + 1)
            act.activation(rsn[:, :t], rsn[:, :t], ACT.Exp, scale=-0.5).then_inc(n_rs, 1)

        def act_norm(act, n):
            act_rstd(act, n)
            act_shift(act, n)

        def act_shift(act, n):
            t = NORM_T[n]
            for d in range(DB):
                act.wait_ge(n_t, 8 * n + d + 1)
                src, dst = (hid_f[:, d % 2], u_hi[:, d]) if n in FF_NORM else (u[:, d], u[:, d])
                for t0, t1, s in SEGS:
                    if t0 < t:
                        x = act.activation(dst[:, t0:t1], src[:, t0:t1], ACT.Identity,
                                           bias=mod_group(n)[:, 0, d, s:s + 1])
                x.then_inc(n_u, 1)

        def pe_norm(pe, n):
            t = NORM_T[n]
            if n == 0:
                pe.wait_ge(const_in, 16)
            for d in range(DB):
                pe.wait_ge(n_sq, 8 * n + d + 1)
                for c0 in range(0, t, 512):
                    c1 = min(t, c0 + 512)
                    mm = pe.matmul(pair(3)[:, c0:c1], ones, sqn[:, d % 2, c0:c1], start=d == 0, stop=d == DB - 1)
                mm.then_inc(n_ss, 1)

        def dve_norm(dve, n):
            t = NORM_T[n]
            dve.wait_ge(n_rs, n + 1)
            dve.wait_ge(mod_done, n + 1)
            for q in range(DB + 1):
                if q < DB:
                    h_ready(dve, n, q)
                    dst = hid_f[:, q % 2] if n in FF_NORM else u[:, q]
                    if n in FF_NORM and q >= 2:
                        dve.wait_ge(n_lo, 8 * FF_NORM.index(n) + q - 1)
                    for t0, t1, s in SEGS:
                        if t0 < t:
                            x = dve.scalar_tensor_tensor(out=dst[:, t0:t1], in0=h[:, q, t0:t1],
                                                         scalar=mod_group(n)[:, 1, q, s:s + 1],
                                                         in1=rsn[:, t0:t1], op0=ALU.mult, op1=ALU.mult)
                    x.then_inc(n_t, 1)
                d = q - 1
                if d >= 0 and n in FF_NORM:
                    dve.wait_ge(n_u, 8 * n + d + 1)
                    for t0, t1, s in SEGS:
                        if t0 < t:
                            x = dve.scalar_tensor_tensor(out=u_lo[:, d, t0:t1], in0=hid_f[:, d % 2, t0:t1],
                                                         scalar=mod_group(n)[:, 0, d, s:s + 1],
                                                         in1=u_hi[:, d, t0:t1], op0=ALU.add, op1=ALU.subtract)
                    x.then_inc(n_lo, 1)

        def pool_mod(pool, g):
            if g in (1, 3, 4):
                pool.wait_ge(n_t, 8 * ({1: 0, 3: 2, 4: 3}[g] + 1))
            for k in range(DB):
                for q in range(3):
                    n = 24 * g + 3 * k + q
                    if n % 24 >= 2:
                        pool.wait_ge(m_used, n - 1)
                    elif g > 0:
                        pool.wait_ge(m_mm, 3 * g)
                    pool.dma_start(m_in[g > 0][:, D * (n % 2):D * (n % 2) + D],
                                   w_mod[g // 3][:, k, (g % 3 * 3 + q) * D:(g % 3 * 3 + q + 1) * D]).then_inc(m_full[n % 2], 16)

        def dve_mod_sum(dve, g, k, q):
            n = 24 * g + 3 * k + q
            if n == 0:
                dve.wait_ge(sc_done, 1)
            if k:
                dve.wait_ge(m_used, n - 2)
            elif g:
                dve.wait_ge(m_mm, 3 * g)
            dve.wait_ge(m_full[n % 2], 16 * (n // 2 + 1))
            w = m_in[g > 0][:, D * (n % 2):D * (n % 2) + D]
            for s in range(2):
                at_, by = m_sum[:, D * (2 * q + s):D * (2 * q + s) + D], sc[:, 2 * k + s:2 * k + s + 1]
                if k:
                    x = dve.scalar_tensor_tensor(out=at_, in0=w, scalar=by, in1=at_, op0=ALU.mult, op1=ALU.add)
                else:
                    x = dve.tensor_scalar(at_, w, by, None, ALU.mult)
            x.then_inc(m_used, 1)

        def act_mod_hi(act, g, q):
            if q == 0:
                act.wait_ge(m_used, 24 * g + 24)
            else:
                act.wait_ge(m_mm, 3 * g + q)
            act.copy(m_hi[g > 0][:, :], m_sum[:, 2 * D * q:2 * D * q + 2 * D]).then_inc(m_split_hi, 1)

        def dve_mod_lo(dve, g, q):
            dve.wait_ge(m_split_hi, 3 * g + q + 1)
            dve.tensor_tensor(m_lo[:, 2 * D * q:2 * D * q + 2 * D], m_sum[:, 2 * D * q:2 * D * q + 2 * D],
                              m_hi[g > 0][:, :], ALU.subtract).then_inc(m_split_lo, 1)

        def pe_mod(pe, g, q):
            pe.wait_ge(m_split_lo, 3 * g + q + 1)
            for d in range(DB):
                for s in range(2):
                    at_ = bank(4, 2 * (16 * q + 2 * d + s), 2 * (16 * q + 2 * d + s) + 2)
                    c0 = D * s + P * d
                    pe.matmul(at_, m_hi[g > 0][:, c0:c0 + P], ones_r[:, :], start=True, stop=False)
                    mm = pe.matmul(at_, m_lo[:, 2 * D * q + c0:2 * D * q + c0 + P], ones_r[:, :], start=False, stop=True)
            mm.then_inc(m_mm, 1)

        def dve_mod(dve, g):
            dve.wait_ge(m_mm, 3 * g + 3)
            raw = bank(4, 0, 96).rearrange("p (q d s o) -> p q d s o", q=3, d=8, s=2)
            m = mod_group(g)
            for q in range(3):
                for s in range(2):
                    x = dve.scalar_tensor_tensor(out=m[:, q, :, s], in0=raw[:, q, :, s, 0],
                                                 scalar=1.0 if q == 1 else 0.0, in1=bmod(g)[:, q, :],
                                                 op0=ALU.add, op1=ALU.add)
            x.then_inc(mod_raw, 1)
            dve.wait_ge(mod_raw, g + 1)
            dve.tensor_scalar(m[:, 2, :, :], m[:, 2, :, :], 1.0 if g % 3 == 1 else 0.5, None,
                              ALU.mult).then_inc(mod_done, 1)

        def sync_ffi(f, i_f, part):
            def body(i):
                for jj in range(2):
                    for up in range(2):
                        col = up * FFN + (sum(PART[:part]) + jj) * P
                        f.put(block(w_ffi[i_f], 0, 8, i * (2 * P) + col), i, 4, 2 * jj + up)

            body(0)
            with f.sp.Fori(1, PART[part] // 2) as i:
                body(i)
            f.n += 2 * PART[part]

        def pe_ffi(pe, dr, i_f, part):
            t, b, m = FF_T[i_f], FH[i_f, part], SPLIT["ffi", i_f, part]
            if part:
                pe.wait_ge(o_res, RES[R_FF(i_f, part - 1)] + DB)

            def body(i):
                for jj in range(2):
                    for up, sem_ in ((0, f_silu), (1, f_prod)):
                        v = b + jj - 1
                        if not isinstance(i, int):
                            pe.wait_ge(sem_, i * 2 + v)
                        elif v > 0:
                            pe.wait_ge(sem_, v)
                        mm_ = m + 2 * jj + up
                        pe.wait_ge(w_split_lo, i * 4 + (mm_ + 1))
                        for k in range(DB):
                            if isinstance(i, int) and jj == 0 and up == 0 and part == 0:
                                pe.wait_ge(n_lo, 8 * i_f + k + 1)
                            mm = three_products(pe, 2 * up + jj, mm_, k, u_hi[:, k], u_lo[:, k], t, k == 0, k == DB - 1)
                        mm.then_inc(w_used, 1)

            body(0)
            with pe.Fori(1, PART[part] // 2) as i:
                body(i)
            dr.passed(2 * PART[part])

        def act_ffi(act, ar, i_f, part):
            t, n, m, b = FF_T[i_f], BASE["ffi", i_f, part], SPLIT["ffi", i_f, part], FH[i_f, part]

            def body(i):
                for jj in range(2):
                    for up in range(2):
                        c = 2 * jj + up
                        s = ar.get(i, 4, c)
                        v = i * 4 + (n + c - 1)
                        if not isinstance(v, int) or v > 0:
                            act.wait_ge(w_used, v)
                        act_split(act, s, m + c, SLOT)
                    if not isinstance(i, int) or jj:
                        round_hidden(act, i * 2 + (jj - 1), 1 - jj, i * 2 + (b + jj), t)
                    act.wait_ge(w_used, i * 4 + (n + 2 * jj + 1))
                    v = b + jj - 1
                    if not isinstance(i, int):
                        act.wait_ge(f_lo, i * 2 + v)
                    elif v > 0:
                        act.wait_ge(f_lo, v)
                    act.activation(hid_f[:, jj, :t], pair(jj, t), ACT.Silu).then_inc(f_silu, 1)

            body(0)
            with act.Fori(1, PART[part] // 2) as i:
                body(i)
            ar.passed(2 * PART[part])

        def round_hidden(act, j, q, done, t):
            act.wait_ge(f_prod, done)
            dst = hid_hi[:, j:j + 1, :t] if isinstance(j, int) else hid_hi[:, bass.ds(j, 1), :t]
            act.copy(dst, hid_f[:, q:q + 1, :t]).then_inc(f_hi, 1)

        def dve_ffi(dve, dv, i_f, part):
            mods = MODS.get((i_f, part))
            t, n, m, b = FF_T[i_f], BASE["ffi", i_f, part], SPLIT["ffi", i_f, part], FH[i_f, part]

            def body(i):
                for jj in range(2):
                    s = (dv.n + 2 * jj) % RING
                    dve_split(dve, s, m + 2 * jj, SLOT, i, 4)
                    j = i * 2 + (jj - 1)
                    if not isinstance(j, int) or j >= 0:
                        dve.wait_ge(w_used, i * 4 + (n + 2 * jj))
                        dve.wait_ge(f_silu, i * 2 + (b + jj))
                        q = 1 - jj
                        dve.tensor_tensor(hid_f[:, q, :t], hid_f[:, q, :t], pair(2 + q, t), ALU.mult).then_inc(f_prod, 1)
                    if mods is not None:
                        dve_mod_sum(dve, mods, 2 * i + jj, 0)
                    s = (dv.n + 2 * jj + 1) % RING
                    dve_split(dve, s, m + 2 * jj + 1, SLOT, i, 4)
                    if mods is not None:
                        dve_mod_sum(dve, mods, 2 * i + jj, 1)
                    if not isinstance(j, int) or j >= 0:
                        dve.wait_ge(f_hi, i * 2 + (b + jj))
                        d = (lambda x: x[:, j:j + 1, :t] if isinstance(j, int) else x[:, bass.ds(j, 1), :t])
                        dve.tensor_tensor(d(hid_lo), hid_f[:, q:q + 1, :t], d(hid_hi), ALU.subtract).then_inc(f_lo, 1)
                    if mods is not None:
                        dve_mod_sum(dve, mods, 2 * i + jj, 2)

            if mods is not None:
                for i in range(PART[part] // 2):
                    body(i)
            else:
                body(0)
                with dve.Fori(1, PART[part] // 2) as i:
                    body(i)
            dv.n += 2 * PART[part]

        def act_out_ff(act, ar, r):
            w, k0, nk, t, g, (i_f, part) = OUT[r]
            for d in range(DB):
                s = ar.get()
                act.wait_ge(w_used, BASE["out", r] + d - 1)
                act_split(act, s, SPLIT["out", r] + d, P * nk)
                if d == 1:
                    round_hidden(act, nk - 1, (nk - 1) % 2, FH[i_f, part] + nk, t)
                if (i_f, part) in MODS and 1 <= d <= 3:
                    act_mod_hi(act, MODS[i_f, part], d - 1)

        def dve_out_ff(dve, dv, r):
            w, k0, nk, t, g, (i_f, part) = OUT[r]
            b, q = BASE["out", r], (nk - 1) % 2
            for x in range(DB + 2):
                if x < DB:
                    dve_split(dve, dv.n % RING, SPLIT["out", r] + x, P * nk)
                    dv.n += 1
                if x == 0:
                    dve.wait_ge(w_used, b)
                    dve.wait_ge(f_silu, FH[i_f, part] + nk)
                    dve.tensor_tensor(hid_f[:, q, :t], hid_f[:, q, :t], pair(2 + q, t), ALU.mult).then_inc(f_prod, 1)
                if x == 1:
                    dve.wait_ge(f_hi, FH[i_f, part] + nk)
                    dve.tensor_tensor(hid_lo[:, nk - 1, :t], hid_f[:, q, :t], hid_hi[:, nk - 1, :t],
                                      ALU.subtract).then_inc(f_lo, 1)
                if x >= 2:
                    dve_residual(dve, r, x - 2)
                if (i_f, part) in MODS:
                    if 1 <= x <= 3:
                        dve_mod_lo(dve, MODS[i_f, part], x - 1)
                    if x == 6:
                        dve_mod(dve, MODS[i_f, part])

        def pe_out(pe, dr, r):
            w, k0, nk, t, g, src = OUT[r]
            ff = r >= 3
            if ff:
                pe.wait_ge(f_lo, FH[src] + nk - 1)
            mods = MODS.get(src) if ff else None

            def body(i, first_round):
                for dd in range(RING):
                    v = i * RING + (RES[r] + dd - 1)
                    if not isinstance(v, int) or v > 0:
                        pe.wait_ge(o_res, v)
                    if ff:
                        m = SPLIT["out", r] + dd
                        pe.wait_ge(w_split_lo, i * RING + (m + 1))
                    else:
                        s = dr.get(i, RING, dd)
                    for k in range(nk):
                        first, last = k == 0, k == nk - 1
                        if ff:
                            if first_round and dd == 0 and last:
                                pe.wait_ge(f_lo, FH[src] + nk)
                            mm = three_products(pe, dd % 2, m, k, hid_hi[:, k], hid_lo[:, k], t, first, last)
                            continue
                        for c0 in range(0, t, 512):
                            c1 = min(t, c0 + 512)
                            mm = pe.matmul(pair(dd % 2)[:, c0:c1], slot(s, nk)[:, k, :],
                                           src[:, k, c0:c1], start=first, stop=last)
                    mm.then_inc(w_used, 1)
                    if mods is not None and 2 <= i * RING + dd <= 4:
                        pe_mod(pe, mods, i * RING + dd - 2)

            for i in range(DB // RING):
                body(i, i == 0)
            dr.passed(DB)

        def dve_residual(dve, r, d):
            t, g = OUT[r][3:5]
            dve.wait_ge(w_used, BASE["out", r] + d + 1)
            for t0, t1, s in SEGS:
                if t0 < t:
                    x = dve.scalar_tensor_tensor(out=h[:, d, t0:t1], in0=pair(d % 2)[:, t0:t1],
                                                 scalar=mod_group(g)[:, 2, d, s:s + 1],
                                                 in1=h[:, d, t0:t1], op0=ALU.mult, op1=ALU.add)
            x.then_inc(o_res, 1)

        def dve_out(dve, r):
            for d in range(DB):
                dve_residual(dve, r, d)

        GAIN = {"qn": VB_QN, "kn": VB_KN, "qr": VB_QR, "kr": VB_KR, "gq": VB_GQ, "gk": VB_GK}
        WIDTH = {"qa": 384, "ckv": 256, "kr": 64, "qn": 128, "kn": 128, "qr": 64, "gk": 64, "gq": 64}
        DST = {"qa": qa, "ckv": ckv, "qn": qn, "kn": kn, "qr": qr, "gk": gk, "gq": gq}

        def dst_of(it):
            return kr if it["kind"] == "kr" else DST[it["kind"]][:, it["i"], :]

        def gain_of(it):
            k = {"qa": VB_QA + it["i"], "ckv": VB_KV + it["i"]}.get(it["kind"], GAIN.get(it["kind"]))
            return vb[:, k:k + 1]

        def item_chunk(it):
            kind, i = it["kind"], it["i"]
            if kind == "qa":
                return block(w_ine, 0, 8, QA0 + P * i)
            if kind == "ckv":
                return block(w_ine, 0, 8, CKV0 + P * i)
            if kind == "kr":
                return None
            if kind == "qn":
                return block(w_qb, 0, 3, i * (DN + DR))
            if kind == "kn":
                return block(w_kvb, 0, 2, i * (DN + DV))
            if kind == "gk":
                return block(w_ino, 0, 8, QH * HD + P * i)
            if kind == "qr":
                c0 = 2 * i * (DN + DR) + DN
                return lambda s: [(slot(s, 3)[:, :, 64 * e:64 * e + 64],
                                   w_qb[:, :, c0 + e * (DN + DR):c0 + e * (DN + DR) + 64]) for e in range(2)]
            c0 = HD * (8 * (i // 4) + i % 4)
            return lambda s: [(slot(s, 8)[:, :, 64 * e:64 * e + 64],
                               w_ino[:, :, c0 + 4 * HD * e:c0 + 4 * HD * e + 64]) for e in range(2)]

        def item_in(it):
            return {"qn": (3, qa), "qr": (3, qa), "kn": (2, ckv)}.get(it["kind"], (8, u))

        def sync_items(f, m0, m1):
            for m in range(m0, m1):
                it = items[m]
                if it["kind"] == "kr":
                    src = w_ine[:, :, KR0:KR0 + DR]
                    s = f.n % RING
                    f.sp.wait_ge(w_used, f.n - RING + 1)
                    f.sp.dma_start(slot(s, 8)[:, :, 0:64], src).then_inc(w_full[s], 16)
                    f.n += 1
                else:
                    f.put(item_chunk(it))

        def pe_items(pe, dr, m0, m1, norm_n):
            for q in range(m0, m1 + 2):
                if q < m1:
                    it = items[q]
                    nk, src = item_in(it)
                    if q - m0 >= 2:
                        pe.wait_ge(hn_raw, q - 1)
                    if q == m0:
                        pe.wait_ge(n_u, 8 * norm_n + 8)
                    if it["kind"] in ("qn", "qr", "kn"):
                        pe.wait_ge(hn_n, 2 if it["kind"] == "kn" else 1)
                    s = dr.get(parts=2 if it["kind"] in ("qr", "gq") else 1)
                    for k in range(nk):
                        for c0 in range(0, it["t"], 512):
                            c1 = min(it["t"], c0 + 512)
                            if it["kind"] == "kr":
                                for e in range(2):
                                    mm = pe.matmul(pair(q % 2)[64 * e:64 * e + 64, c0:c1], slot(s, 8)[:, k, 0:64],
                                                   src[:, k, c0:c1], start=k == 0, stop=k == nk - 1)
                            else:
                                mm = pe.matmul(pair(q % 2)[:, c0:c1], slot(s, nk)[:, k, :], src[:, k, c0:c1],
                                               start=k == 0, stop=k == nk - 1)
                    mm.then_inc(w_used, 1)
                m = q - 1
                if m0 <= m < m1:
                    it = items[m]
                    pe.wait_ge(hn_sq, m + 1)
                    if it["start"] and it["norm"] > 0:
                        pe.wait_ge(hn_ln, it["norm"])
                    w = blk64 if WIDTH[it["kind"]] == 64 else ones
                    for c0 in range(0, it["t"], 512):
                        c1 = min(it["t"], c0 + 512)
                        mm = pe.matmul(pair(2)[:, c0:c1], w, sqh[:, m % 2, c0:c1], start=it["start"], stop=it["stop"])
                    mm.then_inc(hn_ss, 1)
                m = q - 2
                if m0 <= m < m1 and items[m]["rope"]:
                    it = items[m]
                    pe.wait_ge(hn_n, it["norm"] + 1)
                    if it["nrope"] > 0:
                        pe.wait_ge(hn_sin, it["nrope"])
                    pe.matmul(bank(6), c_(C_SW), dst_of(it)[:, 0:SEQ], start=True, stop=True).then_inc(hn_rp, 1)

        def act_items(act, m0, m1, base):
            for q in range(m0, m1 + 1):
                if q < m1:
                    it = items[q]
                    t = it["t"]
                    act.wait_ge(w_used, base + q - m0 + 1)
                    if q >= 2:
                        act.wait_ge(hn_ss, q - 1)
                    act.activation(sqh[:, q % 2, :t], pair(q % 2, t), ACT.Square).then_inc(hn_sq, 1)
                    act.activation(dst_of(it)[:, :t], pair(q % 2, t), ACT.Identity,
                                   scale=gain_of(it)).then_inc(hn_raw, 1)
                m = q - 1
                if m0 <= m and items[m]["stop"]:
                    it = items[m]
                    t, nn = it["t"], it["norm"]
                    act.wait_ge(hn_ss, m + 1)
                    if nn >= 2:
                        act.wait_ge(hn_n, nn - 1)
                        last = [x for x in items if x["stop"]][nn - 2]
                        if last["rope"]:
                            act.wait_ge(hn_fin, last["nrope"] + 1)
                    act.activation(rsh[:, nn % 2, :t], pair(2, t), ACT.Ln, bias=eps,
                                   scale=1.0 / WIDTH[it["kind"]]).then_inc(hn_ln, 1)
                    act.wait_ge(hn_ln, nn + 1)
                    act.activation(rsh[:, nn % 2, :t], rsh[:, nn % 2, :t], ACT.Exp, scale=-0.5).then_inc(hn_rs, 1)

        def dve_items(dve, m0, m1):
            for m in range(m0, m1):
                it = items[m]
                if not it["stop"]:
                    continue
                t, nn, kind = it["t"], it["norm"], it["kind"]
                dve.wait_ge(hn_rs, nn + 1)
                dve.wait_ge(hn_raw, m + 1)
                for i in range(it["i"] + 1 if kind in ("qa", "ckv") else 1):
                    d = DST[kind][:, i, :t] if kind in ("qa", "ckv") else dst_of(it)[:, :t]
                    x = dve.tensor_tensor(d, d, rsh[:, nn % 2, :t], ALU.mult)
                x.then_inc(hn_n, 1)
                if it["rope"]:
                    d, nr = dst_of(it)[:, 0:SEQ], it["nrope"]
                    tmp = rsh[:, nn % 2, 0:SEQ]
                    dve.wait_ge(hn_rp, nr + 1)
                    dve.tensor_tensor(tmp, cst[:, C_SIN:C_SIN + SEQ], bank(6), ALU.mult).then_inc(hn_sin, 1)
                    dve.tensor_tensor(d, d, cst[:, C_COS:C_COS + SEQ], ALU.mult).then_inc(hn_cos, 1)
                    dve.wait_ge(hn_sin, nr + 1)
                    dve.wait_ge(hn_cos, nr + 1)
                    dve.tensor_tensor(d, d, tmp, ALU.add).then_inc(hn_fin, 1)

        def sync_v(f, which):
            for half in range(2):
                if which == "e":
                    src = w_kvb.rearrange("p k (h n) -> p k h n", n=DN + DV)[:, :, 4 * half:4 * half + 4, DN:DN + DV]
                    f.put(lambda s, src=src: [(slot(s, 2, 512)[:, k, :].rearrange("p (h n) -> p h n", n=DV),
                                               src[:, k]) for k in range(2)])
                else:
                    f.put(block(w_ino, 0, 8, (QH + KVH) * HD + P * half))

        def pe_v(pe, dr, which):
            nk, m, src = (2, 512, ckv) if which == "e" else (8, P, u)
            off = 0 if which == "e" else 12
            for half in range(2):
                s = dr.get(parts=2 if which == "e" else 1)
                for n in range(NT):
                    q = half * NT + n
                    if q >= 4:
                        pe.wait_ge(v_done, off + q - 3)
                    elif q == 0:
                        pe.wait_ge(hn_raw, n_even if which == "e" else len(items))
                    for k in range(nk):
                        mm = pe.matmul(bank(q % 4, 0, m), src[:, k, P * n:P * n + P], slot(s, nk, m)[:, k, :],
                                       start=k == 0, stop=k == nk - 1)
                    mm.then_inc(w_used if n == NT - 1 else v_mm, 1)

        def dve_v(dve, which):
            m, dst, base = (512, vt, BASE["v_e"]) if which == "e" else (P, gv, BASE["v_o"])
            off = 0 if which == "e" else 10
            for half in range(2):
                for n in range(NT):
                    if n < NT - 1:
                        dve.wait_ge(v_mm, off + 5 * half + n + 1)
                    else:
                        dve.wait_ge(w_used, base + half + 1)
                    dve.tensor_copy(dst[:, n, m * half:m * half + m], bank((half * NT + n) % 4, 0, m)).then_inc(v_done, 1)

        units = []
        for hh in range(MH):
            e = 64 * (hh % 2)
            for qt in range(NT):
                q0 = P * qt
                keys = [(0, SEQ), (SEQ, T)] if qt < 4 else [(SEQ, T)]
                sco = []
                at = 0
                for k0, k1 in keys:
                    sco.append((qn[:, hh, q0:q0 + P], kn[:, hh, k0:k1], at, True, False))
                    sco.append((qr[e:e + 64, hh // 2, q0:q0 + P], kr[e:e + 64, k0:k1], at, False, True))
                    at += k1 - k0
                tiles = range(NT) if qt < 4 else range(4, NT)
                units.append(dict(sc=sco, n=at, masks=[], scale=(DN + DR) ** -0.5, sink=None, m=DV, o=0,
                                  v=[vt[:, k, DV * hh:DV * hh + DV] for k in tiles], out=qn[:, hh, q0:q0 + P]))
        n_mla = len(units)
        for hh in range(QH):
            b, e8, ii = hh // 8, (hh % 8) // 4, hh % 4
            e, g = 64 * e8, hh // 4
            for qt in range(SEQ // P):
                q0 = P * qt
                q = gq[e:e + 64, 4 * b + ii, q0:q0 + P]
                sco = [(q, gk[e:e + 64, b, SEQ:T], 0, True, True)]
                tiles = [4, 5]
                masks = []
                lo, hi = max(0, qt - 1), min(3, qt + 1)
                if qt > 0:
                    masks.append((256, c_(C_MP)))
                if qt < 3:
                    masks.append((256 + P * (qt + 1 - lo), c_(C_MN)))
                sco.append((q, gk[e:e + 64, b, P * lo:P * lo + 256], 256, True, True))
                if hi - lo == 2:
                    sco.append((q, gk[e:e + 64, b, P * hi:P * hi + P], 512, True, True))
                tiles += list(range(lo, hi + 1))
                units.append(dict(sc=sco, n=P * len(tiles), masks=masks, scale=HD ** -0.5,
                                  sink=sink[:, hh:hh + 1], m=HD, o=64 * (hh % 2),
                                  v=[gv[:, k, HD * g:HD * g + HD] for k in tiles],
                                  out=go[64 * (hh % 2):64 * (hh % 2) + 64, hh // 2, q0:q0 + P]))
        n_mask = n_sink = 0
        for x in units:
            x["nmask"], x["nsink"] = n_mask, n_sink
            n_mask += len(x["masks"])
            n_sink += x["sink"] is not None

        def pe_attend(pe, u0, u1):
            for q in range(u0, u1 + 3):
                if q < u1:
                    x = units[q]
                    if q - u0 >= 2:
                        pe.wait_ge(at_ex, q - 1)
                    for lhs, rhs, c0, start, stop in x["sc"]:
                        mm = pe.matmul(pair(q % 2, 1024)[:, c0:c0 + rhs.shape[-1]], lhs, rhs, start=start, stop=stop)
                    mm.then_inc(at_sc, 1)
                i = q - 2
                if u0 <= i < u1:
                    pe.wait_ge(at_pn, i + 1)
                    if i > u0:
                        pe.wait_ge(at_pt, i)
                    nb = units[i]["n"] // P
                    for k in range(nb):
                        mm = pe.transpose(pair(2)[:, P * k:P * k + P], prob[:, i % 3, P * k:P * k + P], ident)
                    mm.then_inc(at_tr, 1)
                i = q - 3
                if u0 <= i < u1:
                    x = units[i]
                    pe.wait_ge(at_pt, i + 1)
                    if i - u0 >= 2:
                        pe.wait_ge(at_o, i - 1)
                    for k, v in enumerate(x["v"]):
                        mm = pe.matmul(bank(6 + i % 2)[x["o"]:x["o"] + x["m"], 0:P], v, probT[:, i % 2, P * k:P * k + P],
                                       start=k == 0, stop=k == len(x["v"]) - 1)
                    mm.then_inc(at_pv, 1)

        def act_attend(act, u0, u1):
            for q in range(u0, u1 + 2):
                if q < u1:
                    x = units[q]
                    act.wait_ge(at_nm, q + 1)
                    if q >= 3:
                        act.wait_ge(at_tr, q - 2)
                    act.activation(prob[:, q % 3, :x["n"]], pair(q % 2, 1024)[:, :x["n"]], ACT.Exp,
                                   bias=stat[:, 4 + q % 4:5 + q % 4], scale=x["scale"],
                                   accum_out=stat[:, 8 + q % 4:9 + q % 4]).then_inc(at_ex, 1)
                    if x["sink"] is not None:
                        act.activation(stat[:, 12 + q % 4:13 + q % 4], x["sink"], ACT.Exp,
                                       bias=stat[:, 4 + q % 4:5 + q % 4]).then_inc(at_sk, 1)
                i = q - 2
                if u0 <= i:
                    act.wait_ge(at_tr, i + 1)
                    if i >= 2:
                        act.wait_ge(at_pv, i - 1)
                    n = units[i]["n"]
                    act.copy(probT[:, i % 2, :n], pair(2, n)).then_inc(at_pt, 1)

        def dve_attend(dve, u0, u1):
            for q in range(u0, u1 + 3):
                if q < u1:
                    x = units[q]
                    dve.wait_ge(at_sc, q + 1)
                    s = pair(q % 2, 1024)
                    for c0, mk in x["masks"]:
                        dve.tensor_tensor(s[:, c0:c0 + P], mk, s[:, c0:c0 + P], ALU.add).then_inc(at_mk, 1)
                    if x["masks"]:
                        dve.wait_ge(at_mk, x["nmask"] + len(x["masks"]))
                    m = stat[:, q % 4:q % 4 + 1]
                    dve.tensor_reduce(m, s[:, :x["n"]], AX, ALU.max).then_inc(at_m0, 1)
                    dve.wait_ge(at_m0, q + 1)
                    nm = stat[:, 4 + q % 4:5 + q % 4]
                    if x["sink"] is not None:
                        dve.tensor_scalar(m, m, x["scale"], x["sink"], ALU.mult, ALU.max).then_inc(at_m1, 1)
                        dve.wait_ge(at_m1, x["nsink"] + 1)
                        dve.tensor_scalar(nm, m, -1.0, None, ALU.mult).then_inc(at_nm, 1)
                    else:
                        dve.tensor_scalar(nm, m, -x["scale"], None, ALU.mult).then_inc(at_nm, 1)
                i = q - 1
                if u0 <= i < u1:
                    x = units[i]
                    ls = stat[:, 8 + i % 4:9 + i % 4]
                    dve.wait_ge(at_ex, i + 1)
                    if x["sink"] is not None:
                        dve.wait_ge(at_sk, x["nsink"] + 1)
                        dve.tensor_tensor(ls, ls, stat[:, 12 + i % 4:13 + i % 4], ALU.add).then_inc(at_l, 1)
                        dve.wait_ge(at_l, x["nsink"] + 1)
                    ri = stat[:, 16 + i % 4:17 + i % 4]
                    dve.reciprocal(ri, ls).then_inc(at_ri, 1)
                    dve.wait_ge(at_ri, i + 1)
                    dve.tensor_scalar(prob[:, i % 3, :x["n"]], prob[:, i % 3, :x["n"]], ri, None,
                                      ALU.mult).then_inc(at_pn, 1)
                i = q - 3
                if u0 <= i < u1:
                    x = units[i]
                    dve.wait_ge(at_pv, i + 1)
                    dve.tensor_copy(x["out"], bank(6 + i % 2)[x["o"]:x["o"] + x["m"], 0:P]).then_inc(at_o, 1)

        PJ = [("dt", 0)] + [("c", i) for i in range(12)] + [("z", i) for i in range(8)]

        def sync_proj(f):
            f.put(block(w_ine, 0, 8, DT0, 32))
            with f.sp.Fori(0, 3) as i:
                for c in range(4):
                    f.put(block(w_ine, 0, 8, i * 512 + (XBC0 + P * c)), i, 4, c)
            f.n += 12
            with f.sp.Fori(0, 2) as i:
                for c in range(4):
                    f.put(block(w_ine, 0, 8, i * 512 + (Z0 + P * c)), i, 4, c)
            f.n += 8

        def pe_proj(pe, dr):
            def product(q, m, s):
                for k in range(DB):
                    for c0 in range(0, T, 512):
                        c1 = min(T, c0 + 512)
                        mm = pe.matmul(pair(q % 4)[0:m, c0:c1], slot(s, 8, m)[:, k, :], u[:, k, c0:c1],
                                       start=k == 0, stop=k == DB - 1)
                mm.then_inc(w_used, 1)

            pe.wait_ge(o_res, RES[R_MLA] + 8)
            product(0, 32, dr.get())
            for q in range(1, 5):
                if q == 4:
                    pe.wait_ge(pj_ev, 1)
                product(q, P, dr.get())
            with pe.Fori(1, 5) as i:
                for c in range(4):
                    pe.wait_ge(pj_ev, i * 4 + (c - 2))
                    product(1 + c, P, dr.get(i - 1, 4, c))
            dr.passed(16)

        def act_proj(act):
            b = BASE["proj"]
            for q in range(len(PJ) + 1):
                if q < len(PJ):
                    kind, i = PJ[q]
                    act.wait_ge(w_used, b + q + 1)
                    if kind == "dt":
                        act.activation(dtw[:, 0, :], pair(0)[0:32, :], ACT.Identity, bias=dtb).then_inc(pj_ev, 1)
                    elif kind == "c":
                        if i == 0:
                            act.wait_ge(pad_zero, 1)
                        if i >= 2:
                            act.wait_ge(cv_tap, 5 * (i - 1))
                        act.copy(pad[:, i % 2, 2:2 + SEQ], pair(q % 4)[:, 0:SEQ]).then_inc(cv_pad, 1)
                        act.copy(pad[:, i % 2, 4 + SEQ:4 + T], pair(q % 4)[:, SEQ:T]).then_inc(pj_ev, 1)
                    else:
                        act.activation(z[:, i, :], pair(q % 4), ACT.Silu).then_inc(pj_ev, 1)
                if q >= 2 and PJ[q - 1][0] == "c":
                    i = PJ[q - 1][1]
                    act.wait_ge(cv_tap, 5 * (i + 1))
                    dst = xs[:, i, :] if i < 8 else bc[:, i - 8, :]
                    bias = vb[:, VB_CB + i:VB_CB + i + 1]
                    act.activation(dst[:, 0:SEQ], cv[:, i % 2, 0:SEQ], ACT.Silu, bias=bias)
                    act.activation(dst[:, SEQ:T], cv[:, i % 2, 2 + SEQ:2 + T], ACT.Silu, bias=bias).then_inc(cv_out, 1)
            act.wait_ge(pj_ev, 1)
            act.activation(dtw[:, 1, :], dtw[:, 0, :], ACT.Abs).then_inc(dt_abs, 1)
            act.wait_ge(dt_abs, 1)
            act.activation(dtw[:, 1, :], dtw[:, 1, :], ACT.Exp, scale=-1.0).then_inc(dt_exp, 1)
            act.wait_ge(dt_exp, 1)
            act.activation(dtw[:, 2, :], dtw[:, 1, :], ACT.Ln, bias=1.0).then_inc(dt_ln, 1)
            act.activation(aexp, alog, ACT.Exp).then_inc(a_exp, 1)

        def dve_proj(dve):
            dve.wait_ge(at_o, n_mla)
            dve.wait_ge(o_res, RES[R_MLA] + 8)
            for b in range(2):
                dve.memset(pad[:, b, 0:2], 0.0)
                dve.memset(pad[:, b, 2 + SEQ:4 + SEQ], 0.0)
                x = dve.memset(pad[:, b, 4 + T:6 + T], 0.0)
            x.then_inc(pad_zero, 1)
            dve.wait_ge(pad_zero, 1)
            n = T + 2
            for i in range(12):
                dve.wait_ge(cv_pad, i + 1)
                dve.wait_ge(pj_ev, i + 2)
                if i >= 2:
                    dve.wait_ge(cv_out, i - 1)
                y = cv[:, i % 2, 0:n]
                for tap in range(5):
                    w = vc[:, 12 * tap + i:12 * tap + i + 1]
                    if tap:
                        dve.wait_ge(cv_tap, 5 * i + tap)
                        dve.scalar_tensor_tensor(out=y, in0=pad[:, i % 2, tap:tap + n], scalar=w, in1=y,
                                                 op0=ALU.mult, op1=ALU.add).then_inc(cv_tap, 1)
                    else:
                        dve.tensor_scalar(y, pad[:, i % 2, 0:n], w, None, ALU.mult).then_inc(cv_tap, 1)
            dve.wait_ge(dt_ln, 1)
            dve.scalar_tensor_tensor(out=dtw[:, 3, :], in0=dtw[:, 0, :], scalar=0.0, in1=dtw[:, 2, :],
                                     op0=ALU.max, op1=ALU.add).then_inc(dt_dt, 1)
            dve.wait_ge(dt_dt, 1)
            dve.wait_ge(a_exp, 1)
            dve.tensor_scalar(dtw[:, 4, :], dtw[:, 3, :], aexp, -1.0, ALU.mult, ALU.mult).then_inc(dt_da, 1)

        ORDER = ((4, 5, 0, 1, 2, 3), (5, 4, 3, 2, 1, 0))

        def pe_turn(pe):
            pe.wait_ge(dt_da, 1)
            pe.wait_ge(pj_ev, len(PJ))
            for kk in range(2):
                for c in range(NT):
                    mm = pe.transpose(bank(0)[:, 192 * kk + 32 * c:192 * kk + 32 * c + 32],
                                      dtw[:, 3 + kk, P * c:P * c + P], ident[0:32, 0:32])
            mm.then_inc(tk_dt, 1)
            pe.wait_ge(cv_out, 12)
            for c in range(NT):
                if c >= 2:
                    pe.wait_ge(tk_xc, c - 1)
                for b in range(8):
                    mm = pe.transpose(pair(1 + c % 2, 1024)[:, P * b:P * b + P], xs[:, b, P * c:P * c + P], ident)
                mm.then_inc(tk_x, 1)
            for c2 in range(3):
                if c2 == 2:
                    pe.wait_ge(tk_bc, 1)
                for k in range(4):
                    c, g = 2 * c2 + k // 2, k % 2
                    mm = pe.transpose(bank(6 + c2 % 2)[:, P * k:P * k + P], bc[:, g, P * c:P * c + P], ident)
                mm.then_inc(tk_b, 1)

        def dve_turn(dve):
            dve.wait_ge(tk_dt, 1)
            dve.tensor_copy(mix[:, 14848:15232], bank(0, 0, 384)).then_inc(tk_dtc, 1)
            for c in range(NT):
                dve.wait_ge(tk_x, c + 1)
                dve.tensor_copy(xtok[:, c, :], pair(1 + c % 2, 1024)).then_inc(tk_xc, 1)
            for c2 in range(3):
                dve.wait_ge(tk_b, c2 + 1)
                dve.tensor_copy(big[:, 20 * T + 512 * c2:20 * T + 512 * c2 + 512], bank(6 + c2 % 2)).then_inc(tk_bc, 1)
            dve.wait_ge(dc_exp, 1)
            dve.tensor_tensor(wdt[:, 0], dec[:, 0:96].rearrange("p (c h) -> p c h", c=NT), dtk[:, 0, :, 0:16], ALU.mult)
            dve.tensor_tensor(wdt[:, 1], dec[:, 96:192].rearrange("p (c h) -> p c h", c=NT), dtk[:, 0, :, 16:32],
                              ALU.mult).then_inc(dc_w, 1)

        def pe_decay(pe):
            pe.wait_ge(tk_dtc, 1)
            pe.matmul(bank(0, 0, 96), c_(C_UF), dtk[:, 1, :, 0:16], start=True, stop=True)
            pe.matmul(bank(0, 96, 192), c_(C_UB), dtk[:, 1, :, 16:32], start=True, stop=True)
            pe.matmul(bank(0, 192, 384), ones, dtk[:, 1, :, :], start=True, stop=True).then_inc(dc_mm, 1)

        def act_decay(act):
            act.wait_ge(dc_mm, 1)
            act.activation(dec[:, 0:384], bank(0, 0, 384), ACT.Exp).then_inc(dc_exp, 1)

        STEPS = [(g, dr_, k) for g in range(2) for k in range(5) for dr_ in range(2)]

        def head_bc(v, n):
            return v.rearrange("p (h o) -> p h o", o=1).broadcast_to([P, v.shape[-1], n])

        def pool_states(pool, g):
            for q in range(10 * g, 10 * g + 10):
                _, dr_, k = STEPS[q]
                c = ORDER[dr_][k]
                if q == 0:
                    pool.wait_ge(dc_w, 1)
                    pool.wait_ge(tk_xc, NT)
                if q % 10 == 0 and g == 1:
                    pool.wait_ge(y_mm, 12)
                if q >= 2:
                    pool.wait_ge(s_mm, q - 1)
                pool.tensor_tensor(xw[:, q % 2, :].rearrange("p (h n) -> p h n", n=SP),
                                   xtok[:, c, 512 * g:512 * g + 512].rearrange("p (h n) -> p h n", n=SP),
                                   head_bc(wdt[:, dr_, c, 8 * g:8 * g + 8], SP), ALU.mult).then_inc(s_xw, 1)

        def pe_states(pe, g):
            for q in range(10 * g, 10 * g + 10):
                _, dr_, k = STEPS[q]
                c = ORDER[dr_][k]
                pe.wait_ge(s_xw, q + 1)
                if q == 0:
                    pe.wait_ge(tk_bc, 3)
                if q == 10:
                    pe.wait_ge(y_out, 12)
                if q >= 2:
                    pe.wait_ge(s_st, q - 1)
                pe.matmul(bank(6 + q % 2), btok[:, c, P * g:P * g + P], xw[:, q % 2, :],
                          start=True, stop=True).then_inc(s_mm, 1)

        def dve_states(dve, g):
            ndec = 8 * g
            for q in range(10 * g, 10 * g + 10):
                _, dr_, k = STEPS[q]
                c = ORDER[dr_][k]
                s = st[:, dr_, k, :]
                if k == 0:
                    dve.wait_ge(s_mm, q + 1)
                    dve.tensor_copy(s, bank(6 + q % 2)).then_inc(s_st, 1)
                    continue
                dve.wait_ge(s_st, q - 1)
                h0 = 16 * dr_ + 8 * g
                dve.tensor_tensor(s.rearrange("p (h n) -> p h n", n=SP),
                                  st[:, dr_, k - 1, :].rearrange("p (h n) -> p h n", n=SP),
                                  head_bc(dcb[:, c, h0:h0 + 8], SP), ALU.mult).then_inc(s_dec, 1)
                ndec += 1
                dve.wait_ge(s_dec, ndec)
                dve.wait_ge(s_mm, q + 1)
                dve.tensor_tensor(s, s, bank(6 + q % 2), ALU.add).then_inc(s_st, 1)

        def pe_gram(pe, g):
            for c in range(NT):
                q = NT * g + c
                if q % NT >= 2:
                    pe.wait_ge(g_done, 2 * (q - 1))
                elif g == 1:
                    pe.wait_ge(s_st, 20)
                else:
                    pe.wait_ge(s_st, 10)
                t0 = P * c
                pe.matmul(bank(6 + c % 2, 0, P), bc[:, g, t0:t0 + P], bc[:, 2 + g, t0:t0 + P],
                          start=True, stop=True).then_inc(g_mm, 1)

        def dve_gram(dve, g):
            for c in range(NT):
                dve.wait_ge(g_mm, NT * g + c + 1)
                for dr_, tri in ((0, C_TF), (1, C_TB)):
                    dve.tensor_tensor(gg[:, c, dr_, :], c_(tri), bank(6 + c % 2, 0, P), ALU.mult).then_inc(g_done, 1)

        YU = [(g, c, hf) for g in range(2) for c in range(NT) for hf in range(2)]

        def pool_y(pool, g):
            for v in range(12 * g, 12 * g + 12):
                _, c, hf = YU[v]
                q = v // 2
                if hf == 0:
                    if v % 12 == 0:
                        pool.wait_ge(s_mm, 10 * g + 10)
                    if q % NT >= 2:
                        pool.wait_ge(y_mm, 2 * (q - 1))
                    for dr_ in range(2):
                        pool.tensor_tensor(xdt[:, q % 2, dr_, :].rearrange("p (h n) -> p h n", n=SP),
                                           xtok[:, c, 512 * g:512 * g + 512].rearrange("p (h n) -> p h n", n=SP),
                                           head_bc(dtk[:, 0, c, 16 * dr_ + 8 * g:16 * dr_ + 8 * g + 8], SP),
                                           ALU.mult).then_inc(y_xdt, 1)
                if v >= 2:
                    pool.wait_ge(y_seg, v - 1)
                for dr_, tri in ((0, C_TF), (1, C_TB)):
                    h0 = 16 * dr_ + 8 * g + 4 * hf
                    pool.tensor_tensor(rr[:, v % 2, dr_, :].rearrange("p (h n) -> p h n", n=P),
                                       c_(tri).rearrange("p (o n) -> p o n", o=1).broadcast_to([P, 4, P]),
                                       head_bc(dtk[:, 1, c, h0:h0 + 4], P), ALU.mult).then_inc(y_r, 1)

        def pe_y(pe, g):
            for v in range(12 * g, 12 * g + 13):
                if v < 12 * g + 12:
                    pe.wait_ge(y_r, 2 * v + 2)
                    if v % 12 < 2:
                        pe.wait_ge(s_st, 10 * g + 10)
                        pe.wait_ge(g_done, 12 * g + 12)
                    if v >= 2:
                        pe.wait_ge(y_exp, v - 1)
                    b = 3 * (v % 2)
                    pe.matmul(bank(b), c_(C_UF), rr[:, v % 2, 0, :], start=True, stop=False)
                    pe.matmul(bank(b), c_(C_UB), rr[:, v % 2, 1, :], start=False, stop=True)
                    pe.matmul(bank(b + 1), ones, rr[:, v % 2, 0, :], start=True, stop=True)
                    pe.matmul(bank(b + 2), ones, rr[:, v % 2, 1, :], start=True, stop=True).then_inc(y_seg, 1)
                w = v - 1
                if w >= 12 * g:
                    _, c, hf = YU[w]
                    q = w // 2
                    pe.wait_ge(y_m, 4 * w + 4)
                    pe.wait_ge(y_xdt, 2 * q + 2)
                    if w % 12 >= 2:
                        pe.wait_ge(y_out, w - 1)
                    e = ee[:, w % 2, :]
                    for pp in range(2):
                        for eo in range(2):
                            i = 2 * pp + eo
                            at = bank(6 + w % 2)[64 * eo:64 * eo + 64, P * pp:P * pp + P]
                            x0 = SP * (4 * hf + i)
                            terms = [(xdt[:, q % 2, 0, x0:x0 + SP], mf[:, w % 2, P * i:P * i + P]),
                                     (xdt[:, q % 2, 1, x0:x0 + SP], e[:, P * i:P * i + P])]
                            for dr_ in range(2):
                                k = ORDER[dr_].index(c)
                                if k:
                                    terms.append((st[:, dr_, k - 1, x0:x0 + SP],
                                                  e[:, 512 * (1 + dr_) + P * i:512 * (1 + dr_) + P * i + P]))
                            for n, (lhs, rhs) in enumerate(terms):
                                mm = pe.matmul(at, lhs, rhs, start=n == 0, stop=n == len(terms) - 1)
                    mm.then_inc(y_mm, 1)

        def act_y(act, g):
            for v in range(12 * g, 12 * g + 12):
                act.wait_ge(y_seg, v + 1)
                if v >= 2:
                    act.wait_ge(y_mm, v - 1)
                act.activation(ee[:, v % 2, :], ps[:, 1536 * (v % 2):1536 * (v % 2) + 1536], ACT.Exp).then_inc(y_exp, 1)

        def dve_y(dve, g):
            for v in range(12 * g, 12 * g + 13):
                if v < 12 * g + 12:
                    _, c, hf = YU[v]
                    dve.wait_ge(y_exp, v + 1)
                    if v % 12 == 0:
                        dve.wait_ge(g_done, 12 * g + 12)
                    if v >= 2:
                        dve.wait_ge(y_mm, v - 1)
                    e = ee[:, v % 2, :].rearrange("p (k h n) -> p k h n", k=3, h=4)
                    over = lambda x: x.rearrange("p (o n) -> p o n", o=1).broadcast_to([P, 4, P])
                    dve.tensor_tensor(mf[:, v % 2, :].rearrange("p (h n) -> p h n", h=4), e[:, 0],
                                      over(gg[:, c, 0, :]), ALU.mult).then_inc(y_m, 1)
                    dve.tensor_tensor(e[:, 0], e[:, 0], over(gg[:, c, 1, :]), ALU.mult).then_inc(y_m, 1)
                    cc = over(bc[:, 2 + g, P * c:P * c + P])
                    dve.tensor_tensor(e[:, 1], e[:, 1], cc, ALU.mult).then_inc(y_m, 1)
                    dve.tensor_tensor(e[:, 2], e[:, 2], cc, ALU.mult).then_inc(y_m, 1)
                w = v - 1
                if w >= 12 * g:
                    _, c, hf = YU[w]
                    dve.wait_ge(y_mm, w + 1)
                    for pp in range(2):
                        b = 4 * g + 2 * hf + pp
                        y = xs[:, b, P * c:P * c + P]
                        x = dve.scalar_tensor_tensor(out=y, in0=y, scalar=dskip[:, b:b + 1],
                                                     in1=bank(6 + w % 2, P * pp, P * pp + P),
                                                     op0=ALU.mult, op1=ALU.add)
                    x.then_inc(y_out, 1)

        def pool_merge(pool):
            pool.wait_ge(y_out, 24)
            for b in range(8):
                pool.tensor_tensor(xs[:, b, :], xs[:, b, :], z[:, b, :], ALU.mult).then_inc(m_z, 1)

        def act_merge(act):
            act.wait_ge(y_mm, 24)
            for b in range(8):
                act.wait_ge(m_z, b + 1)
                if b >= 2:
                    act.wait_ge(m_ss, b - 1)
                act.activation(sqn[:, b % 2, :], xs[:, b, :], ACT.Square).then_inc(m_sq, 1)
            for g in range(2):
                act.wait_ge(m_ss, 4 * g + 4)
                if g == 1:
                    act.wait_ge(m_y, 4)
                act.activation(rsn, pair(2 + g), ACT.Ln, bias=eps, scale=1.0 / 512).then_inc(m_ln, 1)
                act.wait_ge(m_ln, g + 1)
                act.activation(rsn, rsn, ACT.Exp, scale=-0.5).then_inc(m_rs, 1)

        def pe_merge(pe):
            pe.wait_ge(y_out, 24)
            for b in range(8):
                pe.wait_ge(m_sq, b + 1)
                for c0, c1 in ((0, 512), (512, T)):
                    mm = pe.matmul(pair(2 + b // 4)[:, c0:c1], ones, sqn[:, b % 2, c0:c1], start=b % 4 == 0, stop=b % 4 == 3)
                mm.then_inc(m_ss, 1)
            pe.wait_ge(m_y, 8)

        def dve_merge(dve):
            for b in range(8):
                dve.wait_ge(m_rs, b // 4 + 1)
                dve.wait_ge(m_sq, b + 1)
                dve.scalar_tensor_tensor(out=xs[:, b, :], in0=xs[:, b, :], scalar=vb[:, VB_SSD + b:VB_SSD + b + 1],
                                         in1=rsn, op0=ALU.mult, op1=ALU.mult).then_inc(m_y, 1)

        def sync_ff(f, i_f):
            for part in PARTS:
                sync_ffi(f, i_f, part)
                sync_out(f, R_FF(i_f, part))

        def pe_ff(pe, dr, i_f):
            for part in PARTS:
                pe_ffi(pe, dr, i_f, part)
                pe_out(pe, dr, R_FF(i_f, part))

        def act_ff(act, ar, i_f):
            for part in PARTS:
                act_ffi(act, ar, i_f, part)
                act_out_ff(act, ar, R_FF(i_f, part))

        def dve_ff(dve, dv, i_f):
            for part in PARTS:
                dve_ffi(dve, dv, i_f, part)
                dve_out_ff(dve, dv, R_FF(i_f, part))

        block_ = ctx.enter_context(nc.Block())

        @block_.sync
        def _(sp):
            f = Filler(sp)
            sp.dma_start(cst[:, :], a["shape_constants"]).then_inc(const_in, 16)
            flat = lambda x: x.rearrange("l (n p) -> l n p", p=P)
            for dst, src in [
                (rows[VA_MOD:VA_MOD + 72, 0, :], flat(a["b_mod"])[0]),
                (rows[VA_C:VA_C + 8, 0, :], flat(a["c"])[0]),
                (rows[VA_CC:VA_CC + 8, 0, :], a["c_ctx"].rearrange("(n p) -> n p", p=P)),
                (rows[VB_MOD:VB_MOD + 72, 1, :], flat(a["b_mod"])[1]),
                (rows[VB_SSD:VB_SSD + 8, 1, :], flat(a["ssd_norm"])[0]),
                (rows[VB_QA:VB_QA + 3, 1, :], flat(a["mla_qa_norm"])[0]),
                (rows[VB_KV:VB_KV + 2, 1, :], flat(a["mla_kv_norm"])[0]),
                (rows[VB_QN:VB_QN + 1, 1, :], a["mla_qn_norm"]),
                (rows[VB_KN:VB_KN + 1, 1, :], a["mla_kn_norm"]),
                (rows[VB_QR:VB_QR + 1, 1, 0:64], a["mla_qr_norm"]),
                (rows[VB_QR:VB_QR + 1, 1, 64:128], a["mla_qr_norm"]),
                (rows[VB_KR:VB_KR + 1, 1, 0:64], a["mla_kr_norm"]),
                (rows[VB_KR:VB_KR + 1, 1, 64:128], a["mla_kr_norm"]),
                (rows[VB_GQ:VB_GQ + 1, 1, 0:64], a["gqa_q_norm"]),
                (rows[VB_GQ:VB_GQ + 1, 1, 64:128], a["gqa_q_norm"]),
                (rows[VB_GK:VB_GK + 1, 1, 0:64], a["gqa_k_norm"]),
                (rows[VB_GK:VB_GK + 1, 1, 64:128], a["gqa_k_norm"]),
                (rows[VB_CB:VB_CB + 12, 1, :], flat(a["conv_b"])[0]),
                (rows[0:60, 2, :], a["conv_w"][0].rearrange("t (n p) -> (t n) p", p=P)),
                (dtb, a["dt_bias"][0].rearrange("a (h o) -> (a h) o", o=1)),
                (alog, a["a_log"][0].rearrange("a (h o) -> (a h) o", o=1)),
                (dskip[0:64, :], a["d_skip"].rearrange("l (b e) -> l b e", e=2)[:, :, 0].broadcast_to([64, 8])),
                (dskip[64:128, :], a["d_skip"].rearrange("l (b e) -> l b e", e=2)[:, :, 1].broadcast_to([64, 8])),
                (sink[:, :], a["sink"].broadcast_to([P, QH])),
            ]:
                sp.dma_start(dst, src, allow_slow_non_contiguous=True).then_inc(rows_in, 16)
            for n in range(NT):
                src = a["x"][0, P * n:P * n + P, :] if n < 4 else a["ctx"][0, P * (n - 4):P * (n - 3), :]
                sp.dma_start(xin[:, n, :], src).then_inc(x_in, 16)
            sync_ff(f, 0)
            assert f.n == BASE["even"]
            sync_items(f, 0, n_even)
            sync_v(f, "e")
            sync_out(f, R_MLA)
            sync_proj(f)
            sync_out(f, R_SSD)
            sync_ff(f, 1)
            sync_ff(f, 2)
            sync_items(f, n_even, len(items))
            sync_v(f, "o")
            sync_out(f, R_GQA)
            sync_ff(f, 3)
            assert f.n == n_
            for n in range(SEQ // P):
                sp.wait_ge(out_c, 2 * n + 2)
                sp.dma_start(out[P * n:P * n + P, :], xin[:, n, :]).then_inc(out_st, 16)
            sp.wait_ge(out_st, 16 * (SEQ // P))

        @block_.tensor
        def _(pe):
            dr = Drainer(pe)
            pe.wait_ge(const_in, 16)
            pe.wait_ge(rows_in, 16 * 24)
            for n, rn in ((0, VA_N), (1, VB_N), (2, VC_N)):
                mm = pe.transpose(bank(7)[:, P * n:P * n + rn], rows[0:rn, n, :], ident[0:rn, 0:rn])
            mm.then_inc(vec_t, 1)
            pe.wait_ge(x_in, 16 * NT)
            for d in range(DB):
                if d >= 2:
                    pe.wait_ge(h_loaded, d - 1)
                for n in range(NT):
                    mm = pe.transpose(pair(d % 2)[:, P * n:P * n + P], xin[:, n, P * d:P * d + P], ident)
                mm.then_inc(xt_done, 1)
            pe.wait_ge(vec_done, 3)
            pe_norm(pe, 0)
            pe.wait_ge(ones_set, 1)
            for q in range(3):
                pe_mod(pe, 0, q)
            pe_ff(pe, dr, 0)
            pe_norm(pe, 1)
            pe_items(pe, dr, 0, n_even, 1)
            pe_v(pe, dr, "e")
            pe.wait_ge(v_done, 12)
            pe.wait_ge(hn_fin, ropes_to(n_even))
            pe.wait_ge(hn_n, norms_to(n_even))
            pe_attend(pe, 0, n_mla)
            pe.wait_ge(at_o, n_mla)
            pe_out(pe, dr, R_MLA)
            pe_proj(pe, dr)
            pe_turn(pe)
            pe_decay(pe)
            for g in range(2):
                pe_states(pe, g)
                pe_gram(pe, g)
                pe_y(pe, g)
            pe_merge(pe)
            pe_out(pe, dr, R_SSD)
            for i_f in (1, 2):
                pe_norm(pe, FF_NORM[i_f])
                pe_ff(pe, dr, i_f)
            pe_norm(pe, 4)
            pe_items(pe, dr, n_even, len(items), 4)
            pe_v(pe, dr, "o")
            pe.wait_ge(v_done, 24)
            pe.wait_ge(hn_fin, ropes_to(len(items)))
            pe_attend(pe, n_mla, len(units))
            pe.wait_ge(at_o, len(units))
            pe_out(pe, dr, R_GQA)
            pe_norm(pe, 5)
            pe_ff(pe, dr, 3)
            for n in range(SEQ // P):
                if n >= 2:
                    pe.wait_ge(out_c, 2 * (n - 1))
                for d in range(DB):
                    if n == 0:
                        pe.wait_ge(o_res, RES[R_FF(3, 2)] + d + 1)
                    mm = pe.transpose(pair(2 + n % 2, 1024)[:, P * d:P * d + P], h[:, d, P * n:P * n + P], ident)
                mm.then_inc(out_t, 1)

        @block_.scalar
        def _(act):
            act.wait_ge(vec_done, 1)
            act.activation(sc[:, :].rearrange("p (k s) -> p s k", s=2),
                           va[:, VA_C:VA_C + 16].rearrange("p (s k) -> p s k", s=2), ACT.Silu).then_inc(sc_done, 1)
            ar = Drainer(act)
            act.wait_ge(const_in, 16)
            act.copy(ones_r[:, :], ones[:, 0:2]).then_inc(ones_set, 1)
            act_rstd(act, 0)
            for q in range(3):
                act_mod_hi(act, 0, q)
            act_shift(act, 0)
            act_ff(act, ar, 0)
            act_norm(act, 1)
            ar.passed_items(0, n_even)
            ar.passed_v(2)
            ar.passed(DB + 21 + DB)
            act_items(act, 0, n_even, BASE["even"])
            act_attend(act, 0, n_mla)
            act_proj(act)
            act_decay(act)
            act_y(act, 0)
            act_y(act, 1)
            act_merge(act)
            for i_f in (1, 2):
                act_norm(act, FF_NORM[i_f])
                act_ff(act, ar, i_f)
            act_norm(act, 4)
            ar.passed_items(n_even, len(items))
            ar.passed_v(1)
            ar.passed(DB)
            act_items(act, n_even, len(items), BASE["odd"])
            act_attend(act, n_mla, len(units))
            act_norm(act, 5)
            act_ff(act, ar, 3)
            for n in range(SEQ // P):
                act.wait_ge(out_t, n + 1)
                act.wait_ge(w_used, n_)
                act.copy(xin[:, n, 0:512], pair(2 + n % 2, 1024)[:, 0:512]).then_inc(out_c, 1)
                act.copy(xin[:, n, 512:1024], pair(2 + n % 2, 1024)[:, 512:1024]).then_inc(out_c, 1)

        @block_.vector
        def _(dve):
            dve.memset(eps, EPS).then_inc(eps_set, 1)
            dve.wait_ge(vec_t, 1)
            for n, (v, rn) in enumerate(((va, VA_N), (vb, VB_N), (vc, VC_N))):
                dve.tensor_copy(v[:, :], bank(7)[:, P * n:P * n + rn]).then_inc(vec_done, 1)
            for d in range(DB):
                dve.wait_ge(xt_done, d + 1)
                dve.tensor_copy(h[:, d, :], pair(d % 2)).then_inc(h_loaded, 1)
            dve.wait_ge(vec_done, 3)
            for k in range(DB):
                for q in range(3):
                    dve_mod_sum(dve, 0, k, q)
            for q in range(3):
                dve_mod_lo(dve, 0, q)
            dve_mod(dve, 0)
            dv = Drainer(dve)
            dv.n = BASE["ffi", 0, 0]
            dve_norm(dve, 0)
            dve_ff(dve, dv, 0)
            dve_norm(dve, 1)
            dve_items(dve, 0, n_even)
            dve_v(dve, "e")
            dve_attend(dve, 0, n_mla)
            dv.n = BASE["out", R_MLA]
            dve_out(dve, R_MLA)
            dve_proj(dve)
            dve_turn(dve)
            for g in range(2):
                dve_states(dve, g)
                dve_gram(dve, g)
                dve_y(dve, g)
            dve_merge(dve)
            dv.n = BASE["out", R_SSD]
            dve_out(dve, R_SSD)
            for i_f in (1, 2):
                dve_norm(dve, FF_NORM[i_f])
                dve_ff(dve, dv, i_f)
            dve_norm(dve, 4)
            dve_items(dve, n_even, len(items))
            dve_v(dve, "o")
            dve_attend(dve, n_mla, len(units))
            dv.n = BASE["out", R_GQA]
            dve_out(dve, R_GQA)
            dve_norm(dve, 5)
            dve_ff(dve, dv, 3)

        @block_.gpsimd
        def _(pool):
            for g in range(3):
                pool_mod(pool, g)
            for g in range(2):
                pool_states(pool, g)
                pool_y(pool, g)
            pool_merge(pool)
            for g in range(3, 6):
                pool_mod(pool, g)


INPUTS = ["x", "c", "ctx", "c_ctx", "w_mod", "b_mod", "w_ff1_in", "w_ff1_out", "w_ff2_in", "w_ff2_out",
          "w_in_e", "conv_w", "conv_b", "dt_bias", "a_log", "d_skip", "ssd_norm", "mla_qa_norm", "w_qb",
          "mla_kv_norm", "w_kvb", "mla_qn_norm", "mla_qr_norm", "mla_kn_norm", "mla_kr_norm", "w_out_e",
          "w_in_o", "gqa_q_norm", "gqa_k_norm", "sink", "w_out_o"]


def kernel(**inputs):
    import concourse.bacc as bacc
    from concourse.bass_utils import run_bass_kernel_spmd

    nc = bacc.Bacc("TRN2", target_bir_lowering=False, num_devices=1)
    arrays = {"shape_constants": shape_constants()}
    for name in INPUTS:
        arrays[name] = np.ascontiguousarray(inputs[name])
    sent, aps = {}, {}
    for name, v in arrays.items():
        sent[f"in_{name}"] = v
        aps[name] = nc.dram_tensor(f"in_{name}", v.shape, mybir.dt.from_np(v.dtype), kind="ExternalInput").ap()
    out = nc.dram_tensor("out_h", (SEQ, D), F32, kind="ExternalOutput").ap()
    build(nc, aps, out)
    r = run_bass_kernel_spmd(nc, [sent], core_ids=[0])
    return r.results[0]["out_h"].reshape(1, SEQ, D)
```
